# Optimizing a Trainium2 kernel written in Bass

```python
import math
import jax
import jax.numpy as jnp
from jax import lax
import numpy as np

D_MODEL = 1024
BATCH = 1
SEQ = 256
DEPTH = 2

CHUNK = 64
NORM_EPS = 1e-6
A_HEAD_DIM = 64
A_WIDTH = D_MODEL // 2
A_HEADS = A_WIDTH // A_HEAD_DIM
A_DECAY_LORA = 64
A_ICLR_LORA = 64
A_VRES_LORA = 32
A_GATE_LORA = 128
A_GN_EPS = 64e-5
B_HEAD_DIM = 128
B_WIDTH = D_MODEL // 2
B_HEADS = B_WIDTH // B_HEAD_DIM
B_CONV = 4
EVEN_IN = 3 * A_WIDTH + 4 * B_WIDTH + 2 * B_HEADS
MIX_WIDTH = A_WIDTH + B_WIDTH
C_HEAD_DIM = 64
C_HEADS = D_MODEL // C_HEAD_DIM
C_WIDTH = C_HEADS * C_HEAD_DIM
C_WINDOW_CHUNKS = 8
C_MAX_REL = 256
D_FF = 4 * D_MODEL
PLE_DIM = 256
N_EVEN = (DEPTH + 1) // 2
N_ODD = DEPTH // 2


def rmsnorm(x, g, eps=NORM_EPS):
    xf = x.astype(jnp.float32)
    y = xf * lax.rsqrt(jnp.mean(xf * xf, -1, keepdims=True) + eps)
    return (y * g.astype(jnp.float32)).astype(x.dtype)

def l2norm(x, eps=1e-6):
    xf = x.astype(jnp.float32)
    return xf * lax.rsqrt(jnp.sum(xf * xf, -1, keepdims=True) + eps)

def token_shift(z):
    return jnp.pad(z, ((0, 0), (1, 0), (0, 0)))[:, :-1]

def causal_depthwise_conv(z, w):
    kw = w.shape[0]
    zp = jnp.pad(z, ((0, 0), (kw - 1, 0), (0, 0)))
    return lax.conv_general_dilated(zp, w[:, None, :].astype(z.dtype), window_strides=(1,), padding='VALID',
                                    dimension_numbers=('NWC', 'WIO', 'NWC'), feature_group_count=z.shape[-1])

def wkv7_scan(r, w, k, v, a, b):
    bsz, seq, nh, n = r.shape
    xs = tuple(jnp.swapaxes(z, 0, 1) for z in (r, w, k, v, a, b))

    def step(state, inp):
        r_t, w_t, k_t, v_t, a_t, b_t = inp
        sa = jnp.einsum('bhij,bhj->bhi', state, a_t)
        state = state * w_t[:, :, None, :] + sa[..., None] * b_t[:, :, None, :] + v_t[..., None] * k_t[:, :, None, :]
        return state, jnp.einsum('bhij,bhj->bhi', state, r_t)

    s0 = jnp.zeros((bsz, nh, n, n), jnp.float32)
    _, ys = lax.scan(step, s0, xs)
    return jnp.swapaxes(ys, 0, 1)

def rwkv7_group(h, dh, r, k, v, v_first, mu_proj, mu_lora, w0, w1, w2, a0, a1, a2, g1, g2,
                k_k, k_a, r_k, ln_g, ln_b, vres):
    bsz, seq, _ = h.shape
    heads = lambda z: z.reshape(bsz, seq, A_HEADS, A_HEAD_DIM)
    r = r + (token_shift(r) - r) * mu_proj[0]
    k = k + (token_shift(k) - k) * mu_proj[1]
    v = v + (token_shift(v) - v) * mu_proj[2]
    xw = h + dh * mu_lora[0]
    xa = h + dh * mu_lora[1]
    xg = h + dh * mu_lora[2]
    w_log = -jax.nn.softplus(-(w0 + jnp.tanh(xw @ w1) @ w2).astype(jnp.float32)) - 0.5
    decay = jnp.exp(-jnp.exp(w_log))
    a = jax.nn.sigmoid(a0 + (xa @ a1) @ a2)
    g = jax.nn.sigmoid(xg @ g1) @ g2
    kk = l2norm(heads(k * k_k))
    k = k * (1.0 + (a - 1.0) * k_a)
    if vres is None:
        v_first = v
    else:
        v_mu, v0, v1, v2 = vres
        xv = h + dh * v_mu
        v = v + (v_first - v) * jax.nn.sigmoid(v0 + (xv @ v1) @ v2)
    rh, kh, vh, ah = [heads(z).astype(jnp.float32) for z in (r, k, v, a)]
    y = wkv7_scan(rh, heads(decay), kh, vh, -kk, kk * ah)
    mean = jnp.mean(y, -1, keepdims=True)
    var = jnp.mean(jnp.square(y - mean), -1, keepdims=True)
    gn_g = ln_g.astype(jnp.float32).reshape(A_HEADS, A_HEAD_DIM)
    gn_b = ln_b.astype(jnp.float32).reshape(A_HEADS, A_HEAD_DIM)
    y = (y - mean) * lax.rsqrt(var + A_GN_EPS) * gn_g + gn_b
    y = y + jnp.sum(rh * kh * r_k.astype(jnp.float32), -1, keepdims=True) * vh
    y = y.reshape(bsz, seq, A_WIDTH) * g.astype(jnp.float32)
    return y.astype(h.dtype), v_first

def chunk_gated_delta_rule(q, k, v, beta, g):
    bsz, seq, nh, dk = q.shape
    dv = v.shape[-1]
    n = seq // CHUNK

    def to_chunks(z):
        z = z.astype(jnp.float32).reshape((bsz, n, CHUNK) + z.shape[2:])
        return jnp.moveaxis(z, 3, 1)

    q, k, v, beta, g = [to_chunks(z) for z in (q, k, v, beta, g)]
    gc = jnp.cumsum(g, -1)
    causal = jnp.tril(jnp.ones((CHUNK, CHUNK), bool))
    strict = jnp.tril(jnp.ones((CHUNK, CHUNK), bool), -1)
    decay = jnp.exp(jnp.where(causal, gc[..., :, None] - gc[..., None, :], -jnp.inf))
    kb = k * beta[..., None]
    amat = jnp.where(strict, jnp.einsum('bhncd,bhnsd->bhncs', kb, k) * decay, 0.0)
    rhs = jnp.concatenate([v * beta[..., None], kb * jnp.exp(gc)[..., None]], -1)
    sol = lax.linalg.triangular_solve(amat, rhs, left_side=True, lower=True, unit_diagonal=True)
    u, w = sol[..., :dv], sol[..., dv:]
    qk = jnp.einsum('bhncd,bhnsd->bhncs', q, k) * decay
    q_dec = q * jnp.exp(gc)[..., None]
    k_dec = k * jnp.exp(gc[..., -1:] - gc)[..., None]
    g_last = jnp.exp(gc[..., -1])
    xs = tuple(jnp.moveaxis(z, 2, 0) for z in (q_dec, k_dec, w, u, qk, g_last))

    def step(state, inp):
        qd, kd, wc, uc, qkc, gl = inp
        v_new = uc - jnp.einsum('bhcd,bhde->bhce', wc, state)
        o = jnp.einsum('bhcd,bhde->bhce', qd, state) + jnp.einsum('bhcs,bhse->bhce', qkc, v_new)
        state = state * gl[..., None, None] + jnp.einsum('bhcd,bhce->bhde', kd, v_new)
        return state, o

    s0 = jnp.zeros((bsz, nh, dk, dv), jnp.float32)
    _, o = lax.scan(step, s0, xs)
    return o.transpose(1, 0, 3, 2, 4).reshape(bsz, seq, nh, dv)

def gdn_group(qkv, gate, beta_logit, alpha_logit, conv_w, a_log, dt_bias, norm_g):
    bsz, seq, _ = qkv.shape
    qkv = jax.nn.silu(causal_depthwise_conv(qkv, conv_w))
    heads = lambda z: z.reshape(bsz, seq, B_HEADS, B_HEAD_DIM)
    q = l2norm(heads(qkv[..., :B_WIDTH])) * (B_HEAD_DIM ** -0.5)
    k = l2norm(heads(qkv[..., B_WIDTH:2 * B_WIDTH]))
    v = heads(qkv[..., 2 * B_WIDTH:])
    beta = jax.nn.sigmoid(beta_logit.astype(jnp.float32))
    g = -jnp.exp(a_log.astype(jnp.float32)) * jax.nn.softplus((alpha_logit + dt_bias).astype(jnp.float32))
    o = chunk_gated_delta_rule(q, k, v, beta, g)
    o = rmsnorm(o, norm_g) * jax.nn.silu(heads(gate).astype(jnp.float32))
    return o.reshape(bsz, seq, B_WIDTH).astype(qkv.dtype)

def chunk_band_attention(h, w_qkv, q_g, k_g, rel_bias):
    bsz, seq, _ = h.shape
    qkv = (h @ w_qkv).reshape(bsz, seq, 3, C_HEADS, C_HEAD_DIM)
    q = rmsnorm(qkv[:, :, 0], q_g) * (C_HEAD_DIM ** -0.5)
    k = rmsnorm(qkv[:, :, 1], k_g)
    v = qkv[:, :, 2]
    pad = C_WINDOW_CHUNKS * CHUNK
    band = pad + CHUNK
    kp = jnp.pad(k, ((0, 0), (pad, 0), (0, 0), (0, 0)))
    vp = jnp.pad(v, ((0, 0), (pad, 0), (0, 0), (0, 0)))
    rel = jnp.arange(CHUNK)[:, None] + pad - jnp.arange(band)[None, :]
    bias = rel_bias[:, jnp.clip(rel, -C_MAX_REL, C_MAX_REL) + C_MAX_REL].astype(jnp.float32)

    def one_chunk(c):
        start = c * CHUNK
        q_c = lax.dynamic_slice_in_dim(q, start, CHUNK, axis=1)
        k_b = lax.dynamic_slice_in_dim(kp, start, band, axis=1)
        v_b = lax.dynamic_slice_in_dim(vp, start, band, axis=1)
        s = jnp.einsum('bqhd,bkhd->bhqk', q_c, k_b).astype(jnp.float32) + bias
        valid = (start - pad + jnp.arange(band)) >= 0
        s = jnp.where(valid, s, -jnp.inf)
        prob = jax.nn.softmax(s, -1).astype(v.dtype)
        return jnp.einsum('bhqk,bkhd->bqhd', prob, v_b)

    o = lax.map(one_chunk, jnp.arange(seq // CHUNK))
    return jnp.moveaxis(o, 0, 1).reshape(bsz, seq, C_WIDTH)

def first_inputs(seed: int = 0) -> dict:
    key = jax.random.key(seed)
    keys = jax.random.split(key, 48)
    ctr = [0]

    def nk():
        kk = keys[ctr[0]]
        ctr[0] += 1
        return kk

    def nrm(shape, scale=1.0):
        return scale * jax.random.normal(nk(), shape, jnp.float32)

    def unif(shape, lo, hi):
        return jax.random.uniform(nk(), shape, jnp.float32, lo, hi)

    D, E, O, EV = D_MODEL, N_EVEN, N_ODD, N_EVEN - 1
    dt = jnp.exp(unif((E, B_HEADS), math.log(1e-3), math.log(1e-1)))
    return {
        'x': nrm((BATCH, SEQ, D)),
        'p': nrm((DEPTH, BATCH, SEQ, PLE_DIM)),
        'norm_mix_g': 1.0 + nrm((DEPTH, D), 0.05),
        'norm_ffn_g': 1.0 + nrm((DEPTH, D), 0.05),
        'even_w_in': nrm((E, D, EVEN_IN), D ** -0.5),
        'rwkv_mu_proj': unif((E, 3, A_WIDTH), 0.0, 1.0),
        'rwkv_mu_lora': unif((E, 3, D), 0.0, 1.0),
        'rwkv_w0': unif((E, A_WIDTH), -6.0, 0.0),
        'rwkv_w1': nrm((E, D, A_DECAY_LORA), D ** -0.5),
        'rwkv_w2': nrm((E, A_DECAY_LORA, A_WIDTH), 0.5 * A_DECAY_LORA ** -0.5),
        'rwkv_a0': nrm((E, A_WIDTH), 0.5),
        'rwkv_a1': nrm((E, D, A_ICLR_LORA), D ** -0.5),
        'rwkv_a2': nrm((E, A_ICLR_LORA, A_WIDTH), 0.5 * A_ICLR_LORA ** -0.5),
        'rwkv_g1': nrm((E, D, A_GATE_LORA), D ** -0.5),
        'rwkv_g2': nrm((E, A_GATE_LORA, A_WIDTH), A_GATE_LORA ** -0.5),
        'rwkv_k_k': 0.85 + nrm((E, A_WIDTH), 0.05),
        'rwkv_k_a': 1.0 + nrm((E, A_WIDTH), 0.05),
        'rwkv_r_k': nrm((E, A_HEADS, A_HEAD_DIM), 0.1),
        'rwkv_ln_g': 1.0 + nrm((E, A_WIDTH), 0.05),
        'rwkv_ln_b': nrm((E, A_WIDTH), 0.02),
        'rwkv_v_mu': unif((EV, D), 0.0, 1.0),
        'rwkv_v0': nrm((EV, A_WIDTH), 0.5),
        'rwkv_v1': nrm((EV, D, A_VRES_LORA), D ** -0.5),
        'rwkv_v2': nrm((EV, A_VRES_LORA, A_WIDTH), 0.5 * A_VRES_LORA ** -0.5),
        'gdn_conv_w': nrm((E, B_CONV, 3 * B_WIDTH), B_CONV ** -0.5),
        'gdn_a_log': jnp.log(unif((E, B_HEADS), 1.0, 16.0)),
        'gdn_dt_bias': dt + jnp.log(-jnp.expm1(-dt)),
        'gdn_norm_g': 1.0 + nrm((E, B_HEAD_DIM), 0.05),
        'even_w_out': nrm((E, MIX_WIDTH, D), MIX_WIDTH ** -0.5),
        'attn_w_qkv': nrm((O, D, 3 * C_WIDTH), D ** -0.5),
        'attn_q_g': 1.0 + nrm((O, C_HEAD_DIM), 0.05),
        'attn_k_g': 1.0 + nrm((O, C_HEAD_DIM), 0.05),
        'attn_rel_bias': nrm((O, C_HEADS, 2 * C_MAX_REL + 1), 0.5),
        'attn_w_out': nrm((O, C_WIDTH, D), C_WIDTH ** -0.5),
        'mlp_w1': nrm((DEPTH, D, D_FF), D ** -0.5),
        'mlp_w2': nrm((DEPTH, D_FF, D), D_FF ** -0.5),
        'ple_w_proj': nrm((DEPTH, PLE_DIM, D), PLE_DIM ** -0.5),
        'ple_norm_g': 1.0 + nrm((DEPTH, D), 0.05),
        'ple_w_gate': nrm((DEPTH, D, D), D ** -0.5),
    }

def first_block(x, p, norm_mix_g, norm_ffn_g, even_w_in, rwkv_mu_proj, rwkv_mu_lora, rwkv_w0, rwkv_w1, rwkv_w2,
              rwkv_a0, rwkv_a1, rwkv_a2, rwkv_g1, rwkv_g2, rwkv_k_k, rwkv_k_a, rwkv_r_k, rwkv_ln_g, rwkv_ln_b,
              rwkv_v_mu, rwkv_v0, rwkv_v1, rwkv_v2, gdn_conv_w, gdn_a_log, gdn_dt_bias, gdn_norm_g, even_w_out,
              attn_w_qkv, attn_q_g, attn_k_g, attn_rel_bias, attn_w_out, mlp_w1, mlp_w2,
              ple_w_proj, ple_norm_g, ple_w_gate):
    o_ak, o_av, o_bq = A_WIDTH, 2 * A_WIDTH, 3 * A_WIDTH
    o_bg = o_bq + 3 * B_WIDTH
    o_bb = o_bg + B_WIDTH
    o_ba = o_bb + B_HEADS
    v_first = None
    for i in range(DEPTH):
        h = rmsnorm(x, norm_mix_g[i])
        if i % 2 == 0:
            e = i // 2
            proj = h @ even_w_in[e]
            dh = token_shift(h) - h
            vres = None if e == 0 else (rwkv_v_mu[e - 1], rwkv_v0[e - 1], rwkv_v1[e - 1], rwkv_v2[e - 1])
            y_a, v_first = rwkv7_group(h, dh, proj[..., :o_ak], proj[..., o_ak:o_av], proj[..., o_av:o_bq], v_first,
                                       rwkv_mu_proj[e], rwkv_mu_lora[e], rwkv_w0[e], rwkv_w1[e], rwkv_w2[e],
                                       rwkv_a0[e], rwkv_a1[e], rwkv_a2[e], rwkv_g1[e], rwkv_g2[e],
                                       rwkv_k_k[e], rwkv_k_a[e], rwkv_r_k[e], rwkv_ln_g[e], rwkv_ln_b[e], vres)
            y_b = gdn_group(proj[..., o_bq:o_bg], proj[..., o_bg:o_bb], proj[..., o_bb:o_ba], proj[..., o_ba:],
                            gdn_conv_w[e], gdn_a_log[e], gdn_dt_bias[e], gdn_norm_g[e])
            mix = jnp.concatenate([y_a, y_b], -1) @ even_w_out[e]
        else:
            o = i // 2
            mix = chunk_band_attention(h, attn_w_qkv[o], attn_q_g[o], attn_k_g[o], attn_rel_bias[o]) @ attn_w_out[o]
        x = x + mix
        hf = rmsnorm(x, norm_ffn_g[i])
        x = x + jnp.square(jax.nn.relu(hf @ mlp_w1[i])) @ mlp_w2[i]
        x = x + rmsnorm(p[i] @ ple_w_proj[i], ple_norm_g[i]) * jax.nn.sigmoid(x @ ple_w_gate[i])
    return x


GRID_W = 64
CTX_LEN = 256
HEAD_DIM = 64
Q_BLOCK = 128
ROPE_THETA = 10000.0
EPS = 1e-6
MIX_HALF = D_MODEL // 2
NA_HEADS = MIX_HALF // HEAD_DIM
NA_WIN_R = 8
NA_WIN_C = 16
DA_VDIM = 2 * HEAD_DIM
DA_HEADS = MIX_HALF // DA_VDIM
GQA_Q_HEADS = MIX_HALF // HEAD_DIM
GQA_KV_HEADS = GQA_Q_HEADS // 4
HY_WIDTH = MIX_HALF
HY_EMB_DIM = 33
HY_FILTER_ORDER = 64
HY_FAST_DECAY = 0.3
HY_SLOW_DECAY = 1.5
HY_DECAY_TARGET = 1e-2
FFN_HIDDEN = ((8 * D_MODEL // 3 + 255) // 256) * 256

NA_WIDTH = NA_HEADS * HEAD_DIM
DA_QK_WIDTH = DA_HEADS * 2 * HEAD_DIM
DA_V_WIDTH = DA_HEADS * DA_VDIM
EVEN_IN_2 = 3 * NA_WIDTH + 2 * DA_QK_WIDTH + DA_V_WIDTH
EVEN_MIX = NA_WIDTH + DA_V_WIDTH
GQA_Q_WIDTH = GQA_Q_HEADS * HEAD_DIM
GQA_KV_WIDTH = GQA_KV_HEADS * HEAD_DIM
ODD_IN = GQA_Q_WIDTH + 2 * GQA_KV_WIDTH + 3 * HY_WIDTH
ODD_MIX = GQA_Q_WIDTH + HY_WIDTH
N_EVEN_2 = (DEPTH + 1) // 2
N_ODD_2 = DEPTH // 2


F32 = jnp.float32

def rms_norm(x, gain=None):
    xf = x.astype(F32)
    y = xf * lax.rsqrt(jnp.mean(xf * xf, axis=-1, keepdims=True) + EPS)
    if gain is not None:
        y = y * gain.astype(F32)
    return y.astype(x.dtype)

def modulate(x, shift, scale):
    return rms_norm(x) * (1 + scale) + shift

def split_heads(x, n, d):
    b, l = x.shape[:2]
    return x.reshape(b, l, n, d).transpose(0, 2, 1, 3)

def merge_heads(x):
    b, h, l, d = x.shape
    return x.transpose(0, 2, 1, 3).reshape(b, l, h * d)

def dwconv3(x, w, b):
    xp = jnp.pad(x, ((0, 0), (1, 1), (0, 0)))
    return xp[:, :-2] * w[0] + xp[:, 1:-1] * w[1] + xp[:, 2:] * w[2] + b

def axial_rope(length, head_dim):
    t = jnp.arange(length, dtype=jnp.int32)
    row = (t // GRID_W).astype(F32)
    col = (t % GRID_W).astype(F32)
    n_pairs = head_dim // 4
    inv_freq = ROPE_THETA ** (-jnp.arange(n_pairs, dtype=F32) / n_pairs)
    ang = jnp.concatenate([row[:, None] * inv_freq, col[:, None] * inv_freq], axis=-1)
    return jnp.cos(ang), jnp.sin(ang)

def apply_rope(x, cos, sin):
    xf = x.astype(F32).reshape(x.shape[:-1] + (x.shape[-1] // 2, 2))
    x0, x1 = xf[..., 0], xf[..., 1]
    out = jnp.stack([x0 * cos - x1 * sin, x0 * sin + x1 * cos], axis=-1)
    return out.reshape(x.shape).astype(x.dtype)

def sweep_query_blocks(fn, *qs):
    b, h, l = qs[0].shape[:3]
    n = l // Q_BLOCK
    blocks = tuple(jnp.moveaxis(q.reshape(b, h, n, Q_BLOCK, q.shape[-1]), 2, 0) for q in qs)
    out = lax.map(lambda qb: fn(*qb), blocks)
    return jnp.moveaxis(out, 0, 2).reshape(b, h, l, out.shape[-1])

def attend(q, k, v):
    scale = q.shape[-1] ** -0.5
    s = jnp.einsum('bhqd,bhsd->bhqs', q, k).astype(F32) * scale
    p = jax.nn.softmax(s, axis=-1).astype(v.dtype)
    return jnp.einsum('bhqs,bhsd->bhqd', p, v)

def diff_attend(q1, q2, k1, k2, v, lam):
    scale = q1.shape[-1] ** -0.5
    p1 = jax.nn.softmax(jnp.einsum('bhqd,bhsd->bhqs', q1, k1).astype(F32) * scale, axis=-1)
    p2 = jax.nn.softmax(jnp.einsum('bhqd,bhsd->bhqs', q2, k2).astype(F32) * scale, axis=-1)
    return jnp.einsum('bhqs,bhsd->bhqd', (p1 - lam * p2).astype(v.dtype), v)

def gqa_attend(q, k, v):
    b, hq, nq, d = q.shape
    hkv = k.shape[1]
    qg = q.reshape(b, hkv, hq // hkv, nq, d)
    s = jnp.einsum('bkgqd,bksd->bkgqs', qg, k).astype(F32) * (d ** -0.5)
    p = jax.nn.softmax(s, axis=-1).astype(v.dtype)
    return jnp.einsum('bkgqs,bksd->bkgqd', p, v).reshape(b, hq, nq, d)

def neighbourhood_attention(q, k, v, k_ctx, v_ctx, rpb):
    b, h, l, d = q.shape
    rows = l // GRID_W
    win_r = min(NA_WIN_R, rows)
    n_win = win_r * NA_WIN_C
    scale = d ** -0.5
    qg = q.reshape(b, h, rows, GRID_W, d)
    kg = k.reshape(b, h, rows, GRID_W, d)
    vg = v.reshape(b, h, rows, GRID_W, d)
    row_start = jnp.clip(jnp.arange(rows) - win_r // 2, 0, rows - win_r)
    col_ids = jnp.arange(GRID_W)
    col_start = jnp.clip(col_ids - NA_WIN_C // 2, 0, GRID_W - NA_WIN_C)
    col_idx = col_start[:, None] + jnp.arange(NA_WIN_C)
    col_off = col_idx - col_ids[:, None] + NA_WIN_C - 1
    rpb32 = rpb.astype(F32)

    def one_row(args):
        q_row, r, r0 = args
        k_rows = lax.dynamic_slice_in_dim(kg, r0, win_r, axis=2)
        v_rows = lax.dynamic_slice_in_dim(vg, r0, win_r, axis=2)
        k_win = k_rows[:, :, :, col_idx]
        v_win = v_rows[:, :, :, col_idx]
        row_off = r0 + jnp.arange(win_r) - r + NA_WIN_R - 1
        bias = rpb32[:, row_off[None, :, None], col_off[:, None, :]]
        s_win = jnp.einsum('bhwd,bhrwcd->bhwrc', q_row, k_win).astype(F32) * scale + bias
        s_ctx = jnp.einsum('bhwd,bhsd->bhws', q_row, k_ctx).astype(F32) * scale
        s = jnp.concatenate([s_win.reshape(b, h, GRID_W, n_win), s_ctx], axis=-1)
        p = jax.nn.softmax(s, axis=-1).astype(v.dtype)
        p_win = p[..., :n_win].reshape(b, h, GRID_W, win_r, NA_WIN_C)
        return (jnp.einsum('bhwrc,bhrwcd->bhwd', p_win, v_win)
                + jnp.einsum('bhws,bhsd->bhwd', p[..., n_win:], v_ctx))

    out = lax.map(one_row, (jnp.moveaxis(qg, 2, 0), jnp.arange(rows), row_start))
    return jnp.moveaxis(out, 0, 2).reshape(b, h, l, d)

def hyena_filter(length, w1, b1, w2, b2, w3, b3, w4, freq):
    t = jnp.linspace(0.0, 1.0, length, dtype=F32)[:, None]
    bands = (HY_EMB_DIM - 1) // 2
    w = 2.0 * math.pi * jnp.arange(length, dtype=F32)[:, None] / length
    f = jnp.linspace(1e-4, bands - 1, bands, dtype=F32)[None, :]
    z = jnp.concatenate([t, jnp.cos(f * w), -jnp.sin(f * w)], axis=-1)
    fr = freq.astype(F32)
    hdn = jnp.sin(fr * (z @ w1.astype(F32) + b1.astype(F32)))
    hdn = jnp.sin(fr * (hdn @ w2.astype(F32) + b2.astype(F32)))
    hdn = jnp.sin(fr * (hdn @ w3.astype(F32) + b3.astype(F32)))
    hdn = hdn @ w4.astype(F32)
    max_decay = math.log(HY_DECAY_TARGET) / HY_FAST_DECAY
    min_decay = math.log(HY_DECAY_TARGET) / HY_SLOW_DECAY
    deltas = jnp.linspace(min_decay, max_decay, HY_WIDTH, dtype=F32)
    decay = jnp.exp(-t * jnp.abs(deltas))
    h_fwd = hdn[:, :HY_WIDTH] * decay
    h_bwd = hdn[:, HY_WIDTH:] * decay
    k_two = jnp.concatenate([h_fwd, jnp.zeros((1, HY_WIDTH), F32), h_bwd[:0:-1]], axis=0)
    return k_two / jnp.sum(jnp.abs(k_two), axis=0, keepdims=True)

def hyena(u, conv_w, conv_b, w1, b1, w2, b2, w3, b3, w4, freq, skip):
    length = u.shape[1]
    u = dwconv3(u, conv_w, conv_b)
    x0, x1, val = jnp.split(u, 3, axis=-1)
    z = (val * x1).astype(F32)
    kf = jnp.fft.rfft(hyena_filter(length, w1, b1, w2, b2, w3, b3, w4, freq), n=2 * length, axis=0)
    zf = jnp.fft.rfft(z, n=2 * length, axis=1)
    y = jnp.fft.irfft(zf * kf, n=2 * length, axis=1)[:, :length]
    return (x0.astype(F32) * (y + skip.astype(F32) * z)).astype(u.dtype)

def even_mixer(h_l, h_c, w_in, w_out, na_qg, na_kg, rpb, da_qg, da_kg, lq1, lk1, lq2, lk2, subln,
               lam_init, cos, sin, with_ctx):
    offs = [NA_WIDTH, 2 * NA_WIDTH, 3 * NA_WIDTH, 3 * NA_WIDTH + DA_QK_WIDTH, 3 * NA_WIDTH + 2 * DA_QK_WIDTH]
    qa_l, ka_l, va_l, qb_l, kb_l, vb_l = jnp.split(h_l @ w_in, offs, axis=-1)
    qa_c, ka_c, va_c, qb_c, kb_c, vb_c = jnp.split(h_c @ w_in, offs, axis=-1)
    qa_l = rms_norm(split_heads(qa_l, NA_HEADS, HEAD_DIM), na_qg)
    ka_l = rms_norm(split_heads(ka_l, NA_HEADS, HEAD_DIM), na_kg)
    va_l = split_heads(va_l, NA_HEADS, HEAD_DIM)
    ka_c = rms_norm(split_heads(ka_c, NA_HEADS, HEAD_DIM), na_kg)
    va_c = split_heads(va_c, NA_HEADS, HEAD_DIM)
    ya_l = neighbourhood_attention(qa_l, ka_l, va_l, ka_c, va_c, rpb)
    lam = (jnp.exp(jnp.sum(lq1.astype(F32) * lk1.astype(F32)))
           - jnp.exp(jnp.sum(lq2.astype(F32) * lk2.astype(F32))) + lam_init)
    qb_l = apply_rope(rms_norm(split_heads(qb_l, 2 * DA_HEADS, HEAD_DIM), da_qg), cos, sin)
    kb_l = apply_rope(rms_norm(split_heads(kb_l, 2 * DA_HEADS, HEAD_DIM), da_kg), cos, sin)
    vb_l = split_heads(vb_l, DA_HEADS, DA_VDIM)
    kb_c = rms_norm(split_heads(kb_c, 2 * DA_HEADS, HEAD_DIM), da_kg)
    vb_c = split_heads(vb_c, DA_HEADS, DA_VDIM)
    k1_all = jnp.concatenate([kb_l[:, 0::2], kb_c[:, 0::2]], axis=2)
    k2_all = jnp.concatenate([kb_l[:, 1::2], kb_c[:, 1::2]], axis=2)
    v_all = jnp.concatenate([vb_l, vb_c], axis=2)
    yb_l = sweep_query_blocks(lambda q1, q2: diff_attend(q1, q2, k1_all, k2_all, v_all, lam),
                              qb_l[:, 0::2], qb_l[:, 1::2])
    y_l = jnp.concatenate([merge_heads(ya_l), merge_heads(rms_norm(yb_l, subln) * (1.0 - lam_init))],
                          axis=-1) @ w_out
    if not with_ctx:
        return y_l, None
    qa_c = rms_norm(split_heads(qa_c, NA_HEADS, HEAD_DIM), na_qg)
    ya_c = attend(qa_c, ka_c, va_c)
    qb_c = rms_norm(split_heads(qb_c, 2 * DA_HEADS, HEAD_DIM), da_qg)
    yb_c = diff_attend(qb_c[:, 0::2], qb_c[:, 1::2], kb_c[:, 0::2], kb_c[:, 1::2], vb_c, lam)
    y_c = jnp.concatenate([merge_heads(ya_c), merge_heads(rms_norm(yb_c, subln) * (1.0 - lam_init))],
                          axis=-1) @ w_out
    return y_l, y_c

def odd_mixer(h_l, h_c, w_in, w_out, qg, kg, conv_w, conv_b, w1, b1, w2, b2, w3, b3, w4, freq, skip,
              cos, sin, with_ctx):
    offs = [GQA_Q_WIDTH, GQA_Q_WIDTH + GQA_KV_WIDTH, GQA_Q_WIDTH + 2 * GQA_KV_WIDTH]
    q_l, k_l, v_l, hy_l = jnp.split(h_l @ w_in, offs, axis=-1)
    q_c, k_c, v_c, hy_c = jnp.split(h_c @ w_in, offs, axis=-1)
    q_l = apply_rope(rms_norm(split_heads(q_l, GQA_Q_HEADS, HEAD_DIM), qg), cos, sin)
    k_l = apply_rope(rms_norm(split_heads(k_l, GQA_KV_HEADS, HEAD_DIM), kg), cos, sin)
    v_l = split_heads(v_l, GQA_KV_HEADS, HEAD_DIM)
    k_c = rms_norm(split_heads(k_c, GQA_KV_HEADS, HEAD_DIM), kg)
    v_c = split_heads(v_c, GQA_KV_HEADS, HEAD_DIM)
    k_all = jnp.concatenate([k_l, k_c], axis=2)
    v_all = jnp.concatenate([v_l, v_c], axis=2)
    yc_l = sweep_query_blocks(lambda qb: gqa_attend(qb, k_all, v_all), q_l)
    yd_l = hyena(hy_l, conv_w, conv_b, w1, b1, w2, b2, w3, b3, w4, freq, skip)
    y_l = jnp.concatenate([merge_heads(yc_l), yd_l], axis=-1) @ w_out
    if not with_ctx:
        return y_l, None
    q_c = rms_norm(split_heads(q_c, GQA_Q_HEADS, HEAD_DIM), qg)
    yc_c = gqa_attend(q_c, k_c, v_c)
    yd_c = hyena(hy_c, conv_w, conv_b, w1, b1, w2, b2, w3, b3, w4, freq, skip)
    y_c = jnp.concatenate([merge_heads(yc_c), yd_c], axis=-1) @ w_out
    return y_l, y_c

def conv_ffn(h, w_up, conv_w, conv_b, w_down):
    g, v = jnp.split(h @ w_up, 2, axis=-1)
    g = dwconv3(g, conv_w, conv_b)
    return (jax.nn.silu(g) * v) @ w_down

def second_inputs(seed: int = 0) -> dict:
    key = jax.random.key(seed)
    D = D_MODEL
    specs = [
        ('x', (BATCH, SEQ, D), 1.0, 0.0),
        ('c', (BATCH, D), 1.0, 0.0),
        ('ctx', (BATCH, CTX_LEN, D), 1.0, 0.0),
        ('c_ctx', (D,), 1.0, 0.0),
        ('w_ada', (DEPTH, D, 6 * D), D ** -0.5, 0.0),
        ('b_ada', (DEPTH, 6 * D), 0.02, 0.0),
        ('w_up', (DEPTH, D, 2 * FFN_HIDDEN), D ** -0.5, 0.0),
        ('ffn_conv_w', (DEPTH, 3, FFN_HIDDEN), 3 ** -0.5, 0.0),
        ('ffn_conv_b', (DEPTH, FFN_HIDDEN), 0.02, 0.0),
        ('w_down', (DEPTH, FFN_HIDDEN, D), FFN_HIDDEN ** -0.5, 0.0),
        ('w_in_e', (N_EVEN_2, D, EVEN_IN_2), D ** -0.5, 0.0),
        ('w_out_e', (N_EVEN_2, EVEN_MIX, D), EVEN_MIX ** -0.5, 0.0),
        ('na_q_gain', (N_EVEN_2, HEAD_DIM), 0.05, 1.0),
        ('na_k_gain', (N_EVEN_2, HEAD_DIM), 0.05, 1.0),
        ('na_rpb', (N_EVEN_2, NA_HEADS, 2 * NA_WIN_R - 1, 2 * NA_WIN_C - 1), 0.02, 0.0),
        ('da_q_gain', (N_EVEN_2, HEAD_DIM), 0.05, 1.0),
        ('da_k_gain', (N_EVEN_2, HEAD_DIM), 0.05, 1.0),
        ('da_lambda_q1', (N_EVEN_2, HEAD_DIM), 0.1, 0.0),
        ('da_lambda_k1', (N_EVEN_2, HEAD_DIM), 0.1, 0.0),
        ('da_lambda_q2', (N_EVEN_2, HEAD_DIM), 0.1, 0.0),
        ('da_lambda_k2', (N_EVEN_2, HEAD_DIM), 0.1, 0.0),
        ('da_subln_gain', (N_EVEN_2, DA_VDIM), 0.05, 1.0),
        ('w_in_o', (N_ODD_2, D, ODD_IN), D ** -0.5, 0.0),
        ('w_out_o', (N_ODD_2, ODD_MIX, D), ODD_MIX ** -0.5, 0.0),
        ('gqa_q_gain', (N_ODD_2, HEAD_DIM), 0.05, 1.0),
        ('gqa_k_gain', (N_ODD_2, HEAD_DIM), 0.05, 1.0),
        ('hy_conv_w', (N_ODD_2, 3, 3 * HY_WIDTH), 3 ** -0.5, 0.0),
        ('hy_conv_b', (N_ODD_2, 3 * HY_WIDTH), 0.02, 0.0),
        ('hy_w1', (N_ODD_2, HY_EMB_DIM, HY_FILTER_ORDER), HY_EMB_DIM ** -0.5, 0.0),
        ('hy_b1', (N_ODD_2, HY_FILTER_ORDER), HY_EMB_DIM ** -0.5, 0.0),
        ('hy_w2', (N_ODD_2, HY_FILTER_ORDER, HY_FILTER_ORDER), HY_FILTER_ORDER ** -0.5, 0.0),
        ('hy_b2', (N_ODD_2, HY_FILTER_ORDER), HY_FILTER_ORDER ** -0.5, 0.0),
        ('hy_w3', (N_ODD_2, HY_FILTER_ORDER, HY_FILTER_ORDER), HY_FILTER_ORDER ** -0.5, 0.0),
        ('hy_b3', (N_ODD_2, HY_FILTER_ORDER), HY_FILTER_ORDER ** -0.5, 0.0),
        ('hy_w4', (N_ODD_2, HY_FILTER_ORDER, 2 * HY_WIDTH), HY_FILTER_ORDER ** -0.5, 0.0),
        ('hy_freq', (N_ODD_2, HY_FILTER_ORDER), 0.05, 1.0),
        ('hy_skip', (N_ODD_2, HY_WIDTH), 1.0, 0.0),
    ]
    keys = jax.random.split(key, len(specs))
    return {name: off + scale * jax.random.normal(keys[i], shape, F32)
            for i, (name, shape, scale, off) in enumerate(specs)}

def second_block(x, c, ctx, c_ctx, w_ada, b_ada, w_up, ffn_conv_w, ffn_conv_b, w_down, w_in_e, w_out_e,
              na_q_gain, na_k_gain, na_rpb, da_q_gain, da_k_gain, da_lambda_q1, da_lambda_k1, da_lambda_q2,
              da_lambda_k2, da_subln_gain, w_in_o, w_out_o, gqa_q_gain, gqa_k_gain, hy_conv_w, hy_conv_b,
              hy_w1, hy_b1, hy_w2, hy_b2, hy_w3, hy_b3, hy_w4, hy_freq, hy_skip):
    cos, sin = axial_rope(x.shape[1], HEAD_DIM)
    x_l, x_c = x, ctx
    for layer in range(DEPTH):
        with_ctx = layer < DEPTH - 1
        mod_l = (jax.nn.silu(c) @ w_ada[layer] + b_ada[layer])[:, None, :]
        mod_c = jax.nn.silu(c_ctx) @ w_ada[layer] + b_ada[layer]
        sh1_l, sc1_l, g1_l, sh2_l, sc2_l, g2_l = jnp.split(mod_l, 6, axis=-1)
        sh1_c, sc1_c, g1_c, sh2_c, sc2_c, g2_c = jnp.split(mod_c, 6, axis=-1)
        h_l = modulate(x_l, sh1_l, sc1_l)
        h_c = modulate(x_c, sh1_c, sc1_c)
        i = layer // 2
        if layer % 2 == 0:
            lam_init = 0.8 - 0.6 * math.exp(-0.3 * layer)
            y_l, y_c = even_mixer(h_l, h_c, w_in_e[i], w_out_e[i], na_q_gain[i], na_k_gain[i], na_rpb[i],
                                  da_q_gain[i], da_k_gain[i], da_lambda_q1[i], da_lambda_k1[i],
                                  da_lambda_q2[i], da_lambda_k2[i], da_subln_gain[i], lam_init, cos, sin,
                                  with_ctx)
        else:
            y_l, y_c = odd_mixer(h_l, h_c, w_in_o[i], w_out_o[i], gqa_q_gain[i], gqa_k_gain[i],
                                 hy_conv_w[i], hy_conv_b[i], hy_w1[i], hy_b1[i], hy_w2[i], hy_b2[i],
                                 hy_w3[i], hy_b3[i], hy_w4[i], hy_freq[i], hy_skip[i], cos, sin, with_ctx)
        x_l = x_l + g1_l * y_l
        x_l = x_l + g2_l * conv_ffn(modulate(x_l, sh2_l, sc2_l), w_up[layer], ffn_conv_w[layer],
                                    ffn_conv_b[layer], w_down[layer])
        if with_ctx:
            x_c = x_c + g1_c * y_c
            x_c = x_c + g2_c * conv_ffn(modulate(x_c, sh2_c, sc2_c), w_up[layer], ffn_conv_w[layer],
                                        ffn_conv_b[layer], w_down[layer])
    return x_l


def setup_inputs(seed=0):
    out = dict(first_inputs(seed))
    for name, value in second_inputs(seed + 1).items():
        if name != "x":
            out[name + "_2"] = value
    return out


def reference(
    x, p, norm_mix_g, norm_ffn_g, even_w_in, rwkv_mu_proj, rwkv_mu_lora, rwkv_w0, rwkv_w1,
    rwkv_w2, rwkv_a0, rwkv_a1, rwkv_a2, rwkv_g1, rwkv_g2, rwkv_k_k, rwkv_k_a, rwkv_r_k,
    rwkv_ln_g, rwkv_ln_b, rwkv_v_mu, rwkv_v0, rwkv_v1, rwkv_v2, gdn_conv_w, gdn_a_log,
    gdn_dt_bias, gdn_norm_g, even_w_out, attn_w_qkv, attn_q_g, attn_k_g, attn_rel_bias,
    attn_w_out, mlp_w1, mlp_w2, ple_w_proj, ple_norm_g, ple_w_gate, c_2, ctx_2, c_ctx_2,
    w_ada_2, b_ada_2, w_up_2, ffn_conv_w_2, ffn_conv_b_2, w_down_2, w_in_e_2, w_out_e_2,
    na_q_gain_2, na_k_gain_2, na_rpb_2, da_q_gain_2, da_k_gain_2, da_lambda_q1_2,
    da_lambda_k1_2, da_lambda_q2_2, da_lambda_k2_2, da_subln_gain_2, w_in_o_2, w_out_o_2,
    gqa_q_gain_2, gqa_k_gain_2, hy_conv_w_2, hy_conv_b_2, hy_w1_2, hy_b1_2, hy_w2_2, hy_b2_2,
    hy_w3_2, hy_b3_2, hy_w4_2, hy_freq_2, hy_skip_2,
):
    x = first_block(
        x, p, norm_mix_g, norm_ffn_g, even_w_in, rwkv_mu_proj, rwkv_mu_lora, rwkv_w0, rwkv_w1,
        rwkv_w2, rwkv_a0, rwkv_a1, rwkv_a2, rwkv_g1, rwkv_g2, rwkv_k_k, rwkv_k_a, rwkv_r_k,
        rwkv_ln_g, rwkv_ln_b, rwkv_v_mu, rwkv_v0, rwkv_v1, rwkv_v2, gdn_conv_w, gdn_a_log,
        gdn_dt_bias, gdn_norm_g, even_w_out, attn_w_qkv, attn_q_g, attn_k_g, attn_rel_bias,
        attn_w_out, mlp_w1, mlp_w2, ple_w_proj, ple_norm_g, ple_w_gate,
    )
    return second_block(
        x, c_2, ctx_2, c_ctx_2, w_ada_2, b_ada_2, w_up_2, ffn_conv_w_2, ffn_conv_b_2, w_down_2,
        w_in_e_2, w_out_e_2, na_q_gain_2, na_k_gain_2, na_rpb_2, da_q_gain_2, da_k_gain_2,
        da_lambda_q1_2, da_lambda_k1_2, da_lambda_q2_2, da_lambda_k2_2, da_subln_gain_2,
        w_in_o_2, w_out_o_2, gqa_q_gain_2, gqa_k_gain_2, hy_conv_w_2, hy_conv_b_2, hy_w1_2,
        hy_b1_2, hy_w2_2, hy_b2_2, hy_w3_2, hy_b3_2, hy_w4_2, hy_freq_2, hy_skip_2,
    )


_drawn_inputs = setup_inputs


def setup_inputs(seed=0):
    import zlib

    import numpy as np

    out = dict(_drawn_inputs(seed))
    spreads = {}
    factors = {'rwkv_w1': 5.432,
     'rwkv_w2': 5.354,
     'rwkv_k_k': 3.618,
     'rwkv_ln_g': 2.963,
     'rwkv_ln_b': 6.437,
     'gdn_norm_g': 2.847,
     'attn_q_g': 8.0,
     'attn_k_g': 8.0,
     'ffn_conv_b_2': 8.0,
     'na_q_gain_2': 8.0,
     'na_k_gain_2': 8.0,
     'na_rpb_2': 200.0,
     'da_q_gain_2': 8.0,
     'da_k_gain_2': 8.0,
     'da_lambda_q1_2': 8.0,
     'da_lambda_k1_2': 6.979,
     'da_lambda_q2_2': 8.0,
     'da_lambda_k2_2': 8.0,
     'da_subln_gain_2': 6.721,
     'gqa_q_gain_2': 8.0,
     'gqa_k_gain_2': 8.0,
     'hy_conv_b_2': 5.446,
     'hy_freq_2': 8.0}
    for name, (base, spread) in spreads.items():
        noise = np.random.default_rng([zlib.crc32(name.encode()), seed]).standard_normal(out[name].shape)
        drawn = base * np.exp(spread * noise) if base else spread * noise
        out[name] = jnp.asarray(drawn.astype(out[name].dtype))
    for name, factor in factors.items():
        out[name] = (out[name] * factor).astype(out[name].dtype)
    return out
```

```python
from contextlib import ExitStack
import math

import numpy as np
import concourse.bass as bass
from concourse import mybir

ACT = mybir.ActivationFunctionType
ALU = mybir.AluOpType
AX = mybir.AxisListType
F32 = mybir.dt.float32

P = 128
D = 1024
KT = D // P
SEQ = 256
CH = 64
RING = 3
SLOT = 4096
NEG = -1e30


def shape_constants():
    s = np.arange(P)[:, None]
    t = np.arange(P)[None, :]
    same = (s // CH) == (t // CH)
    c = {
        "ident": np.eye(P),
        "ones": np.ones((P, P)),
        "head_ones": same,
        "upto": same & (s <= t),
        "before": same & (s < t),
        "head_pick": (s // CH) == np.arange(2)[None, :],
        "flip": s == P - 1 - t,
        "flip64": same & (s % CH == CH - 1 - t % CH),
    }
    for k in range(6):
        c[f"pair{k}"] = ((s >> (k + 1)) == (t >> (k + 1))) & (((s >> k) & 1) == 0) & (((t >> k) & 1) == 1)
    rot = np.zeros((P, P))
    rot[np.arange(1, P, 2), np.arange(0, P, 2)] = -1.0
    rot[np.arange(0, P, 2), np.arange(1, P, 2)] = 1.0
    c["rotate_pairs"] = rot
    c["carry"] = np.broadcast_to(np.arange(SEQ) % CH != 0, (P, SEQ))
    for i in range(2):
        c[f"stream{i}"] = np.broadcast_to(s == i, (P, P))
    c["late_query"] = np.broadcast_to(t < CH, (P, P))
    c["late_key"] = np.broadcast_to(np.where(t >= CH, NEG, 0.0), (P, P))
    for name, v in (("eps", 1e-6), ("gn_eps", 64e-5), ("one", 1.0)):
        c[name] = np.full((P, 1), v)
    return {k: np.ascontiguousarray(v, dtype=np.float32) for k, v in c.items()}


def rope_constants():
    tok = np.arange(SEQ)
    inv = 10000.0 ** (-np.arange(16, dtype=np.float32) / np.float32(16))
    ang = np.concatenate([(tok // 64)[:, None] * inv, (tok % 64)[:, None] * inv], -1).astype(np.float32)
    ang = np.repeat(ang.T, 2, axis=0)
    ang = np.concatenate([ang, ang], 0)
    return np.concatenate([np.cos(ang), np.sin(ang)], 1).astype(np.float32)


def neighbour_mask():
    q = np.arange(64)
    start = np.clip(q - 8, 0, 48)
    m = np.where((q[None, :] >= start[:, None]) & (q[None, :] < start[:, None] + 16), 0.0, NEG)
    m = m[::-1]
    return np.tile(m, (2, 4)).astype(np.float32)


def hyena_constants():
    n = SEQ
    t = np.linspace(0.0, 1.0, n, dtype=np.float32)[:, None]
    w = 2.0 * math.pi * np.arange(n, dtype=np.float32)[:, None] / n
    f = np.linspace(1e-4, 15, 16, dtype=np.float32)[None, :]
    z = np.concatenate([t, np.cos(f * w), -np.sin(f * w)], -1)
    zt = np.zeros((P, n))
    zt[:33] = z.T
    deltas = np.linspace(math.log(1e-2) / 1.5, math.log(1e-2) / 0.3, 512, dtype=np.float32)
    decay = np.exp(-t * np.abs(deltas))
    back = decay.copy()
    back[0] = 0.0
    dec = np.concatenate([decay.reshape(2, P, 512), back.reshape(2, P, 512)], 0).transpose(1, 0, 2).reshape(P, -1)
    tt = np.arange(n)[:, None].astype(np.float64)
    ff = np.arange(n + 1)[None, :].astype(np.float64)
    ang = 2 * np.pi * tt * ff / (2 * n)
    fre, fim = np.cos(ang), -np.sin(ang)
    fwd = np.zeros((P, 2, 2 * n + P))
    fwd[:, :, :n] = fre[:, :n].reshape(2, P, n).transpose(1, 0, 2)
    fwd[:, :, n:2 * n] = fim[:, :n].reshape(2, P, n).transpose(1, 0, 2)
    fwd[:, :, 2 * n:2 * n + 1] = fre[:, n:].reshape(2, P, 1).transpose(1, 0, 2)
    cf = np.full((n, 1), 2.0)
    cf[0] = 1.0
    ire = cf * fre[:, :n].T / (2 * n)
    iim = cf * fim[:, :n].T / (2 * n)
    ilast = np.zeros((P, n))
    ilast[0] = fre[:, n] / (2 * n)
    inv = np.concatenate([ire.reshape(2, P, n), iim.reshape(2, P, n), ilast[None]], 0).transpose(1, 0, 2)
    return (np.ascontiguousarray(np.concatenate([zt, dec], 1), np.float32),
            np.ascontiguousarray(np.concatenate([fwd.reshape(P, -1), inv.reshape(P, -1)], 1), np.float32))


def weight_plan():
    plan = []
    plan += [(f"rkv{i}", 4096) for i in range(3)] + [("lora_in", 8 * 256), ("lora_out", 3 * 512)]
    plan += [(f"bqkv{i}", 4096) for i in range(3)] + [("bgate", 4096), ("bab", 64)]
    plan += [(f"eout{i}", 4096) for i in range(2)]

    def mlp(i):
        return ([(f"up{i}.{n}", 4096) for n in range(8)] + [(f"down{i}.{h}.{n}", 4096) for h in range(2) for n in range(4)]
                + [(f"pproj{i}", 2048)] + [(f"pgate{i}.{h}", 4096) for h in range(2)])

    def ada(i):
        return [(f"ada{i}.{n}", 4096) for n in range(12)]

    def ffn(i):
        return ([(f"cup{i}.{n}", 4096) for n in range(11)]
                + [(f"cdown{i}.{h}.{n}", 4096 if n < 2 else 3072) for h in range(2) for n in range(3)])

    plan += mlp(0) + [(f"qkv{i}", 4096) for i in range(6)] + [(f"aout{i}", 4096) for i in range(2)] + mlp(1)
    plan += ada(0) + [(f"win{i}", 4096) for i in range(6)] + [(f"wout{i}", 4096) for i in range(2)] + ffn(0)
    plan += ada(1) + [("gq", 4096), ("gkv", 8 * 256)] + [(f"hin{i}", 4096) for i in range(3)]
    plan += [("hfilter", 3 * 64 + 1024)] + [(f"oout{i}", 4096) for i in range(2)] + ffn(1)
    return plan


COLS = {}


def column_plan():
    at, out = 0, {}
    for name, n in (("mix0", 8), ("mix1", 8), ("ffn0", 8), ("ffn1", 8), ("mu_proj", 12), ("mu_lora", 24),
                    ("w0", 4), ("a0", 4), ("k_k", 4), ("k_a", 4), ("r_k", 4), ("conv", 48), ("attn_q", 1), ("attn_k", 1),
                    ("c", 16), ("fconv_w0", 66), ("fconv_b0", 22), ("fconv_w1", 66), ("fconv_b1", 22),
                    ("na_q", 1), ("na_k", 1), ("da_q", 1), ("da_k", 1), ("lam", 4), ("gqa_q", 1), ("gqa_k", 1),
                    ("hconv_w", 36), ("hconv_b", 12), ("hb", 3), ("hfreq", 1), ("hskip", 4)):
        out[name] = (at, n)
        at += n
    return out, at


ROWS = (("ln_g", 512), ("ln_b", 512), ("gdn_g", 128), ("a_log", 4), ("dt", 4), ("ple0", 1024), ("ple1", 1024),
        ("bada0", 6144), ("bada1", 6144), ("subln", 128))


def row_plan():
    at, out = 0, {}
    for name, n in ROWS:
        out[name] = (at, n)
        at += n
    return out, at


LOADS = ("start", "rwkv_rows", "gdn_rows", "ple0", "rel", "ple1", "ada0", "even", "bias", "ada1", "odd")
CPLAN, NCOL = column_plan()
RPLAN, NROW = row_plan()
CONST = shape_constants()
KPLAN = {}
_at = 0
for _k, _v in CONST.items():
    KPLAN[_k] = (_at, _v.shape[1])
    _at += _v.shape[1]
NCONST = _at


class Steps:

    def __init__(self, eng, done, marks, by=1):
        self.eng, self.done, self.marks, self.by = eng, done, marks, by
        self.n, self.seen = 0, {}

    def one(self):
        self.n += self.by
        return self.by

    def wait_ge(self, sem, n):
        key = str(sem)
        if n > self.seen.get(key, 0):
            self.eng.wait_ge(sem, n)
            self.seen[key] = n

    def mark(self, *names):
        for name in names:
            self.marks[name] = (self.done, self.n)


def build(nc, T, out, counts):
    with ExitStack() as ctx:
        def sb(name, shape):
            return ctx.enter_context(nc.sbuf_tensor(name, shape, F32))

        def sem(name):
            return ctx.enter_context(nc.semaphore(name))

        tensor_done, scalar_done, vector_done = sem("tensor_done"), sem("scalar_done"), sem("vector_done")
        slot_loaded = [sem(f"slot_loaded{i}") for i in range(RING)]
        stored = sem("stored")
        loaded = {n: sem("loaded_" + n) for n in LOADS}
        sems = {"pe": tensor_done, "act": scalar_done, "dve": vector_done, **loaded}
        marks = {}
        for k, v in counts.items():
            if k != "unknown" and k != "banks":
                marks[k] = (sems[v[0]], v[1])
        banks = counts.setdefault("banks", {})
        unknown = counts["unknown"] = set()
        marks["unknown"] = unknown

        X = sb("X", [P, 4, D])
        HT = sb("HT", [P, KT, 512])
        ring = sb("ring", [P, RING, SLOT])
        KC = sb("KC", [P, NCONST])
        CP = sb("CP", [P, NCOL])
        small = sb("small", [P, 256])
        AR = (nc.sbuf_bytes_remaining if not callable(nc.sbuf_bytes_remaining) else nc.sbuf_bytes_remaining()) // 4 - 32
        arena = sb("arena", [P, AR])
        PS = [ctx.enter_context(nc.psum_tensor(f"bank{i}", [P, 512], F32)) for i in range(8)]

        def K(name):
            a, n = KPLAN[name]
            return KC[:, a:a + n]

        def C(name, i=0, n=1):
            a, _ = CPLAN[name]
            return CP[:, a + i:a + i + n]

        def bc(ap, shape):
            return ap.unsqueeze(len(shape) - 1).broadcast_to(shape)

        def rows(ap, n):
            return ap.unsqueeze(1).broadcast_to([P, n, ap.shape[-1]])

        class Arena:
            def __init__(self, at=0):
                self.at = at

            def take(self, *shape):
                n = int(np.prod(shape))
                v = arena[:, self.at:self.at + n]
                self.at += n
                assert self.at <= AR, (self.at, AR)
                names = "abc"[:len(shape)]
                if len(shape) > 1:
                    v = v.rearrange("p (" + " ".join(names) + ") -> p " + " ".join(names),
                                    **{names[i]: shape[i] for i in range(1, len(shape))})
                return v

        SM = small
        block = ctx.enter_context(nc.Block())
        PLAN = weight_plan()
        WAT = {name: i for i, (name, _) in enumerate(PLAN)}

        def at(name):
            if name not in marks:
                unknown.add(name)
                return 0
            return marks[name][1]

        state = {"bank": 0, "last": [None] * 8, "w": 0}

        pe = Steps(nc.tensor, tensor_done, marks)
        act = Steps(nc.scalar, scalar_done, marks)
        dve = Steps(nc.vector, vector_done, marks)

        def open_bank(name):
            b = state["bank"] % 8
            state["bank"] += 1
            if state["last"][b]:
                reader, n = marks.get("read " + state["last"][b], (scalar_done, 0))
                pe.wait_ge(reader, n)
            state["last"][b] = name
            banks[name] = b
            return PS[b]

        def full(e, name):
            e.wait_ge(tensor_done, at(name))
            return PS[banks.get(name, 0)]

        def weight(name):
            i = WAT[name]
            assert i == state["w"], (name, i, state["w"])
            pe.wait_ge(slot_loaded[i % RING], 16 * (i // RING + 1))
            state["w"] += 1
            return ring[:, i % RING, :]

        def mm(out_, lhsT, rhs, start, stop):
            return nc.tensor.matmul(out_, lhsT, rhs, start=start, stop=stop, skip_group_check=True)

        def weight_used(ins, name):
            ins.then_inc(tensor_done, pe.one())
            pe.mark("slot of " + name)

        def pe_feature_block(wname, label, tok=SEQ, kt=KT, tiles=4, act_of=None, m0=0, col=None, after=None):
            w = weight(wname)
            w = w[:, 0:kt * tiles * P].rearrange("p (k c) -> p k c", k=kt)
            per = 512 // tok
            act_of = act_of or (lambda k: HT[:, k, 0:tok])
            for m in range(tiles):
                if m % per == 0:
                    ps = open_bank(f"{label}.{(m0 + m) // per}")
                for k in range(kt):
                    last = mm(ps[:, (m % per) * tok:(m % per + 1) * tok], w[:, k, m * P:(m + 1) * P], act_of(k),
                              k == 0, k == kt - 1)
                if m == tiles - 1:
                    weight_used(last, wname)
                    pe.mark(f"{label}.{(m0 + m) // per}")
                elif m % per == per - 1:
                    last.then_inc(tensor_done, pe.one())
                    pe.mark(f"{label}.{(m0 + m) // per}")

        def pe_token_blocks(wnames, kts, label, lhs, tiles=2):
            pss = []
            k0 = 0
            total = sum(kts)
            for wname, kt in zip(wnames, kts):
                w = weight(wname)[:, 0:kt * 512].rearrange("p (k c) -> p k c", k=kt)
                for t in range(tiles):
                    if k0 == 0:
                        pss.append(open_bank(f"{label}.{t}"))
                    for k in range(kt):
                        last = mm(pss[t][:, :], lhs(k0 + k, t), w[:, k, :], k0 + k == 0, k0 + k == total - 1)
                    if t == tiles - 1:
                        weight_used(last, wname)
                    elif k0 + kt == total:
                        last.then_inc(tensor_done, pe.one())
                    if k0 + kt == total:
                        pe.mark(f"{label}.{t}")
                k0 += kt

        def ht(k, t):
            return HT[:, k, t * P:(t + 1) * P]

        def pe_turn(label, srcs):
            ps = open_bank(label)
            for i, s in enumerate(srcs):
                last = nc.tensor.transpose(ps[:, i * P:(i + 1) * P], s, K("ident"))
            last.then_inc(tensor_done, pe.one())
            pe.mark(label)

        def copy_out(e, label, dst, src=None):
            ps = full(e, label)
            s = ps[:, :] if src is None else src(ps)
            if e is act:
                nc.scalar.activation(dst, s, ACT.Copy).then_inc(e.done, e.one())
            else:
                nc.vector.tensor_copy(dst, s).then_inc(e.done, e.one())
            e.mark("read " + label)

        def phase_end(e, name, me):
            if me != "pe":
                e.wait_ge(e.done, e.n)
            e.mark(f"{me} end {name}")
            for other, done in (("pe", tensor_done), ("act", scalar_done), ("dve", vector_done)):
                if other != me:
                    e.wait_ge(done, at(f"{other} end {name}"))

        tt = nc.vector.tensor_tensor
        ts = nc.vector.tensor_scalar
        stt = nc.vector.scalar_tensor_tensor
        activation = nc.scalar.activation

        SS = SM[:, 0:4]
        RS = SM[:, 4:8]

        def act_norm(label, tiles, junk):
            if tiles:
                act.wait_ge(vector_done, at(label + " x"))
            for t in tiles:
                activation(junk[:, t % 2, :], X[:, t, :], ACT.Square, accum_out=SS[:, t:t + 1]).then_inc(scalar_done, act.one())
                act.wait_ge(scalar_done, act.n)
            a, b = tiles[0], tiles[-1] + 1
            activation(RS[:, a:b], SS[:, a:b], ACT.Sqrt, bias=K("eps"), scale=1.0 / D).then_inc(scalar_done, act.one())
            act.wait_ge(scalar_done, act.n)
            act.mark(label + " rms")

        def dve_norm(label, tiles, xn, scale, shift=None):
            dve.wait_ge(vector_done, dve.n)
            dve.mark(label + " x")
            dve.wait_ge(scalar_done, at(label + " rms"))
            a, b = tiles[0], tiles[-1] + 1
            nc.vector.reciprocal(RS[:, a:b], RS[:, a:b]).then_inc(vector_done, dve.one())
            dve.wait_ge(vector_done, dve.n)

            def turned(t):
                for h in range(2):
                    n = f"{label} turned {t}.{h}"
                    ps = full(dve, n)
                    dst = HT[:, 4 * h:4 * h + 4, t * P:(t + 1) * P]
                    tt(dst, ps[:, :].rearrange("p (k c) -> p k c", k=4), bc(scale(t)[:, 4 * h:4 * h + 4], [P, 4, P]),
                         ALU.mult).then_inc(vector_done, dve.one())
                    dve.wait_ge(vector_done, dve.n)
                    dve.mark("read " + n)
                    if shift:
                        tt(dst, dst, bc(shift(t)[:, 4 * h:4 * h + 4], [P, 4, P]), ALU.add).then_inc(vector_done, dve.one())
                        dve.wait_ge(vector_done, dve.n)
                dve.mark(f"{label} ready {t}")

            for i, t in enumerate(tiles):
                if i >= 2:
                    dve.wait_ge(tensor_done, at(f"{label} turned {t - 2}.1"))
                ts(xn[:, t % 2, :], X[:, t, :], RS[:, t:t + 1], None, ALU.mult).then_inc(vector_done, dve.one())
                dve.wait_ge(vector_done, dve.n)
                dve.mark(f"{label} xn {t}")
                if i >= 1:
                    turned(tiles[i - 1])
            turned(tiles[-1])

        def pe_norm(label, tiles, xn):
            for t in tiles:
                pe.wait_ge(vector_done, at(f"{label} xn {t}"))
                for h in range(2):
                    pe_turn(f"{label} turned {t}.{h}", [xn[:, t % 2, (4 * h + i) * P:(4 * h + i + 1) * P] for i in range(4)])
            pe.wait_ge(vector_done, at(f"{label} ready {tiles[-1]}"))

        def pe_turn_all(label, src, tiles, parts=8):
            pe.wait_ge(vector_done, at(label + " src"))
            for t in tiles:
                for h in range(parts // 4):
                    pe_turn(f"{label} turned {t}.{h}", [src[:, t, (4 * h + i) * P:(4 * h + i + 1) * P] for i in range(4)])
            pe.wait_ge(scalar_done, at(label + " ready"))

        def act_turn_all(label, tiles):
            for t in tiles:
                for h in range(2):
                    n = f"{label} turned {t}.{h}"
                    ps = full(act, n)
                    activation(HT[:, 4 * h:4 * h + 4, t * P:(t + 1) * P], ps[:, :].rearrange("p (k c) -> p k c", k=4), ACT.Copy).then_inc(scalar_done, act.one())
                    act.mark("read " + n)
            act.wait_ge(scalar_done, act.n)
            act.mark(label + " ready")

        def dve_head_norm(label, src, sq, n, gains, scale=1.0):
            dve.wait_ge(vector_done, dve.n)
            tt(sq, src, src, ALU.mult).then_inc(vector_done, dve.one())
            dve.wait_ge(vector_done, dve.n)
            dve.mark(label + " sq")
            dve.wait_ge(scalar_done, at(label + " root"))
            nc.vector.reciprocal(sq, sq).then_inc(vector_done, dve.one())
            dve.wait_ge(vector_done, dve.n)
            tt(src, src, sq, ALU.mult).then_inc(vector_done, dve.one())
            dve.wait_ge(vector_done, dve.n)
            for i in range(n):
                g = gains(i)
                c = src[:, i * 512:(i + 1) * 512]
                if g is not None:
                    ts(c, c, g, scale, ALU.mult, ALU.mult).then_inc(vector_done, dve.one())
                    dve.wait_ge(vector_done, dve.n)
            dve.mark(label + " normed")

        def pe_head_norm(label, sq, n, which="head_ones"):
            pe.wait_ge(vector_done, at(label + " sq"))
            for i in range(n):
                ps = open_bank(f"{label} ss{i}")
                mm(ps[:, :], K(which), sq[:, i * 512:(i + 1) * 512], True, True).then_inc(tensor_done, pe.one())
                pe.mark(f"{label} ss{i}")

        def act_head_norm(label, sq, n, scale, eps="eps"):
            for i in range(n):
                ps = full(act, f"{label} ss{i}")
                activation(sq[:, i * 512:(i + 1) * 512], ps[:, :], ACT.Sqrt, bias=K(eps), scale=scale).then_inc(scalar_done, act.one())
                act.mark(f"read {label} ss{i}")
            act.wait_ge(scalar_done, act.n)
            act.mark(label + " root")

        def pe_solve(label, groups, XI, XT, tmp):
            for k in range(6):
                for g in range(groups):
                    lab = f"{label} {k}.{g}"
                    pe.wait_ge(vector_done, at(lab + " masked"))
                    ps = open_bank(lab + " LX")
                    for i in range(4):
                        last = mm(ps[:, i * P:(i + 1) * P], tmp[:, g % 2, i, :], XI[:, 4 * g + i, :], True, True)
                    last.then_inc(tensor_done, pe.one())
                    pe.mark(lab + " LX")
                for g in range(groups):
                    lab = f"{label} {k}.{g}"
                    pe.wait_ge(vector_done, at(lab + " LX out"))
                    ps = open_bank(lab + " XLX")
                    for i in range(4):
                        last = mm(ps[:, i * P:(i + 1) * P], XT[:, 4 * g + i, :], tmp[:, 2 + g, i, :], True, True)
                    last.then_inc(tensor_done, pe.one())
                    pe.mark(lab + " XLX")
                    ps = open_bank(lab + " XLXt")
                    for i in range(4):
                        last = mm(ps[:, i * P:(i + 1) * P], tmp[:, 2 + g, i, :], XT[:, 4 * g + i, :], True, True)
                    last.then_inc(tensor_done, pe.one())
                    pe.mark(lab + " XLXt")

        def dve_solve(label, groups, LT, XI, XT, tmp):
            for i in range(4 * groups):
                nc.vector.tensor_copy(XI[:, i, :], K("ident")).then_inc(vector_done, dve.one())
                nc.vector.tensor_copy(XT[:, i, :], K("ident")).then_inc(vector_done, dve.one())
            dve.wait_ge(vector_done, dve.n)
            for k in range(6):
                for g in range(groups):
                    lab = f"{label} {k}.{g}"
                    if g >= 2:
                        dve.wait_ge(tensor_done, at(f"{label} {k}.{g - 2} LX"))
                    elif k > 0:
                        dve.wait_ge(tensor_done, at(f"{label} {k - 1}.{groups - 1} XLX"))
                    tt(tmp[:, g % 2, :, :], LT[:, 4 * g:4 * g + 4, :], rows(K(f"pair{k}"), 4), ALU.mult).then_inc(vector_done, dve.one())
                    dve.wait_ge(vector_done, dve.n)
                    dve.mark(lab + " masked")
                    if g >= 1:
                        copy_out(dve, f"{label} {k}.{g - 1} LX", tmp[:, 1 + g, :, :],
                                 lambda ps: ps[:, :].rearrange("p (k c) -> p k c", k=4))
                        dve.mark(f"{label} {k}.{g - 1} LX out")
                copy_out(dve, f"{label} {k}.{groups - 1} LX", tmp[:, 1 + groups, :, :],
                         lambda ps: ps[:, :].rearrange("p (k c) -> p k c", k=4))
                dve.wait_ge(vector_done, dve.n)
                dve.mark(f"{label} {k}.{groups - 1} LX out")
                for g in range(groups):
                    lab = f"{label} {k}.{g}"
                    dve.wait_ge(tensor_done, at(lab + " XLXt"))
                    for M, n in ((XI, lab + " XLX"), (XT, lab + " XLXt")):
                        ps = full(dve, n)
                        tt(M[:, 4 * g:4 * g + 4, :], M[:, 4 * g:4 * g + 4, :],
                              ps[:, :].rearrange("p (k c) -> p k c", k=4), ALU.add).then_inc(vector_done, dve.one())
                        dve.mark("read " + n)
                dve.wait_ge(vector_done, dve.n)
            dve.mark(label + " solved")

        def unit_buffers(ar, dv=P):
            return {"P": ar.take(2, 512), "PT": ar.take(2, 512), "st": ar.take(2, 4)}

        def pe_attention(label, units, B):
            n = len(units)
            for i in range(n + 2):
                if i < n:
                    u = units[i]
                    ps = open_bank(f"{label} s{i}")
                    calls = [(ps[:, a:b], u["q"], k) for a, b, k in u["k"]] + [(ps[:, a:b], l, r) for a, b, l, r in u.get("bias", [])]
                    nb = len(calls)
                    for j, (o, l, r) in enumerate(calls):
                        first = j < len(u["k"])
                        last = mm(o, l, r, first, (not first) or not u.get("bias"))
                    last.then_inc(tensor_done, pe.one())
                    pe.mark(f"{label} s{i}")
                if 1 <= i <= n:
                    j = i - 1
                    pe.wait_ge(scalar_done, at(f"{label} p{j}"))
                    ps = open_bank(f"{label} pt{j}")
                    for a in range(0, units[j]["nk"], P):
                        last = nc.tensor.transpose(ps[:, a:a + P], B["P"][:, j % 2, a:a + P], K("ident"))
                    last.then_inc(tensor_done, pe.one())
                    pe.mark(f"{label} pt{j}")
                if i >= 2:
                    j = i - 2
                    u = units[j]
                    pe.wait_ge(vector_done, at(f"{label} pt out{j}"))
                    ps = open_bank(f"{label} o{j}")
                    nk = len(u["v"])
                    for a, v in enumerate(u["v"]):
                        last = mm(ps[:, 0:u["dv"]], B["PT"][:, j % 2, a * P:(a + 1) * P], v, a == 0, a == nk - 1)
                    last.then_inc(tensor_done, pe.one())
                    pe.mark(f"{label} o{j}")

        def act_attention(label, units, B):
            for i, u in enumerate(units):
                act.wait_ge(tensor_done, at(f"{label} s{i}"))
                act.wait_ge(vector_done, at(f"{label} max{i}"))
                if i >= 2:
                    act.wait_ge(tensor_done, at(f"{label} pt{i - 2}"))
                    act.wait_ge(vector_done, at(f"{label} inv{i - 2}"))
                ps = PS[banks.get(f"{label} s{i}", 0)]
                activation(B["P"][:, i % 2, 0:u["nk"]], ps[:, 0:u["nk"]], ACT.Exp, bias=B["st"][:, i % 2, 0:1],
                       accum_out=B["st"][:, i % 2, 1:2]).then_inc(scalar_done, act.one())
                act.wait_ge(scalar_done, act.n)
                act.mark(f"read {label} s{i}", f"{label} p{i}")

        def dve_attention(label, units, B):
            n = len(units)
            for i in range(n + 2):
                if i < n:
                    u = units[i]
                    ps = full(dve, f"{label} s{i}")
                    if i >= 2:
                        dve.wait_ge(scalar_done, at(f"{label} p{i - 2}"))
                    dve.wait_ge(vector_done, dve.n)
                    nc.vector.tensor_reduce(B["st"][:, i % 2, 0:1], ps[:, 0:u["nk"]], AX.X, ALU.max, negate=True).then_inc(vector_done, dve.one())
                    dve.wait_ge(vector_done, dve.n)
                    dve.mark(f"{label} max{i}")
                if 1 <= i <= n:
                    j = i - 1
                    if j >= 2:
                        dve.wait_ge(tensor_done, at(f"{label} o{j - 2}"))
                    copy_out(dve, f"{label} pt{j}", B["PT"][:, j % 2, 0:units[j]["nk"]], lambda p: p[:, 0:units[j]["nk"]])
                    dve.mark(f"{label} pt out{j}")
                    dve.wait_ge(vector_done, dve.n)
                    nc.vector.reciprocal(B["st"][:, j % 2, 2:3], B["st"][:, j % 2, 1:2]).then_inc(vector_done, dve.one())
                    dve.wait_ge(vector_done, dve.n)
                    dve.mark(f"{label} inv{j}")
                if i >= 2:
                    j = i - 2
                    u = units[j]
                    ps = full(dve, f"{label} o{j}")
                    ts(u["o"], ps[:, 0:u["dv"]], B["st"][:, j % 2, 2:3], None, ALU.mult).then_inc(vector_done, dve.one())
                    dve.mark(f"read {label} o{j}")
            dve.wait_ge(vector_done, dve.n)
            dve.mark(label + " done")

        def k4(ap):
            return ap.rearrange("p (k c) -> p k c", k=4)

        def flat(ap):
            return ap.rearrange("p a b -> p (a b)")

        ar = Arena()
        R1 = {}
        for n in ("R", "Kf", "Vf", "AV", "KK", "WI", "WN", "TMP"):
            R1[n] = ar.take(4, SEQ)
        R, KF, VF, AV, KK, WI, WN, TMP = (R1[n] for n in ("R", "Kf", "Vf", "AV", "KK", "WI", "WN", "TMP"))
        YA = ar.take(2, 512)
        GA = ar.take(2, 512)
        YB = ar.take(2, 512)
        base1 = ar.at
        VT, AT_, BT, KTM = (ar.take(2, 512) for _ in range(4))
        MRB, MRK = ar.take(16, P), ar.take(16, P)
        LT1, XI1, XT1 = ar.take(16, P), ar.take(16, P), ar.take(16, P)
        T1 = ar.take(6, 4 * P)
        T1v = T1.rearrange("p a (c d) -> p a c d", c=4)
        ar2 = Arena(base1)
        XN1 = ar2.take(2, D)
        DH = ar2.take(KT, SEQ)
        XW = [ar2.take(KT, SEQ) for _ in range(3)]
        ar2b = XW[0].rearrange("p a b -> p (a b)").rearrange("p (a b) -> p a b", a=2)
        LO = [ar2.take(SEQ) for _ in range(3)]
        LAK = XI1
        PU = T1[:, 0:2, :]
        APT = TMP
        AT_T = AT_
        SAs = LT1.rearrange("p a b -> p (a b)")[:, 0:512]
        ST = LT1.rearrange("p a b -> p (a b)")[:, 512:768]
        SQ1 = LT1.rearrange("p a b -> p (a b)")[:, 1024:2048].rearrange("p (a c) -> p a c", a=2)
        BON = SM[:, 16:32].rearrange("p (a b) -> p a b", a=2)
        LNG = XI1.rearrange("p a b -> p (a b)")[:, 0:512]
        LNB = XI1.rearrange("p a b -> p (a b)")[:, 512:1024]

        def slot8(t, hd):
            return t * 8 + (hd % 2) * 4 + hd // 2

        def pe_rwkv():
            for i, n in enumerate("rkv"):
                pe_feature_block(f"rkv{i}", f"raw {n}")
            w = weight("lora_in")[:, 0:2048].rearrange("p (k c) -> p k c", k=KT)
            for i, (a, b) in enumerate(((0, 64), (64, 128), (128, 256))):
                pe.wait_ge(vector_done, at(f"xw{i}"))
                ps = open_bank(f"lora{i}")
                for k in range(KT):
                    last = mm(ps[0:b - a, 0:SEQ], w[:, k, a:b], XW[i][:, k, :], k == 0, k == KT - 1)
                last.then_inc(tensor_done, pe.one())
                pe.mark(f"lora{i}")
            pe.mark("slot of lora_in")
            w = weight("lora_out")[:, 0:1536].rearrange("p (k c) -> p k c", k=3)
            for i in range(2):
                pe.wait_ge(scalar_done, at(f"lora out{i}"))
                for h in range(2):
                    ps = open_bank(f"lora up{i}.{h}")
                    for j in range(2):
                        m = 2 * h + j
                        last = mm(ps[:, j * SEQ:(j + 1) * SEQ], w[0:64, i, m * P:(m + 1) * P], LO[i][0:64, :], True, True)
                    last.then_inc(tensor_done, pe.one())
                    pe.mark(f"lora up{i}.{h}")
            pe.wait_ge(scalar_done, at("lora out2"))
            for t in range(2):
                ps = open_bank(f"gate a{t}")
                mm(ps[:, :], LO[2][:, t * P:(t + 1) * P], w[:, 2, :], True, True).then_inc(tensor_done, pe.one())
                pe.mark(f"gate a{t}")
            pe.mark("slot of lora_out")
            pe.wait_ge(vector_done, at("kk sq"))
            for h in range(2):
                ps = open_bank(f"kk ss{h}")
                mm(ps[:, :], K("head_ones"), flat(TMP)[:, h * 512:(h + 1) * 512], True, True).then_inc(tensor_done, pe.one())
                pe.mark(f"kk ss{h}")
            pe.wait_ge(vector_done, at("rkr"))
            ps = open_bank("bonus")
            for t in range(2):
                for g in range(4):
                    last = mm(ps[:, t * 8 + 2 * g:t * 8 + 2 * g + 2], TMP[:, g, t * P:(t + 1) * P], K("head_pick"), True, True)
            last.then_inc(tensor_done, pe.one())
            pe.mark("bonus")
            pe.wait_ge(vector_done, at("tilde"))
            for n, src in (("vt", VF), ("at", KK), ("bt", AV), ("kt", KF)):
                for t in range(2):
                    pe_turn(f"{n}{t}", [src[:, g, t * P:(t + 1) * P] for g in range(4)])
            for n, a, b in (("lt", AV, KK), ("lak", KF, KK), ("mrb", AV, R), ("mrk", KF, R)):
                for q in range(4):
                    ps = open_bank(f"{n}{q}")
                    for i in range(4):
                        t, g, r = q // 2, i, 64 * (q % 2)
                        last = mm(ps[:, i * P:(i + 1) * P], a[r:r + 64, g, t * P:(t + 1) * P],
                                  b[r:r + 64, g, t * P:(t + 1) * P], True, True)
                    last.then_inc(tensor_done, pe.one())
                    pe.mark(f"{n}{q}")
            pe.wait_ge(vector_done, at("lak ready"))
            pe.wait_ge(scalar_done, at("token-major"))
            for t in range(2):
                ps = open_bank(f"lv{t}")
                for hd in range(8):
                    last = mm(ps[:, hd * 64:hd * 64 + 64], LAK[:, slot8(t, hd), :], VT[:, t, hd * 64:hd * 64 + 64], True, True)
                last.then_inc(tensor_done, pe.one())
                pe.mark(f"lv{t}")
            pe_solve("rwkv", 4, XI1, XT1, T1v)
            pe.wait_ge(vector_done, at("rwkv solved"))
            for t in range(2):
                ps = open_bank(f"u{t}")
                for hd in range(8):
                    last = mm(ps[:, hd * 64:hd * 64 + 64], XT1[:, slot8(t, hd), :], SQ1b[:, t, hd * 64:hd * 64 + 64], True, True)
                last.then_inc(tensor_done, pe.one())
                pe.mark(f"u{t}")
                ps = open_bank(f"apt{t}")
                for hd in range(8):
                    g, r = hd // 2, 64 * (hd % 2)
                    last = mm(ps[r:r + 64, g * P:(g + 1) * P], AT_[:, t, hd * 64:hd * 64 + 64], XT1[:, slot8(t, hd), :], True, True)
                last.then_inc(tensor_done, pe.one())
                pe.mark(f"apt{t}")
            for c in range(4):
                t, rb = c // 2, 64 * (c % 2)
                cols = slice(c * 64, c * 64 + 64)
                if c > 0:
                    pe.wait_ge(vector_done, at(f"state{c - 1}"))
                    pe.wait_ge(vector_done, at("apt ready"))
                    for half in range(2):
                        r = slice(64 * half, 64 * half + 64)
                        ps = open_bank(f"sa{c}.{half}")
                        for g in range(4):
                            for j, Q in enumerate((APT, R)):
                                last = mm(ps[rb:rb + 64, j * 256 + g * 64:j * 256 + g * 64 + 64], Q[r, g, cols],
                                          ST[r, g * 64:g * 64 + 64], True, True)
                        last.then_inc(tensor_done, pe.one())
                        pe.mark(f"sa{c}.{half}")
                pe.wait_ge(vector_done, at(f"sa out{c}"))
                ps = open_bank(f"y{c}")
                for hd in range(8):
                    o = ps[rb:rb + 64, hd * 64:hd * 64 + 64]
                    n = slot8(t, hd)
                    mm(o, MRB[rb:rb + 64, n, rb:rb + 64], SAs[rb:rb + 64, hd * 64:hd * 64 + 64], True, False)
                    last = mm(o, MRK[rb:rb + 64, n, rb:rb + 64], VT[rb:rb + 64, t, hd * 64:hd * 64 + 64], False, True)
                last.then_inc(tensor_done, pe.one())
                pe.mark(f"y{c}")
                if c < 3:
                    ps = open_bank(f"ds{c}")
                    for hd in range(8):
                        g, r = hd // 2, 64 * (hd % 2)
                        o = ps[r:r + 64, g * 64:g * 64 + 64]
                        mm(o, BT[rb:rb + 64, t, hd * 64:hd * 64 + 64], SAs[rb:rb + 64, hd * 64:hd * 64 + 64], True, False)
                        last = mm(o, KTM[rb:rb + 64, t, hd * 64:hd * 64 + 64], VT[rb:rb + 64, t, hd * 64:hd * 64 + 64], False, True)
                    last.then_inc(tensor_done, pe.one())
                    pe.mark(f"ds{c}")

        def act_rwkv():
            for n, dst in (("r", R), ("k", KF), ("v", VF)):
                for h in range(2):
                    copy_out(act, f"raw {n}.{h}", dst[:, 2 * h:2 * h + 2, :], lambda ps: ps[:, :].rearrange("p (a c) -> p a c", a=2))
                act.wait_ge(scalar_done, act.n)
                act.mark(f"raw {n} out")
            for i, f, m in ((0, ACT.Tanh, 64), (1, ACT.Copy, 64), (2, ACT.Sigmoid, P)):
                ps = full(act, f"lora{i}")
                activation(LO[i][0:m, :], ps[0:m, 0:SEQ], f).then_inc(scalar_done, act.one())
                act.wait_ge(scalar_done, act.n)
                act.mark(f"read lora{i}", f"lora out{i}")
            for i, dst, bias in ((0, TMP, "w0"), (1, AV, "a0")):
                for h in range(2):
                    ps = full(act, f"lora up{i}.{h}")
                    for j in range(2):
                        m = 2 * h + j
                        activation(dst[:, m, :], ps[:, j * SEQ:(j + 1) * SEQ], ACT.Sigmoid, bias=C(bias, m)).then_inc(scalar_done, act.one())
                    act.mark(f"read lora up{i}.{h}")
                act.wait_ge(scalar_done, act.n)
                act.mark(f"lora sig{i}")
            for t in range(2):
                copy_out(act, f"gate a{t}", GA[:, t, :])
            act.wait_ge(vector_done, at("cw"))
            activation(WI, WI, ACT.Exp).then_inc(scalar_done, act.one())
            activation(KK, KK, ACT.Exp).then_inc(scalar_done, act.one())
            activation(WN, WN, ACT.Exp).then_inc(scalar_done, act.one())
            act.wait_ge(scalar_done, act.n)
            act.mark("decays")
            act.wait_ge(vector_done, at("kk sq"))
            for h in range(2):
                ps = full(act, f"kk ss{h}")
                activation(flat(TMP)[:, h * 512:(h + 1) * 512], ps[:, :], ACT.Sqrt, bias=K("eps")).then_inc(scalar_done, act.one())
                act.wait_ge(scalar_done, act.n)
                act.mark(f"read kk ss{h}")
            act.mark("kk root")
            ps = full(act, "bonus")
            activation(SM[:, 16:32], ps[:, 0:16], ACT.Copy).then_inc(scalar_done, act.one())
            act.wait_ge(scalar_done, act.n)
            act.mark("read bonus")
            for n, dst in (("vt", VT), ("at", AT_), ("bt", BT), ("kt", KTM)):
                for t in range(2):
                    copy_out(act, f"{n}{t}", dst[:, t, :])
            act.wait_ge(scalar_done, act.n)
            act.mark("token-major")
            for t in range(2):
                copy_out(act, f"lv{t}", SQ1b[:, t, :])
            act.wait_ge(scalar_done, act.n)
            act.mark("lv out")
            act.wait_ge(vector_done, at("y var"))
            activation(SM[:, 48:64], SM[:, 32:48], ACT.Sqrt, bias=K("gn_eps"), scale=1.0 / 64).then_inc(scalar_done, act.one())
            act.wait_ge(scalar_done, act.n)
            act.mark("y root")

        def shift_mix(src, diff, n):
            tt(diff[:, :, 1:SEQ], src[:, :, 0:SEQ - 1], src[:, :, 1:SEQ], ALU.subtract).then_inc(vector_done, dve.one())
            ts(diff[:, :, 0:1], src[:, :, 0:1], -1.0, None, ALU.mult).then_inc(vector_done, dve.one())
            dve.wait_ge(vector_done, dve.n)

        def heads_of(ap, half):
            return ap.rearrange("p (g h c) -> p h g c", h=2, c=64)[:, half]

        def dve_rwkv():
            for i, (n, X_) in enumerate((("r", R), ("k", KF), ("v", VF))):
                dve.wait_ge(scalar_done, at(f"raw {n} out"))
                shift_mix(X_, TMP, 4)
                for g in range(4):
                    stt(X_[:, g, :], TMP[:, g, :], C("mu_proj", 4 * i + g), X_[:, g, :], ALU.mult, ALU.add).then_inc(vector_done, dve.one())
                dve.wait_ge(vector_done, dve.n)
            H2 = HT[:, :, 0:SEQ]
            shift_mix(H2, DH, 8)
            for i in range(3):
                for k in range(8):
                    stt(XW[i][:, k, :], DH[:, k, :], C("mu_lora", 8 * i + k), H2[:, k, :], ALU.mult, ALU.add).then_inc(vector_done, dve.one())
                dve.wait_ge(vector_done, dve.n)
                dve.mark(f"xw{i}")
            dve.wait_ge(scalar_done, at("lora sig0"))
            ts(TMP, TMP, -math.exp(-0.5), None, ALU.mult).then_inc(vector_done, dve.one())
            dve.wait_ge(vector_done, dve.n)
            for g in range(4):
                nc.vector.tensor_tensor_scan(WI[:, g, :], K("carry"), TMP[:, g, :], 0.0, ALU.mult, ALU.add).then_inc(vector_done, dve.one())
            dve.wait_ge(vector_done, dve.n)
            ts(WN, WI, -1.0, None, ALU.mult).then_inc(vector_done, dve.one())
            tt(KK, WI, TMP, ALU.subtract).then_inc(vector_done, dve.one())
            dve.wait_ge(vector_done, dve.n)
            dve.mark("cw")
            dve.wait_ge(scalar_done, at("decays"))
            for g in range(4):
                ts(VN1[:, g, :], KF[:, g, :], C("k_k", g), None, ALU.mult).then_inc(vector_done, dve.one())
            dve.wait_ge(vector_done, dve.n)
            tt(TMP, VN1, VN1, ALU.mult).then_inc(vector_done, dve.one())
            dve.wait_ge(vector_done, dve.n)
            dve.mark("kk sq")
            dve.wait_ge(scalar_done, at("kk root"))
            nc.vector.reciprocal(TMP, TMP).then_inc(vector_done, dve.one())
            dve.wait_ge(vector_done, dve.n)
            tt(VN1, VN1, TMP, ALU.mult).then_inc(vector_done, dve.one())
            dve.wait_ge(vector_done, dve.n)
            stt(KK, KK, -1.0, VN1, ALU.mult, ALU.mult).then_inc(vector_done, dve.one())
            dve.wait_ge(vector_done, dve.n)
            dve.wait_ge(scalar_done, at("lora sig1"))
            for g in range(4):
                ts(TMP[:, g, :], AV[:, g, :], 1.0, C("k_a", g), ALU.subtract, ALU.mult).then_inc(vector_done, dve.one())
            dve.wait_ge(vector_done, dve.n)
            stt(KF, TMP, 1.0, KF, ALU.add, ALU.mult).then_inc(vector_done, dve.one())
            dve.wait_ge(vector_done, dve.n)
            for g in range(4):
                stt(TMP[:, g, :], R[:, g, :], C("r_k", g), KF[:, g, :], ALU.mult, ALU.mult).then_inc(vector_done, dve.one())
            dve.wait_ge(vector_done, dve.n)
            dve.mark("rkr")
            tt(R, R, WI, ALU.mult).then_inc(vector_done, dve.one())
            tt(AV, AV, VN1, ALU.mult).then_inc(vector_done, dve.one())
            dve.wait_ge(vector_done, dve.n)
            tt(AV, AV, WN, ALU.mult).then_inc(vector_done, dve.one())
            tt(KF, KF, WN, ALU.mult).then_inc(vector_done, dve.one())
            dve.wait_ge(vector_done, dve.n)
            dve.mark("tilde")
            for n, dst, mask in (("lt", LT1, "before"), ("lak", LAK, "before"), ("mrb", MRB, "upto"), ("mrk", MRK, "upto")):
                for q in range(4):
                    ps = full(dve, f"{n}{q}")
                    tt(dst[:, 4 * q:4 * q + 4, :], ps[:, :].rearrange("p (k c) -> p k c", k=4), rows(K(mask), 4), ALU.mult).then_inc(vector_done, dve.one())
                    dve.mark(f"read {n}{q}")
                dve.wait_ge(vector_done, dve.n)
                dve.mark(f"{n} ready")
            dve.wait_ge(tensor_done, at("lv1"))
            dve_solve("rwkv", 4, LT1, XI1, XT1, T1v)
            dve.wait_ge(scalar_done, at("lv out"))
            dve.mark("rwkv solved")
            for t in range(2):
                copy_out(dve, f"u{t}", PU[:, t, :])
                copy_out(dve, f"apt{t}", APT[:, :, t * P:(t + 1) * P], lambda ps: ps[:, :].rearrange("p (k c) -> p k c", k=4))
            dve.wait_ge(vector_done, dve.n)
            dve.mark("apt ready")
            for c in range(4):
                t, rb = c // 2, 64 * (c % 2)
                r = slice(rb, rb + 64)
                if c == 0:
                    nc.vector.tensor_copy(SAs[r, :], PU[r, t, :]).then_inc(vector_done, dve.one())
                    dve.wait_ge(vector_done, dve.n)
                else:
                    for half in range(2):
                        ps = full(dve, f"sa{c}.{half}")
                        tt(heads_of(SAs[r, :], half), ps[r, 0:256].rearrange("p (g c) -> p g c", g=4),
                              heads_of(PU[r, t, :], half), ALU.add).then_inc(vector_done, dve.one())
                    dve.wait_ge(vector_done, dve.n)
                dve.mark(f"sa out{c}")
                if c < 3:
                    ps = full(dve, f"ds{c}")
                    wl = bc(WI[:, :, c * 64 + 63], [P, 4, 64])
                    S3 = ST.rearrange("p (g c) -> p g c", g=4)
                    p3 = ps[:, 0:256].rearrange("p (g c) -> p g c", g=4)
                    if c == 0:
                        tt(S3, p3, wl, ALU.mult).then_inc(vector_done, dve.one())
                        dve.wait_ge(vector_done, dve.n)
                    else:
                        tt(S3, S3, p3, ALU.add).then_inc(vector_done, dve.one())
                        dve.wait_ge(vector_done, dve.n)
                        tt(S3, S3, wl, ALU.mult).then_inc(vector_done, dve.one())
                        dve.wait_ge(vector_done, dve.n)
                    dve.mark(f"read ds{c}", f"state{c}")
                copy_out(dve, f"y{c}", YA[r, t, :], lambda ps: ps[r, :])
                dve.wait_ge(vector_done, dve.n)
                if c > 0:
                    for half in range(2):
                        ps = full(dve, f"sa{c}.{half}")
                        y_ = heads_of(YA[r, t, :], half)
                        tt(y_, y_, ps[r, 256:512].rearrange("p (g c) -> p g c", g=4), ALU.add).then_inc(vector_done, dve.one())
                        dve.mark(f"read sa{c}.{half}")
            dve.wait_ge(vector_done, dve.n)
            y = YA.rearrange("p t (h c) -> p (t h) c", h=8)
            sq = SQ1.rearrange("p t (h c) -> p (t h) c", h=8)
            nc.vector.tensor_reduce(SM[:, 32:48], y, AX.X, ALU.add).then_inc(vector_done, dve.one())
            dve.wait_ge(vector_done, dve.n)
            ts(SM[:, 32:48], SM[:, 32:48], 1.0 / 64, None, ALU.mult).then_inc(vector_done, dve.one())
            dve.wait_ge(vector_done, dve.n)
            tt(y, y, bc(SM[:, 32:48], [P, 16, 64]), ALU.subtract).then_inc(vector_done, dve.one())
            dve.wait_ge(vector_done, dve.n)
            tt(sq, y, y, ALU.mult).then_inc(vector_done, dve.one())
            dve.wait_ge(vector_done, dve.n)
            nc.vector.tensor_reduce(SM[:, 32:48], sq, AX.X, ALU.add).then_inc(vector_done, dve.one())
            dve.wait_ge(vector_done, dve.n)
            dve.mark("y var")
            dve.wait_ge(scalar_done, at("y root"))
            nc.vector.reciprocal(SM[:, 48:64], SM[:, 48:64]).then_inc(vector_done, dve.one())
            dve.wait_ge(vector_done, dve.n)
            tt(y, y, bc(SM[:, 48:64], [P, 16, 64]), ALU.mult).then_inc(vector_done, dve.one())
            dve.wait_ge(vector_done, dve.n)
            tt(sq, VT.rearrange("p t (h c) -> p (t h) c", h=8), bc(SM[:, 16:32], [P, 16, 64]), ALU.mult).then_inc(vector_done, dve.one())
            dve.wait_ge(vector_done, dve.n)
            dve.wait_ge(loaded["rwkv_rows"], at("rows 1b"))
            tt(YA, YA, rows(LNG, 2), ALU.mult).then_inc(vector_done, dve.one())
            dve.wait_ge(vector_done, dve.n)
            tt(YA, YA, rows(LNB, 2), ALU.add).then_inc(vector_done, dve.one())
            dve.wait_ge(vector_done, dve.n)
            tt(YA, YA, SQ1, ALU.add).then_inc(vector_done, dve.one())
            dve.wait_ge(vector_done, dve.n)
            tt(YA, YA, GA, ALU.mult).then_inc(vector_done, dve.one())
            dve.wait_ge(vector_done, dve.n)

        VN1 = YA.rearrange("p t c -> p (t c)").rearrange("p (g c) -> p g c", g=4)
        SQ1b = WN.rearrange("p g c -> p (g c)").rearrange("p (t c) -> p t c", t=2)

        ar = Arena()
        ar.at = 11 * 1024
        QR = ar.take(12, SEQ + 4)
        CV = ar.take(12, SEQ)
        YB_ = YB
        ar = Arena(0)
        GB = ar.take(2, 512)
        DT = ar.take(8, P)
        EG = ar.take(8, P)
        BB = ar.take(8, P)
        QK = ar.take(8, P)
        KTb, VTb, UB = ar.take(2, 512), ar.take(2, 512), ar.take(2, 512)
        assert ar.at <= 8 * 1024
        ar = Arena(11 * 1024 + 12 * (SEQ + 4) + 12 * SEQ)
        SQ2 = ar.take(8, SEQ)
        LT2, XI2, XT2 = ar.take(8, P), ar.take(8, P), ar.take(8, P)
        T2 = ar.take(4, 4 * P).rearrange("p a (c d) -> p a c d", c=4)
        QD, WT, KD, KBP = (ar.take(8, P) for _ in range(4))
        NG = ar.take(P)
        ar = Arena(11 * 1024)
        SB_, VNb = ar.take(4, P), ar.take(512)
        ALr, DTr = SM[:, 64:68], SM[:, 68:72]
        BETA, GTt, GC = SM[:, 72:80], SM[:, 80:88], SM[:, 88:96]
        BEG, KDS, ZZ, ZN = SM[:, 96:104], SM[:, 104:112], SM[:, 112:120], SM[:, 120:128]
        INV2 = SM[:, 128:136]

        def b3(ap):
            return ap.rearrange("p (t h) -> p t h", t=2)

        def pe_gdn():
            for i in range(3):
                pe_feature_block(f"bqkv{i}", "bq", m0=4 * i)
            pe_token_blocks(["bgate"], [KT], "gate b", ht)
            w = weight("bab")[:, 0:64].rearrange("p (k c) -> p k c", k=KT)
            ps = open_bank("ab")
            for t in range(2):
                for k in range(KT):
                    last = mm(ps[:, t * 8:t * 8 + 8], ht(k, t), w[:, k, :], k == 0, k == KT - 1)
            weight_used(last, "bab")
            pe.mark("ab")
            pe_head_norm("bqk", SQ2f, 4, "ones")
            pe.wait_ge(vector_done, at("g"))
            ps = open_bank("gc")
            mm(ps[:, 0:8], K("upto"), GTt, True, True).then_inc(tensor_done, pe.one())
            pe.mark("gc")
            pe.wait_ge(vector_done, at("g wide"))
            for t in range(2):
                ps = open_bank(f"gcb{t}")
                for h in range(4):
                    last = mm(ps[:, h * P:(h + 1) * P], GW[:, t * 4 + h, :], K("upto"), True, True)
                last.then_inc(tensor_done, pe.one())
                pe.mark(f"gcb{t}")
                ps = open_bank(f"betab{t}")
                for h in range(4):
                    last = mm(ps[:, h * P:(h + 1) * P], BW[:, t * 4 + h, :], K("ident"), True, True)
                last.then_inc(tensor_done, pe.one())
                pe.mark(f"betab{t}")
            pe.wait_ge(vector_done, at("bqk normed"))
            for n, o in (("kb", 4), ("vb", 8)):
                for t in range(2):
                    pe_turn(f"{n}{t}", [CV[:, o + h, t * P:(t + 1) * P] for h in range(4)])
            for t in range(2):
                tk = slice(t * P, (t + 1) * P)
                for n, o in (("kkb", 4), ("qkb", 0)):
                    ps = open_bank(f"{n}{t}")
                    for h in range(4):
                        last = mm(ps[:, h * P:(h + 1) * P], CV[:, 4 + h, tk], CV[:, o + h, tk], True, True)
                    last.then_inc(tensor_done, pe.one())
                    pe.mark(f"{n}{t}")
            pe_solve("gdn", 2, XI2, XT2, T2)
            pe.wait_ge(vector_done, at("gdn solved"))
            for t in range(2):
                ps = open_bank(f"ub{t}")
                for h in range(4):
                    last = mm(ps[:, h * P:(h + 1) * P], XT2[:, t * 4 + h, :], VTb[:, t, h * P:(h + 1) * P], True, True)
                last.then_inc(tensor_done, pe.one())
                pe.mark(f"ub{t}")
                ps = open_bank(f"wb{t}")
                for h in range(4):
                    last = mm(ps[:, h * P:(h + 1) * P], KBP[:, t * 4 + h, :], XT2[:, t * 4 + h, :], True, True)
                last.then_inc(tensor_done, pe.one())
                pe.mark(f"wb{t}")
            for c in range(4):
                t, rb = c // 2, 64 * (c % 2)
                r = slice(rb, rb + 64)
                if c > 0:
                    pe.wait_ge(vector_done, at(f"bstate{c - 1}"))
                    pe.wait_ge(vector_done, at("u ready"))
                    ps = open_bank(f"vn{c}")
                    for h in range(4):
                        last = mm(ps[r, h * P:(h + 1) * P], WT[:, t * 4 + h, r], SB_[:, h, :], True, True)
                    last.then_inc(tensor_done, pe.one())
                    pe.mark(f"vn{c}")
                pe.wait_ge(vector_done, at(f"vn out{c}"))
                ps = open_bank(f"ob{c}")
                for h in range(4):
                    o = ps[r, h * P:(h + 1) * P]
                    if c > 0:
                        mm(o, QD[:, t * 4 + h, r], SB_[:, h, :], True, False)
                    last = mm(o, QK[r, t * 4 + h, r], VNb[r, h * P:(h + 1) * P], c == 0, True)
                last.then_inc(tensor_done, pe.one())
                pe.mark(f"ob{c}")
                if c < 3:
                    ps = open_bank(f"dsb{c}")
                    for h in range(4):
                        last = mm(ps[:, h * P:(h + 1) * P], KD[r, t * 4 + h, :], VNb[r, h * P:(h + 1) * P], True, True)
                    last.then_inc(tensor_done, pe.one())
                    pe.mark(f"dsb{c}")

        def act_gdn():
            for j in range(6):
                copy_out(act, f"bq.{j}", QR[:, 2 * j:2 * j + 2, 3:3 + SEQ], lambda ps: ps[:, :].rearrange("p (a c) -> p a c", a=2))
            act.wait_ge(scalar_done, act.n)
            act.mark("bq out")
            for t in range(2):
                ps = full(act, f"gate b.{t}")
                activation(GB[:, t, :], ps[:, :], ACT.Silu).then_inc(scalar_done, act.one())
                act.mark(f"read gate b.{t}")
            ps = full(act, "ab")
            p3 = ps[:, 0:16].rearrange("p (t c) -> p t c", t=2)
            activation(b3(BETA), p3[:, :, 0:4], ACT.Sigmoid).then_inc(scalar_done, act.one())
            activation(b3(ZZ), p3[:, :, 4:8], ACT.Copy).then_inc(scalar_done, act.one())
            act.wait_ge(scalar_done, act.n)
            act.mark("read ab", "ab out")
            act.wait_ge(vector_done, at("conv"))
            activation(CV, CV, ACT.Silu).then_inc(scalar_done, act.one())
            act.wait_ge(scalar_done, act.n)
            act.mark("conv silu")
            act_head_norm("bqk", SQ2f, 4, 1.0)
            act.wait_ge(vector_done, at("z"))
            activation(ALr, ALr, ACT.Exp).then_inc(scalar_done, act.one())
            activation(ZN, ZN, ACT.Exp).then_inc(scalar_done, act.one())
            act.wait_ge(scalar_done, act.n)
            activation(ZN, ZN, ACT.Ln, bias=K("one")).then_inc(scalar_done, act.one())
            act.wait_ge(scalar_done, act.n)
            act.mark("softplus")
            act.wait_ge(vector_done, at("gcb in"))
            activation(DT, DT, ACT.Exp).then_inc(scalar_done, act.one())
            activation(EG, EG, ACT.Exp).then_inc(scalar_done, act.one())
            act.wait_ge(scalar_done, act.n)
            activation(BEG, GC, ACT.Exp).then_inc(scalar_done, act.one())
            act.wait_ge(scalar_done, act.n)
            act.mark("gcb exp")
            act.wait_ge(vector_done, at("ob sq"))
            activation(INV2, INV2, ACT.Sqrt, bias=K("eps"), scale=1.0 / P).then_inc(scalar_done, act.one())
            act.wait_ge(scalar_done, act.n)
            act.mark("ob root")

        def dve_gdn():
            nc.vector.memset(QR[:, :, 0:3], 0.0).then_inc(vector_done, dve.one())
            dve.wait_ge(vector_done, dve.n)
            dve.wait_ge(scalar_done, at("bq out"))
            for m in range(12):
                ts(CV[:, m, :], QR[:, m, 3:3 + SEQ], C("conv", 36 + m), None, ALU.mult).then_inc(vector_done, dve.one())
            dve.wait_ge(vector_done, dve.n)
            for i in (2, 1, 0):
                for m in range(12):
                    stt(CV[:, m, :], QR[:, m, i:i + SEQ], C("conv", 12 * i + m), CV[:, m, :], ALU.mult, ALU.add).then_inc(vector_done, dve.one())
                dve.wait_ge(vector_done, dve.n)
            dve.mark("conv")
            dve.wait_ge(scalar_done, at("ab out"))
            dve.wait_ge(loaded["start"], at("rows 1c"))
            tt(b3(ZZ), b3(ZZ), rows(DTr, 2), ALU.add).then_inc(vector_done, dve.one())
            dve.wait_ge(vector_done, dve.n)
            stt(ZN, ZZ, -1.0, ZZ, ALU.mult, ALU.min).then_inc(vector_done, dve.one())
            dve.wait_ge(vector_done, dve.n)
            dve.mark("z")
            dve.wait_ge(scalar_done, at("conv silu"))
            dve_head_norm("bqk", CV[:, 0:8, :].rearrange("p a b -> p (a b)"), SQ2f, 4,
                          lambda i: K("one") if i < 2 else None, P ** -0.5)
            dve.wait_ge(scalar_done, at("softplus"))
            stt(ZZ, ZZ, 0.0, ZN, ALU.max, ALU.add).then_inc(vector_done, dve.one())
            dve.wait_ge(vector_done, dve.n)
            stt(b3(GTt), b3(ZZ), -1.0, rows(ALr, 2), ALU.mult, ALU.mult).then_inc(vector_done, dve.one())
            dve.wait_ge(vector_done, dve.n)
            dve.mark("g")
            nc.vector.tensor_copy(GW, bc(GTt, [P, 8, P])).then_inc(vector_done, dve.one())
            dve.wait_ge(vector_done, dve.n)
            nc.vector.tensor_copy(BW, bc(BETA, [P, 8, P])).then_inc(vector_done, dve.one())
            dve.wait_ge(vector_done, dve.n)
            dve.mark("g wide")
            copy_out(dve, "gc", GC, lambda ps: ps[:, 0:8])
            dve.wait_ge(vector_done, dve.n)
            for t in range(2):
                ps = full(dve, f"gcb{t}")
                nc.vector.tensor_copy(EG[:, 4 * t:4 * t + 4, :], k4(ps[:, :])).then_inc(vector_done, dve.one())
                for h in range(4):
                    ts(DT[:, 4 * t + h, :], ps[:, h * P:(h + 1) * P], GC[:, 4 * t + h:4 * t + h + 1], 0.0,
                          ALU.subtract, ALU.min).then_inc(vector_done, dve.one())
                dve.mark(f"read gcb{t}")
                copy_out(dve, f"betab{t}", BB[:, 4 * t:4 * t + 4, :], lambda ps: k4(ps[:, :]))
            dve.wait_ge(vector_done, dve.n)
            dve.mark("gcb in")
            for t in range(2):
                copy_out(dve, f"kb{t}", KTb[:, t, :])
            for t in range(2):
                copy_out(dve, f"vb{t}", VTb[:, t, :])
            dve.wait_ge(vector_done, dve.n)
            dve.wait_ge(scalar_done, at("gcb exp"))
            tt(DT, DT, rows(K("upto"), 8), ALU.mult).then_inc(vector_done, dve.one())
            dve.wait_ge(vector_done, dve.n)
            for t in range(2):
                s4 = slice(4 * t, 4 * t + 4)
                ps = full(dve, f"kkb{t}")
                stt(LT2[:, s4, :].rearrange("p a b -> p (a b)"), ps[:, :], -1.0, DT[:, s4, :].rearrange("p a b -> p (a b)"), ALU.mult, ALU.mult).then_inc(vector_done, dve.one())
                dve.wait_ge(vector_done, dve.n)
                dve.mark(f"read kkb{t}")
                ps = full(dve, f"qkb{t}")
                tt(QK[:, s4, :], k4(ps[:, :]), DT[:, s4, :], ALU.mult).then_inc(vector_done, dve.one())
                dve.mark(f"read qkb{t}")
            tt(LT2, LT2, rows(K("before"), 8), ALU.mult).then_inc(vector_done, dve.one())
            dve.wait_ge(vector_done, dve.n)
            tt(LT2, LT2, BB, ALU.mult).then_inc(vector_done, dve.one())
            dve.wait_ge(vector_done, dve.n)
            dve_solve("gdn", 2, LT2, XI2, XT2, T2)
            tt(BEG, BEG, BETA, ALU.mult).then_inc(vector_done, dve.one())
            dve.wait_ge(vector_done, dve.n)
            nc.vector.tensor_copy(KDS[0:64, :], DT[0:64, :, 63]).then_inc(vector_done, dve.one())
            nc.vector.tensor_copy(KDS[64:P, :], DT[64:P, :, P - 1]).then_inc(vector_done, dve.one())
            dve.wait_ge(vector_done, dve.n)
            k8 = KTb.rearrange("p t (h c) -> p (t h) c", h=4)
            v8 = VTb.rearrange("p t (h c) -> p (t h) c", h=4)
            tt(v8, v8, bc(BETA, [P, 8, P]), ALU.mult).then_inc(vector_done, dve.one())
            tt(KBP, k8, bc(BEG, [P, 8, P]), ALU.mult).then_inc(vector_done, dve.one())
            tt(KD, k8, bc(KDS, [P, 8, P]), ALU.mult).then_inc(vector_done, dve.one())
            for t in range(2):
                tt(QD[:, 4 * t:4 * t + 4, :], CV[:, 0:4, t * P:(t + 1) * P], EG[:, 4 * t:4 * t + 4, :], ALU.mult).then_inc(vector_done, dve.one())
            dve.wait_ge(vector_done, dve.n)
            dve.mark("gdn solved")
            for t in range(2):
                copy_out(dve, f"ub{t}", UB[:, t, :])
                copy_out(dve, f"wb{t}", WT[:, 4 * t:4 * t + 4, :], lambda ps: k4(ps[:, :]))
            dve.wait_ge(vector_done, dve.n)
            dve.mark("u ready")
            for c in range(4):
                t, rb = c // 2, 64 * (c % 2)
                r = slice(rb, rb + 64)
                if c == 0:
                    nc.vector.tensor_copy(VNb[r, :], UB[r, t, :]).then_inc(vector_done, dve.one())
                    dve.wait_ge(vector_done, dve.n)
                else:
                    ps = full(dve, f"vn{c}")
                    tt(VNb[r, :], UB[r, t, :], ps[r, :], ALU.subtract).then_inc(vector_done, dve.one())
                    dve.wait_ge(vector_done, dve.n)
                    dve.mark(f"read vn{c}")
                dve.mark(f"vn out{c}")
                if c < 3:
                    ps = full(dve, f"dsb{c}")
                    if c == 0:
                        nc.vector.tensor_copy(SB_, k4(ps[:, :])).then_inc(vector_done, dve.one())
                        dve.wait_ge(vector_done, dve.n)
                    else:
                        for h in range(4):
                            stt(SB_[:, h, :], SB_[:, h, :], EG[:, 4 * t + h, rb + 63:rb + 64], ps[:, h * P:(h + 1) * P],
                                   ALU.mult, ALU.add).then_inc(vector_done, dve.one())
                        dve.wait_ge(vector_done, dve.n)
                    dve.mark(f"read dsb{c}", f"bstate{c}")
                copy_out(dve, f"ob{c}", YB[r, t, :], lambda ps: ps[r, :])
            dve.wait_ge(vector_done, dve.n)
            y = YB.rearrange("p t (h c) -> p (t h) c", h=4)
            tt(QK, y, y, ALU.mult).then_inc(vector_done, dve.one())
            dve.wait_ge(vector_done, dve.n)
            nc.vector.tensor_reduce(INV2, QK, AX.X, ALU.add).then_inc(vector_done, dve.one())
            dve.wait_ge(vector_done, dve.n)
            dve.mark("ob sq")
            dve.wait_ge(scalar_done, at("ob root"))
            nc.vector.reciprocal(INV2, INV2).then_inc(vector_done, dve.one())
            dve.wait_ge(vector_done, dve.n)
            tt(y, y, bc(INV2, [P, 8, P]), ALU.mult).then_inc(vector_done, dve.one())
            dve.wait_ge(vector_done, dve.n)
            dve.wait_ge(loaded["gdn_rows"], at("norm b"))
            tt(y, y, rows(NG, 8), ALU.mult).then_inc(vector_done, dve.one())
            dve.wait_ge(vector_done, dve.n)
            tt(YB, YB, GB, ALU.mult).then_inc(vector_done, dve.one())
            dve.wait_ge(vector_done, dve.n)

        SQ2f = SQ2.rearrange("p a b -> p (a b)")
        GW = QD
        BW = WT

        def dve_add(label, h, tiles, gate=None):
            for t in tiles:
                ps = full(dve, f"{label}{h}.{t}")
                dst = X[:, t, h * 512:(h + 1) * 512]
                if gate is None:
                    tt(dst, dst, ps[:, :], ALU.add).then_inc(vector_done, dve.one())
                else:
                    tt(junk512, ps[:, :], gate(t)[:, h * 512:(h + 1) * 512], ALU.mult).then_inc(vector_done, dve.one())
                    dve.wait_ge(vector_done, dve.n)
                    tt(dst, dst, junk512, ALU.add).then_inc(vector_done, dve.one())
                    dve.wait_ge(vector_done, dve.n)
                dve.mark(f"read {label}{h}.{t}")

        def pe_start():
            pe.wait_ge(loaded["start"], at("start in"))

        def act_start():
            act.wait_ge(loaded["start"], at("start in"))

        def dve_start():
            dve.wait_ge(loaded["start"], at("start in"))

        def act_eout():
            act.wait_ge(vector_done, at("ymix src"))
            act_turn_all("ymix", [0, 1])

        def dve_eout():
            dve.mark("ymix src")
            for h in range(2):
                dve_add("eout", h, [0, 1])

        def pe_eout():
            pe.wait_ge(vector_done, at("ymix src"))
            for t in range(2):
                for h, Y in enumerate((YA, YB)):
                    pe_turn(f"ymix turned {t}.{h}", [Y[:, t, i * P:(i + 1) * P] for i in range(4)])
            pe.wait_ge(scalar_done, at("ymix ready"))
            for h in range(2):
                pe_token_blocks([f"eout{h}"], [KT], f"eout{h}", ht)

        def mlp_places():
            ar = Arena()
            d = {"xn": ar.take(2, D), "H": ar.take(32, SEQ), "pT": ar.take(2, SEQ), "PP": ar.take(2, D),
                 "pg": ar.take(D), "sg": ar.take(2, 512), "junk": ar.take(2, D)}
            return d

        M = mlp_places()
        HH = M["H"]

        def pe_mlp(i):
            pe_norm(f"ffn{i}", [0, 1], M["xn"])
            for n in range(8):
                pe_feature_block(f"up{i}.{n}", f"up{i}", m0=4 * n)
            pe.wait_ge(vector_done, at(f"hidden{i}"))
            for h in range(2):
                pe_token_blocks([f"down{i}.{h}.{n}" for n in range(4)], [8] * 4, f"down{i}.{h}", lambda k, t: HH[:, k, t * P:(t + 1) * P])
            pe.wait_ge(loaded[f"ple{i}"], at(f"p{i}"))
            w = weight(f"pproj{i}")[:, 0:2048].rearrange("p (k c) -> p k c", k=2)
            for t in range(2):
                for h in range(2):
                    ps = open_bank(f"pproj{i}.{t}.{h}")
                    for k in range(2):
                        last = mm(ps[:, :], M["pT"][:, k, t * P:(t + 1) * P], w[:, k, h * 512:(h + 1) * 512], k == 0, k == 1)
                    last.then_inc(tensor_done, pe.one())
                    pe.mark(f"pproj{i}.{t}.{h}")
            pe.mark(f"slot of pproj{i}")
            pe_turn_all(f"xt{i}", X, [0, 1])
            for h in range(2):
                pe_token_blocks([f"pgate{i}.{h}"], [KT], f"pgate{i}.{h}", ht)

        def act_mlp(i):
            act_norm(f"ffn{i}", [0, 1], M["junk"])
            for j in range(16):
                copyf = f"up{i}.{j}"
                ps = full(act, copyf)
                activation(HH[:, 2 * j:2 * j + 2, :], ps[:, :].rearrange("p (a c) -> p a c", a=2), ACT.Relu).then_inc(scalar_done, act.one())
                act.wait_ge(scalar_done, act.n)
                act.mark("read " + copyf, f"relu{i}.{j}")
            act.wait_ge(vector_done, at(f"xt{i} src"))
            act_turn_all(f"xt{i}", [0, 1])
            for t in range(2):
                for h in range(2):
                    copy_out(act, f"pproj{i}.{t}.{h}", M["PP"][:, t, h * 512:(h + 1) * 512])
            act.wait_ge(scalar_done, act.n)
            for t in range(2):
                activation(M["junk"][:, t, :], M["PP"][:, t, :], ACT.Square, accum_out=SS[:, t:t + 1]).then_inc(scalar_done, act.one())
                act.wait_ge(scalar_done, act.n)
            activation(RS[:, 0:2], SS[:, 0:2], ACT.Sqrt, bias=K("eps"), scale=1.0 / D).then_inc(scalar_done, act.one())
            act.wait_ge(scalar_done, act.n)
            act.mark(f"pproj root{i}")
            for h in range(2):
                for t in range(2):
                    n = f"pgate{i}.{h}.{t}"
                    ps = full(act, n)
                    if h == 1:
                        act.wait_ge(vector_done, at(f"sg used{i}.{t}"))
                    activation(M["sg"][:, t, :], ps[:, :], ACT.Sigmoid).then_inc(scalar_done, act.one())
                    act.wait_ge(scalar_done, act.n)
                    act.mark("read " + n, f"sg{i}.{h}.{t}")

        def dve_mlp(i):
            dve_norm(f"ffn{i}", [0, 1], M["xn"], lambda t: C(f"ffn{i}", 0, 8))
            for j in range(16):
                dve.wait_ge(scalar_done, at(f"relu{i}.{j}"))
                c = HH[:, 2 * j:2 * j + 2, :]
                tt(c, c, c, ALU.mult).then_inc(vector_done, dve.one())
            dve.mark(f"hidden{i}")
            for h in range(2):
                dve_add(f"down{i}.", h, [0, 1])
            dve.wait_ge(vector_done, dve.n)
            dve.mark(f"xt{i} src")
            dve.wait_ge(scalar_done, at(f"pproj root{i}"))
            dve.wait_ge(loaded[f"ple{i}"], at(f"rows ple{i}"))
            nc.vector.reciprocal(RS[:, 0:2], RS[:, 0:2]).then_inc(vector_done, dve.one())
            dve.wait_ge(vector_done, dve.n)
            for t in range(2):
                stt(M["PP"][:, t, :], M["PP"][:, t, :], RS[:, t:t + 1], M["pg"], ALU.mult, ALU.mult).then_inc(vector_done, dve.one())
                dve.wait_ge(vector_done, dve.n)
            for h in range(2):
                for t in range(2):
                    dve.wait_ge(scalar_done, at(f"sg{i}.{h}.{t}"))
                    c = slice(h * 512, (h + 1) * 512)
                    tt(M["sg"][:, t, :], M["sg"][:, t, :], M["PP"][:, t, c], ALU.mult).then_inc(vector_done, dve.one())
                    dve.wait_ge(vector_done, dve.n)
                    tt(X[:, t, c], X[:, t, c], M["sg"][:, t, :], ALU.add).then_inc(vector_done, dve.one())
                    dve.wait_ge(vector_done, dve.n)
                    if h == 0:
                        dve.mark(f"sg used{i}.{t}")

        ar = Arena()
        QB, KB, VB = ar.take(8, SEQ), ar.take(8, SEQ), ar.take(2, D)
        XN3 = ar.take(2, D)
        SQ3 = XN3.rearrange("p a b -> p (a b)")
        JK3 = ar.take(2, D)
        REL = ar.take(16, SEQ)
        OB_ = ar.take(2, D)
        BUF3 = unit_buffers(ar)
        units_b = []
        for hd in range(16):
            g, r = hd // 2, 64 * (hd % 2)
            for t in range(2):
                nk = P * (t + 1)
                u = {"q": QB[r:r + 64, g, t * P:(t + 1) * P], "k": [(0, nk, KB[r:r + 64, g, 0:nk])], "nk": nk, "dv": 64,
                     "v": [VB[:, a, hd * 64:hd * 64 + 64] for a in range(t + 1)], "o": OB_[:, t, hd * 64:hd * 64 + 64]}
                u["bias"] = [(a * P, (a + 1) * P, REL[:, hd, (t - a) * P:(t - a + 1) * P], K("flip")) for a in range(t + 1)]
                u["bias"].append((t * P, (t + 1) * P, K("late_query")[0:1, :], K("late_key")[0:1, :]))
                units_b.append(u)

        def pe_attn():
            pe_norm("mix1", [0, 1], XN3)
            for i in range(4):
                pe_feature_block(f"qkv{i}", "qk", m0=4 * i)
            for i in range(2):
                pe_token_blocks([f"qkv{4 + i}"], [KT], f"v{i}", ht)
            pe_head_norm("q3", SQ3, 4)
            pe_head_norm("k3", SQ3, 4)
            pe.wait_ge(vector_done, at("k3 normed"))
            pe.wait_ge(scalar_done, at("v out"))
            pe.wait_ge(loaded["rel"], at("rel"))
            pe_attention("band", units_b, BUF3)
            pe_turn_all("ob", OB_, [0, 1])
            for h in range(2):
                pe_token_blocks([f"aout{h}"], [KT], f"aout{h}", ht)

        def act_attn():
            act_norm("mix1", [0, 1], JK3)
            for j in range(8):
                dst = (QB if j < 4 else KB)[:, 2 * (j % 4):2 * (j % 4) + 2, :]
                copy_out(act, f"qk.{j}", dst, lambda ps: ps[:, :].rearrange("p (a c) -> p a c", a=2))
            act.wait_ge(scalar_done, act.n)
            act.mark("qk out")
            for i in range(2):
                for t in range(2):
                    copy_out(act, f"v{i}.{t}", VB[:, t, i * 512:(i + 1) * 512])
            act.wait_ge(scalar_done, act.n)
            act.mark("v out")
            act_head_norm("q3", SQ3, 4, 1.0 / 64)
            act_head_norm("k3", SQ3, 4, 1.0 / 64)
            act_attention("band", units_b, BUF3)
            act_turn_all("ob", [0, 1])

        def dve_attn():
            dve_norm("mix1", [0, 1], XN3, lambda t: C("mix1", 0, 8))
            dve.wait_ge(scalar_done, at("qk out"))
            dve_head_norm("q3", QB.rearrange("p a b -> p (a b)"), SQ3, 4, lambda i: C("attn_q"), 0.125)
            dve_head_norm("k3", KB.rearrange("p a b -> p (a b)"), SQ3, 4, lambda i: C("attn_k"), 1.0)
            dve_attention("band", units_b, BUF3)
            dve.mark("ob src")
            for h in range(2):
                dve_add("aout", h, [0, 1])

        ar = Arena()
        GT_ = ar.take(2, 2, D)
        MC = ar.take(4, 8, 2)
        SC = ar.take(8, 2)
        junk512 = ar.take(512)
        base2 = ar.at
        MOD = ar.take(6 * D)
        MODS = (0, 1, 3, 4)

        def pe_ada(i):
            pe.wait_ge(scalar_done, at(f"silu c{i}"))
            for n in range(12):
                w = weight(f"ada{i}.{n}").rearrange("p (k c) -> p k c", k=KT)
                ps = open_bank(f"ada{i}.{n}")
                for k in range(KT):
                    last = mm(ps[0:2, :], SC[:, k, :], w[:, k, :], k == 0, k == KT - 1)
                weight_used(last, f"ada{i}.{n}")
                pe.mark(f"ada{i}.{n}")
            pe.wait_ge(vector_done, at(f"mod{i}"))
            ps = open_bank(f"mod cols{i}")
            for j, m in enumerate(MODS):
                for k in range(8):
                    c = (j * 8 + k) * 2
                    last = mm(ps[:, c:c + 2], MOD[0:2, m * D + k * P:m * D + (k + 1) * P], K("ident")[0:2, 0:2], True, True)
            last.then_inc(tensor_done, pe.one())
            pe.mark(f"mod cols{i}")
            for s in range(2 - i):
                for j, m in enumerate((2, 5)):
                    for h in range(2):
                        ps = open_bank(f"gate{i}.{s}.{j}.{h}")
                        mm(ps[:, :], K(f"stream{s}")[0:2, :], MOD[0:2, m * D + h * 512:m * D + (h + 1) * 512], True, True).then_inc(tensor_done, pe.one())
                        pe.mark(f"gate{i}.{s}.{j}.{h}")

        def act_ada(i):
            activation(SC, C("c", 0, 16).rearrange("p (k s) -> p k s", s=2), ACT.Silu).then_inc(scalar_done, act.one())
            act.wait_ge(scalar_done, act.n)
            act.mark(f"silu c{i}")
            for s in range(2 - i):
                for j in range(2):
                    for h in range(2):
                        copy_out(act, f"gate{i}.{s}.{j}.{h}", GT_[:, s, j, h * 512:(h + 1) * 512])

        def dve_ada(i):
            dve.wait_ge(loaded[f"ada{i}"], at(f"rows ada{i}"))
            for n in range(12):
                ps = full(dve, f"ada{i}.{n}")
                c = MOD[0:2, n * 512:(n + 1) * 512]
                tt(c, c, ps[0:2, :], ALU.add).then_inc(vector_done, dve.one())
                dve.mark(f"read ada{i}.{n}")
            dve.wait_ge(vector_done, dve.n)
            dve.mark(f"mod{i}")
            ps = full(dve, f"mod cols{i}")
            for j in range(4):
                ts(MC[:, j, :, :], ps[:, j * 16:(j + 1) * 16].rearrange("p (k s) -> p k s", s=2), 1.0 if j % 2 else 0.0, None, ALU.add).then_inc(vector_done, dve.one())
                dve.wait_ge(vector_done, dve.n)
            dve.mark(f"read mod cols{i}")

        def mod_scale(w):
            return lambda t: MC[:, 2 * w + 1, :, t // 2]

        def mod_shift(w):
            return lambda t: MC[:, 2 * w, :, t // 2]

        def gate_row(w):
            return lambda t: GT_[:, t // 2, w, :]

        def ffn_places():
            ar = Arena(base2)
            return {"H": ar.take(22, 512), "xn": ar.take(2, D), "junk": ar.take(2, D), "raw": ar.take(2, 2, 260), "cv": ar.take(2, 512),
                    "g": ar.take(2, 512)}

        F = ffn_places()
        FH = F["H"]

        def pe_ffn(i, S):
            tiles = list(range(2 * S))
            pe_norm(f"cffn{i}", tiles, F["xn"])
            for n in range(11):
                w = weight(f"cup{i}.{n}").rearrange("p (k c) -> p k c", k=KT)
                for j in range(2):
                    for gv in range(2):
                        lab = f"{'gv'[gv]}up{i}.{2 * n + j}"
                        ps = open_bank(lab)
                        m = 2 * j + gv
                        for k in range(KT):
                            last = mm(ps[:, 0:S * SEQ], w[:, k, m * P:(m + 1) * P], HT[:, k, 0:S * SEQ], k == 0, k == KT - 1)
                        last.then_inc(tensor_done, pe.one())
                        pe.mark(lab)
                pe.mark(f"slot of cup{i}.{n}")
            pe.wait_ge(vector_done, at(f"chidden{i}"))
            for h in range(2):
                pe_token_blocks([f"cdown{i}.{h}.{n}" for n in range(3)], [8, 8, 6], f"cdown{i}.{h}",
                                lambda k, t: FH[:, k, t * P:(t + 1) * P], tiles=2 * S)

        def act_ffn(i, S):
            act_norm(f"cffn{i}", list(range(2 * S)), F["junk"])
            for m in range(22):
                b = m % 2
                ps = full(act, f"gup{i}.{m}")
                act.wait_ge(vector_done, at(f"raw ready{i}.{m}"))
                for s in range(S):
                    activation(F["raw"][:, b, s, 1:1 + SEQ], ps[:, s * SEQ:(s + 1) * SEQ], ACT.Copy).then_inc(scalar_done, act.one())
                act.wait_ge(scalar_done, act.n)
                act.mark(f"read gup{i}.{m}", f"raw{i}.{m}")
                act.wait_ge(vector_done, at(f"cv{i}.{m}"))
                if m >= 2:
                    act.wait_ge(vector_done, at(f"h{i}.{m - 2}"))
                activation(F["g"][:, b, 0:S * SEQ], F["cv"][:, b, 0:S * SEQ], ACT.Silu, bias=C(f"fconv_b{i}", m)).then_inc(scalar_done, act.one())
                act.wait_ge(scalar_done, act.n)
                act.mark(f"sg{i}.{m}")

        def dve_ffn(i, S):
            tiles = list(range(2 * S))
            dve_norm(f"cffn{i}", tiles, F["xn"], mod_scale(1), mod_shift(1))
            nc.vector.memset(F["raw"], 0.0).then_inc(vector_done, dve.one())
            dve.wait_ge(vector_done, dve.n)
            dve.mark(f"raw ready{i}.0", f"raw ready{i}.1")

            def conv(m):
                b = m % 2
                dve.wait_ge(scalar_done, at(f"raw{i}.{m}"))
                if m >= 2:
                    dve.wait_ge(scalar_done, at(f"sg{i}.{m - 2}"))
                c = F["cv"][:, b, 0:S * SEQ].rearrange("p (s c) -> p s c", s=S)
                raw = F["raw"][:, b, 0:S, :]
                ts(c, raw[:, :, 0:SEQ], C(f"fconv_w{i}", m), None, ALU.mult).then_inc(vector_done, dve.one())
                dve.wait_ge(vector_done, dve.n)
                stt(c, raw[:, :, 1:1 + SEQ], C(f"fconv_w{i}", 22 + m), c, ALU.mult, ALU.add).then_inc(vector_done, dve.one())
                dve.wait_ge(vector_done, dve.n)
                stt(c, raw[:, :, 2:2 + SEQ], C(f"fconv_w{i}", 44 + m), c, ALU.mult, ALU.add).then_inc(vector_done, dve.one())
                dve.wait_ge(vector_done, dve.n)
                dve.mark(f"cv{i}.{m}", f"raw ready{i}.{m + 2}")

            def gate(m):
                b = m % 2
                dve.wait_ge(scalar_done, at(f"sg{i}.{m}"))
                ps = full(dve, f"vup{i}.{m}")
                tt(FH[:, m, 0:S * SEQ], F["g"][:, b, 0:S * SEQ], ps[:, 0:S * SEQ], ALU.mult).then_inc(vector_done, dve.one())
                dve.wait_ge(vector_done, dve.n)
                dve.mark(f"read vup{i}.{m}", f"h{i}.{m}")

            for m in range(22):
                conv(m)
                gate(m)
            dve.mark(f"chidden{i}")
            for h in range(2):
                dve_add(f"cdown{i}.", h, tiles, gate_row(1))

        ar = Arena(base2)
        RC = ar.take(2, SEQ)
        QN, KN, VN = ar.take(4, 512), ar.take(4, 512), ar.take(4, 512)
        QD5, KD5, VD5 = ar.take(4, 512), ar.take(4, 512), ar.take(4, 512)
        SQ5 = ar.take(4, 512)
        YN = ar.take(4, 512)
        BM = ar.take(2, 8, SEQ)
        NM = ar.take(SEQ)
        LAMR, SUBG = SM[:, 136:144], None
        ar = Arena(ar.at)
        SUBG = ar.take(P)
        XN5 = SQ5.rearrange("p a b -> p (a b)").rearrange("p (a b) -> p a b", a=2)
        JK5 = BM.rearrange("p a b c -> p (a b c)")[:, 0:2 * D].rearrange("p (a b) -> p a b", a=2)
        ar = Arena(0)
        BUF5 = {"P": SQ5[:, 0:2, :], "PT": SQ5[:, 2:4, :], "st": SM[:, 144:152].rearrange("p (a b) -> p a b", a=2)}
        OD = HT.rearrange("p k c -> p (k c)").rearrange("p (t c) -> p t c", t=4)
        YD = BM.rearrange("p a b c -> p (a b c)")[:, 0:2048].rearrange("p (t c) -> p t c", t=4)
        OT5 = QN.rearrange("p a b -> p (a b)"), KN.rearrange("p a b -> p (a b)")

        def heads64(Q, g, r, a, b):
            return Q[r:r + 64, g, a:b]

        na_units, na_ctx, da_units, da_ctx = [], [], [], []
        for hd in range(8):
            g, r = hd // 2, 64 * (hd % 2)
            for t in range(4):
                q = QN[r:r + 64, g, t * P:(t + 1) * P]
                o = YN[:, t, hd * 64:hd * 64 + 64]
                lo = 0 if t < 2 else 2
                u = {"q": q, "k": [(0, 512 - lo * P, KN[r:r + 64, g, lo * P:512])], "nk": 512 - lo * P, "dv": 64, "o": o,
                     "v": [VN[:, a, hd * 64:hd * 64 + 64] for a in range(lo, 4)]}
                if t < 2:
                    u["bias"] = [(0, SEQ, K("flip64"), BM[:, t, hd, :])]
                na_units.append(u)
                da_units.append({"q": QD5[r:r + 64, g, t * P:(t + 1) * P], "k": [(0, 512 - lo * P, KD5[r:r + 64, g, lo * P:512])],
                                 "nk": 512 - lo * P, "dv": P, "o": OD[:, t, hd * P:(hd + 1) * P],
                                 "v": [VD5[:, a, g * P:(g + 1) * P] for a in range(lo, 4)]})

        def fl(ap):
            return ap.rearrange("p a b -> p (a b)")

        def pe_even():
            pe_norm("mod e", [0, 1, 2, 3], XN5)
            pe_feature_block("win0", "qn", tok=512)
            pe_feature_block("win1", "kn", tok=512)
            pe_token_blocks(["win2"], [KT], "vn", ht, tiles=4)
            pe_feature_block("win3", "qd", tok=512)
            pe_feature_block("win4", "kd", tok=512)
            pe_token_blocks(["win5"], [KT], "vd", ht, tiles=4)
            for n in ("qn5", "kn5", "qd5", "kd5"):
                pe_head_norm(n, fl(SQ5), 4)
            for n, Q in (("qd", QD5), ("kd", KD5)):
                pe.wait_ge(vector_done, at(f"{n}5 normed"))
                for g in range(4):
                    ps = open_bank(f"rot {n}{g}")
                    mm(ps[:, 0:SEQ], K("rotate_pairs"), Q[:, g, 0:SEQ], True, True).then_inc(tensor_done, pe.one())
                    pe.mark(f"rot {n}{g}")
            ps = open_bank("lam")
            pe.wait_ge(vector_done, at("lam in"))
            mm(ps[:, 0:2], K("ones"), LAMR[:, 0:2], True, True).then_inc(tensor_done, pe.one())
            pe.mark("lam")
            pe.wait_ge(vector_done, at("even heads"))
            pe.wait_ge(vector_done, at("bm ready"))
            pe_attention("na", na_units, BUF5)
            pe_attention("da", da_units, BUF5)
            pe.wait_ge(vector_done, at("yd src"))
            for t in range(4):
                for h, Y in enumerate((YN, YD)):
                    pe_turn(f"yd turned {t}.{h}", [Y[:, t, i * P:(i + 1) * P] for i in range(4)])
            pe.wait_ge(scalar_done, at("yd ready"))
            for h in range(2):
                pe_token_blocks([f"wout{h}"], [KT], f"wout{h}", lambda k, t: (QN if k < 4 else KN)[:, k % 4, t * P:(t + 1) * P], tiles=4)

        def act_even():
            act_norm("mod e", [0, 1, 2, 3], JK5)
            for n, Q in (("qn", QN), ("kn", KN), ("vn", VN), ("qd", QD5), ("kd", KD5), ("vd", VD5)):
                for j in range(4):
                    copy_out(act, f"{n}.{j}", Q[:, j, :])
                act.wait_ge(scalar_done, act.n)
                act.mark(f"{n} out")
            for n in ("qn5", "kn5", "qd5", "kd5"):
                act_head_norm(n, fl(SQ5), 4, 1.0 / 64)
            ps = full(act, "lam")
            activation(LAMR[:, 2:4], ps[:, 0:2], ACT.Exp).then_inc(scalar_done, act.one())
            act.wait_ge(scalar_done, act.n)
            act.mark("read lam", "lam exp")
            act_attention("na", na_units, BUF5)
            act_attention("da", da_units, BUF5)
            act.wait_ge(vector_done, at("subln ss"))
            activation(SM[:, 152:168], SM[:, 152:168], ACT.Sqrt, bias=K("eps"), scale=1.0 / P).then_inc(scalar_done, act.one())
            act.wait_ge(scalar_done, act.n)
            act.mark("subln root")
            for t in range(4):
                for h, Q in enumerate((QN, KN)):
                    n = f"yd turned {t}.{h}"
                    ps = full(act, n)
                    activation(Q[:, :, t * P:(t + 1) * P], k4(ps[:, :]), ACT.Copy).then_inc(scalar_done, act.one())
                    act.mark("read " + n)
            act.wait_ge(scalar_done, act.n)
            act.mark("yd ready")

        def dve_rope(n, Q, tmp):
            for g in range(4):
                ps = full(dve, f"rot {n}{g}")
                tt(tmp[:, 0:SEQ], ps[:, 0:SEQ], RC[:, 1, :], ALU.mult).then_inc(vector_done, dve.one())
                dve.wait_ge(vector_done, dve.n)
                dve.mark(f"read rot {n}{g}")
                tt(Q[:, g, 0:SEQ], Q[:, g, 0:SEQ], RC[:, 0, :], ALU.mult).then_inc(vector_done, dve.one())
                dve.wait_ge(vector_done, dve.n)
                tt(Q[:, g, 0:SEQ], Q[:, g, 0:SEQ], tmp[:, 0:SEQ], ALU.add).then_inc(vector_done, dve.one())
                dve.wait_ge(vector_done, dve.n)

        def dve_even():
            dve_norm("mod e", [0, 1, 2, 3], XN5, mod_scale(0), mod_shift(0))
            for n, Q, sc in (("qn", QN, 0.125), ("kn", KN, 1.0), ("qd", QD5, 0.125), ("kd", KD5, 1.0)):
                dve.wait_ge(scalar_done, at(f"{n} out"))
                col = C({"qn": "na_q", "kn": "na_k", "qd": "da_q", "kd": "da_k"}[n])
                dve_head_norm(n + "5", fl(Q), fl(SQ5), 4, lambda i: col, sc)
            dve.wait_ge(loaded["even"], at("rope in"))
            dve_rope("qd", QD5, fl(SQ5))
            dve_rope("kd", KD5, fl(SQ5))
            tt(LAMR[:, 0:2], C("lam", 0, 2), C("lam", 2, 2), ALU.mult).then_inc(vector_done, dve.one())
            dve.wait_ge(vector_done, dve.n)
            dve.mark("lam in")
            dve.wait_ge(scalar_done, at("lam exp"))
            tt(LAMR[:, 4:5], LAMR[:, 3:4], LAMR[:, 2:3], ALU.subtract).then_inc(vector_done, dve.one())
            dve.wait_ge(vector_done, dve.n)
            ts(LAMR[:, 4:5], LAMR[:, 4:5], -(0.8 - 0.6), None, ALU.add).then_inc(vector_done, dve.one())
            dve.wait_ge(vector_done, dve.n)
            dve.wait_ge(loaded["bias"], at("bm loaded"))
            dve.wait_ge(scalar_done, at("vd out"))
            dve.wait_ge(scalar_done, at("vn out"))
            tt(BM.rearrange("p a b c -> p (a b) c"), BM.rearrange("p a b c -> p (a b) c"), rows(NM, 16), ALU.add).then_inc(vector_done, dve.one())
            dve.wait_ge(vector_done, dve.n)
            dve.mark("bm ready", "even heads")
            dve_attention("na", na_units, BUF5)
            dve_attention("da", da_units, BUF5)
            for t in range(4):
                o = OD[:, t, :].rearrange("p (h w c) -> p h w c", h=4, w=2)
                yd = YD[:, t, :].rearrange("p (h c) -> p h c", h=4)
                stt(yd, o[:, :, 1, :], LAMR[:, 4:5], o[:, :, 0, :], ALU.mult, ALU.add).then_inc(vector_done, dve.one())
                dve.wait_ge(vector_done, dve.n)
            y = YD.rearrange("p t (h c) -> p (t h) c", h=4)
            sq = OD.rearrange("p t c -> p (t c)")[:, 0:2048].rearrange("p (a c) -> p a c", a=16)
            tt(sq, y, y, ALU.mult).then_inc(vector_done, dve.one())
            dve.wait_ge(vector_done, dve.n)
            nc.vector.tensor_reduce(SM[:, 152:168], sq, AX.X, ALU.add).then_inc(vector_done, dve.one())
            dve.wait_ge(vector_done, dve.n)
            dve.mark("subln ss")
            dve.wait_ge(scalar_done, at("subln root"))
            nc.vector.reciprocal(SM[:, 152:168], SM[:, 152:168]).then_inc(vector_done, dve.one())
            dve.wait_ge(vector_done, dve.n)
            tt(y, y, bc(SM[:, 152:168], [P, 16, P]), ALU.mult).then_inc(vector_done, dve.one())
            dve.wait_ge(vector_done, dve.n)
            stt(y, y, 1.0 - (0.8 - 0.6), rows(SUBG, 16), ALU.mult, ALU.mult).then_inc(vector_done, dve.one())
            dve.wait_ge(vector_done, dve.n)
            dve.mark("yd src")
            for h in range(2):
                dve_add("wout", h, [0, 1, 2, 3], gate_row(0))

        ar = Arena(base2)
        QG, KG, VG = ar.take(4, SEQ), ar.take(512), ar.take(4, P)
        UR = ar.take(12, SEQ + 2)
        UC = ar.take(12, SEQ)
        ZT = ar.take(SEQ)
        DEC = ar.take(4, 512)
        DF = ar.take(2, 2 * SEQ + P)
        DI = ar.take(5, SEQ)
        RC7 = ar.take(2, SEQ)
        SQ7 = ar.take(1024)
        HS = ar.take(4, 512)
        YT7 = ar.take(4, SEQ)
        ZTM = ar.take(2, 512)
        KF7 = fl(UR)[:, 0:5 * 512].rearrange("p (a c) -> p a c", a=5)
        HF = ar.take(SEQ)
        XN7 = HS.rearrange("p a b -> p (a b)").rearrange("p (a b) -> p a b", a=2)
        JK7 = UC.rearrange("p a b -> p (a b)")[:, 0:2 * D].rearrange("p (a b) -> p a b", a=2)
        ZF = HT.rearrange("p k c -> p (k c)")[:, 0:2560].rearrange("p (a c) -> p a c", a=5)
        TF = DEC.rearrange("p a b -> p (a b)")[:, 0:1024].rearrange("p (a c) -> p a c", a=2)
        YG = HT.rearrange("p k c -> p (k c)")[:, 2560:3584].rearrange("p (t c) -> p t c", t=2)
        OT7 = SQ7.rearrange("p (g c) -> p g c", g=4)
        BUF7 = {"P": HS[:, 0:2, :], "PT": HS[:, 2:4, :], "st": SM[:, 144:152].rearrange("p (a b) -> p a b", a=2)}
        gqa_units = []
        for kv in range(2):
            r = 64 * kv
            for g in range(4):
                hd = 4 * kv + g
                for t in range(2):
                    gqa_units.append({"q": QG[r:r + 64, g, t * P:(t + 1) * P], "k": [(0, 512, KG[r:r + 64, :])],
                                      "nk": 512, "dv": 64, "o": YG[:, t, hd * 64:hd * 64 + 64],
                                      "v": [VG[:, a, kv * 64:kv * 64 + 64] for a in range(4)]})

        def pe_odd():
            pe_norm("mod o", [0, 1, 2, 3], XN7)
            pe_feature_block("gq", "gq")
            w = weight("gkv")[:, 0:2048].rearrange("p (k c) -> p k c", k=KT)
            ps = open_bank("gk")
            for k in range(KT):
                last = mm(ps[:, :], w[:, k, 0:P], HT[:, k, :], k == 0, k == KT - 1)
            last.then_inc(tensor_done, pe.one())
            pe.mark("gk")
            ps = open_bank("gv")
            for t in range(4):
                for k in range(KT):
                    last = mm(ps[:, t * P:(t + 1) * P], ht(k, t), w[:, k, P:2 * P], k == 0, k == KT - 1)
            weight_used(last, "gkv")
            pe.mark("gv")
            for i in range(3):
                pe_feature_block(f"hin{i}", "hu", m0=4 * i)
            w = weight("hfilter")
            pe.wait_ge(loaded["odd"], at("hyena in"))
            src = ZT[0:33, :]
            for j in range(3):
                if j > 0:
                    pe.wait_ge(scalar_done, at(f"filter{j - 1}"))
                    src = HF[0:64, :]
                ps = open_bank(f"filter mm{j}")
                n = 33 if j == 0 else 64
                mm(ps[0:64, 0:SEQ], w[0:n, j * 64:(j + 1) * 64], src, True, True).then_inc(tensor_done, pe.one())
                pe.mark(f"filter mm{j}")
            pe.wait_ge(scalar_done, at("filter2"))
            for h in range(2):
                for t in range(2):
                    ps = open_bank(f"taps{h}.{t}")
                    mm(ps[:, :], HF[0:64, t * P:(t + 1) * P], w[0:64, 192 + h * 512:192 + (h + 1) * 512], True, True).then_inc(tensor_done, pe.one())
                    pe.mark(f"taps{h}.{t}")
            pe.mark("slot of hfilter")
            pe.wait_ge(vector_done, at("taps abs"))
            ps = open_bank("taps sum")
            for j in range(4):
                last = mm(ps[:, :], K("ones"), TABS[:, j, :], j == 0, j == 3)
            last.then_inc(tensor_done, pe.one())
            pe.mark("taps sum")
            pe.wait_ge(vector_done, at("z fm"))
            for t in range(2):
                pe_turn(f"z turned{t}", [UC[:, 8 + g, t * P:(t + 1) * P] for g in range(4)])

            def spectrum(label, even, odd):
                for j in range(5):
                    ps = open_bank(f"{label}{j}")
                    m = P if j < 4 else 1
                    for t in range(2):
                        s = (even if j in (0, 1, 4) else odd)[:, t, :]
                        last = mm(ps[0:m, :], DF[:, t, j * P:j * P + m], s, t == 0, t == 1)
                    last.then_inc(tensor_done, pe.one())
                    pe.mark(f"{label}{j}")

            pe.wait_ge(scalar_done, at("z tm"))
            spectrum("zf", ZTM, ZTM)
            pe.wait_ge(vector_done, at("taps ready"))
            spectrum("kf", DEC[:, 0:2, :], DEC[:, 2:4, :])
            pe.wait_ge(vector_done, at("spectrum"))
            for q in range(2):
                ps = open_bank(f"long{q}")
                for i in range(2):
                    g = 2 * q + i
                    o = ps[:, i * SEQ:(i + 1) * SEQ]
                    for j in range(4):
                        mm(o, ZF[:, j, g * P:(g + 1) * P], DI[:, j, :], j == 0, False)
                    last = mm(o, ZF[0:1, 4, g * P:(g + 1) * P], DI[0:1, 4, :], False, True)
                last.then_inc(tensor_done, pe.one())
                pe.mark(f"long{q}")
            pe_head_norm("gq7", SQ7, 2)
            pe_head_norm("gk7", SQ7, 1)
            pe.wait_ge(vector_done, at("gk7 normed"))
            for n, Q in [(f"gq{g}", QG[:, g, :]) for g in range(4)] + [("gk", KG[:, 0:SEQ])]:
                ps = open_bank("rot " + n)
                mm(ps[:, 0:SEQ], K("rotate_pairs"), Q, True, True).then_inc(tensor_done, pe.one())
                pe.mark("rot " + n)
            pe.wait_ge(vector_done, at("gqa heads"))
            pe_attention("gqa", gqa_units, BUF7)
            pe.wait_ge(vector_done, at("yg"))
            for t in range(2):
                pe_turn(f"yg turned{t}", [YG[:, t, i * P:(i + 1) * P] for i in range(4)])
            pe.wait_ge(scalar_done, at("yg ready"))
            for h in range(2):
                pe_token_blocks([f"oout{h}"], [KT], f"oout{h}", lambda k, t: (OT7 if k < 4 else YT7)[:, k % 4, t * P:(t + 1) * P])

        def act_odd():
            act_norm("mod o", [0, 1, 2, 3], JK7)
            for j in range(2):
                copy_out(act, f"gq.{j}", QG[:, 2 * j:2 * j + 2, :], lambda ps: ps[:, :].rearrange("p (a c) -> p a c", a=2))
            copy_out(act, "gk", KG)
            copy_out(act, "gv", VG.rearrange("p a b -> p (a b)"))
            act.wait_ge(scalar_done, act.n)
            act.mark("g out")
            act.wait_ge(vector_done, at("ur zero"))
            for j in range(6):
                copy_out(act, f"hu.{j}", UR[:, 2 * j:2 * j + 2, 1:1 + SEQ], lambda ps: ps[:, :].rearrange("p (a c) -> p a c", a=2))
            act.wait_ge(scalar_done, act.n)
            act.mark("hu out")
            for j in range(3):
                act.wait_ge(vector_done, at(f"angle{j}"))
                activation(HF[0:64, :], HF[0:64, :], ACT.Sin).then_inc(scalar_done, act.one())
                act.wait_ge(scalar_done, act.n)
                act.mark(f"filter{j}")
            for t in range(2):
                copy_out(act, f"z turned{t}", ZTM[:, t, :])
            act.wait_ge(scalar_done, act.n)
            act.mark("z tm")
            for j in range(5):
                m = P if j < 4 else 1
                copy_out2(act, f"zf{j}", ZF[0:m, j, :], m)
            act.wait_ge(scalar_done, act.n)
            act.mark("zf out")
            act.wait_ge(vector_done, at("hu free"))
            for j in range(5):
                m = P if j < 4 else 1
                copy_out2(act, f"kf{j}", KF7[0:m, j, :], m)
            act.wait_ge(scalar_done, act.n)
            act.mark("kf out")
            act_head_norm("gq7", SQ7, 2, 1.0 / 64)
            act_head_norm("gk7", SQ7, 1, 1.0 / 64)
            act_attention("gqa", gqa_units, BUF7)
            for t in range(2):
                n = f"yg turned{t}"
                ps = full(act, n)
                activation(OT7[:, :, t * P:(t + 1) * P], k4(ps[:, :]), ACT.Copy).then_inc(scalar_done, act.one())
                act.mark("read " + n)
            act.wait_ge(scalar_done, act.n)
            act.mark("yg ready")

        def copy_out2(e, label, dst, m):
            ps = full(e, label)
            nc.scalar.activation(dst, ps[0:m, :], ACT.Copy).then_inc(e.done, e.one())
            e.mark("read " + label)

        TABS = fl(UR)[:, 0:2048].rearrange("p (a c) -> p a c", a=4)
        TWO_PI_HI = 6.28125
        TWO_PI_LO = 2 * math.pi - 6.28125
        ROUND = 12582912.0

        def dve_odd():
            dve_norm("mod o", [0, 1, 2, 3], XN7, mod_scale(0), mod_shift(0))
            nc.vector.memset(UR, 0.0).then_inc(vector_done, dve.one())
            dve.wait_ge(vector_done, dve.n)
            dve.mark("ur zero")
            dve.wait_ge(scalar_done, at("hu out"))
            for g in range(12):
                ts(UC[:, g, :], UR[:, g, 0:SEQ], C("hconv_w", g), C("hconv_b", g), ALU.mult, ALU.add).then_inc(vector_done, dve.one())
            dve.wait_ge(vector_done, dve.n)
            for i in (1, 2):
                for g in range(12):
                    stt(UC[:, g, :], UR[:, g, i:i + SEQ], C("hconv_w", 12 * i + g), UC[:, g, :], ALU.mult, ALU.add).then_inc(vector_done, dve.one())
                dve.wait_ge(vector_done, dve.n)
            tt(UC[:, 8:12, :], UC[:, 8:12, :], UC[:, 4:8, :], ALU.mult).then_inc(vector_done, dve.one())
            dve.wait_ge(vector_done, dve.n)
            dve.mark("z fm")
            tmp = RC7B[0:64, :]
            h = HF[0:64, :]
            for j in range(3):
                ps = full(dve, f"filter mm{j}")
                ts(h, ps[0:64, 0:SEQ], C("hb", j)[0:64, :], C("hfreq")[0:64, :], ALU.add, ALU.mult).then_inc(vector_done, dve.one())
                dve.wait_ge(vector_done, dve.n)
                dve.mark(f"read filter mm{j}")
                ts(tmp, h, 1.0 / (2 * math.pi), ROUND, ALU.mult, ALU.add).then_inc(vector_done, dve.one())
                dve.wait_ge(vector_done, dve.n)
                ts(tmp, tmp, ROUND, None, ALU.subtract).then_inc(vector_done, dve.one())
                dve.wait_ge(vector_done, dve.n)
                stt(h, tmp, -TWO_PI_HI, h, ALU.mult, ALU.add).then_inc(vector_done, dve.one())
                dve.wait_ge(vector_done, dve.n)
                stt(h, tmp, -TWO_PI_LO, h, ALU.mult, ALU.add).then_inc(vector_done, dve.one())
                dve.wait_ge(vector_done, dve.n)
                ts(h, h, 3.1415925, -3.1415925, ALU.min, ALU.max).then_inc(vector_done, dve.one())
                dve.wait_ge(vector_done, dve.n)
                dve.mark(f"angle{j}")
            dve.wait_ge(loaded["odd"], at("hyena in"))
            for hh in range(2):
                for t in range(2):
                    ps = full(dve, f"taps{hh}.{t}")
                    tt(HS[:, 2 * hh + t, :], ps[:, :], DEC[:, 2 * hh + t, :], ALU.mult).then_inc(vector_done, dve.one())
                    dve.mark(f"read taps{hh}.{t}")
            dve.wait_ge(vector_done, dve.n)
            stt(TABS, HS, -1.0, HS, ALU.mult, ALU.max).then_inc(vector_done, dve.one())
            dve.wait_ge(vector_done, dve.n)
            dve.mark("taps abs")
            ps = full(dve, "taps sum")
            nc.vector.reciprocal(JN, ps[:, :]).then_inc(vector_done, dve.one())
            dve.wait_ge(vector_done, dve.n)
            dve.mark("read taps sum")
            tt(HS, HS, rows(JN, 4), ALU.mult).then_inc(vector_done, dve.one())
            dve.wait_ge(vector_done, dve.n)
            tt(DEC[:, 0:2, :], HS[:, 0:2, :], HS[:, 2:4, :], ALU.add).then_inc(vector_done, dve.one())
            tt(DEC[:, 2:4, :], HS[:, 0:2, :], HS[:, 2:4, :], ALU.subtract).then_inc(vector_done, dve.one())
            dve.wait_ge(vector_done, dve.n)
            dve.mark("taps ready", "hu free")
            dve.wait_ge(scalar_done, at("zf out"))
            dve.wait_ge(scalar_done, at("kf out"))
            Zr, Zi, Kr, Ki = ZF[:, 0:2, :], ZF[:, 2:4, :], KF7[:, 0:2, :], KF7[:, 2:4, :]
            T0, T1_ = DEC[:, 0:2, :], DEC[:, 2:4, :]
            tt(ZF[0:1, 4, :], ZF[0:1, 4, :], KF7[0:1, 4, :], ALU.mult).then_inc(vector_done, dve.one())
            tt(T0, Zi, Ki, ALU.mult).then_inc(vector_done, dve.one())
            tt(T1_, Zi, Kr, ALU.mult).then_inc(vector_done, dve.one())
            dve.wait_ge(vector_done, dve.n)
            tt(Zi, Zr, Ki, ALU.mult).then_inc(vector_done, dve.one())
            dve.wait_ge(vector_done, dve.n)
            tt(Zr, Zr, Kr, ALU.mult).then_inc(vector_done, dve.one())
            dve.wait_ge(vector_done, dve.n)
            tt(Zi, Zi, T1_, ALU.add).then_inc(vector_done, dve.one())
            dve.wait_ge(vector_done, dve.n)
            tt(Zr, Zr, T0, ALU.subtract).then_inc(vector_done, dve.one())
            dve.wait_ge(vector_done, dve.n)
            dve.mark("spectrum")
            for q in range(2):
                ps = full(dve, f"long{q}")
                for i in range(2):
                    g = 2 * q + i
                    stt(YT7[:, g, :], UC[:, 8 + g, :], C("hskip", g), ps[:, i * SEQ:(i + 1) * SEQ], ALU.mult, ALU.add).then_inc(vector_done, dve.one())
                    dve.wait_ge(vector_done, dve.n)
                    tt(YT7[:, g, :], YT7[:, g, :], UC[:, g, :], ALU.mult).then_inc(vector_done, dve.one())
                    dve.wait_ge(vector_done, dve.n)
                dve.mark(f"read long{q}")
            dve.wait_ge(scalar_done, at("g out"))
            dve_head_norm("gq7", fl(QG), SQ7, 2, lambda i: C("gqa_q"), 0.125)
            dve_head_norm("gk7", KG, SQ7[:, 0:512], 1, lambda i: C("gqa_k"), 1.0)
            dve.wait_ge(loaded["odd"], at("rope7 in"))
            for n, Q in [(f"gq{g}", QG[:, g, :]) for g in range(4)] + [("gk", KG[:, 0:SEQ])]:
                ps = full(dve, "rot " + n)
                tt(JN[:, 0:SEQ], ps[:, 0:SEQ], RC7[:, 1, :], ALU.mult).then_inc(vector_done, dve.one())
                dve.wait_ge(vector_done, dve.n)
                dve.mark("read rot " + n)
                tt(Q, Q, RC7[:, 0, :], ALU.mult).then_inc(vector_done, dve.one())
                dve.wait_ge(vector_done, dve.n)
                tt(Q, Q, JN[:, 0:SEQ], ALU.add).then_inc(vector_done, dve.one())
                dve.wait_ge(vector_done, dve.n)
            dve.mark("gqa heads")
            dve_attention("gqa", gqa_units, BUF7)
            dve.mark("yg")
            for h_ in range(2):
                dve_add("oout", h_, [0, 1], gate_row(0))

        def toeplitz(ap, offset, pattern):
            return bass.AP(tensor=ap.tensor, offset=offset, ap=pattern)

        JN = junk512
        RC7B = junk512[:, 0:SEQ]

        XN0 = XN1

        PH = ["start", "rwkv", "gdn", "eout", "mlp0", "attn", "mlp1", "ada0", "even", "ffn0", "ada1", "odd", "ffn1"]

        @block.sync
        def _(sp):
            e = Steps(sp, stored, marks)
            for i, (name, cols) in enumerate(PLAN):
                if i >= RING:
                    e.wait_ge(tensor_done, at("slot of " + PLAN[i - RING][0]))
                sp.dma_start(ring[:, i % RING, 0:cols], T["W"][i, :, 0:cols]).then_inc(slot_loaded[i % RING], 16)
            e.wait_ge(vector_done, at("dve end ffn1"))
            sp.dma_start(out.rearrange("b (t p) d -> p (b t) d", p=P), X[:, 0:2, :]).then_inc(stored, 16)
            sp.wait_ge(stored, 16)

        @block.gpsimd
        def _(pool):
            e = Steps(pool, loaded["start"], marks, by=16)
            group = {n: Steps(pool, loaded[n], marks, by=16) for n in LOADS}

            def load(which, dst, src):
                pool.dma_start(dst, src).then_inc(loaded[which], group[which].one())

            def row(name, n=P):
                a, c = RPLAN[name]
                return T["rowp"][0:1, a:a + c].broadcast_to([n, c])

            load("start", X[:, 0:2, :], T["x"])
            load("start", KC[:, :], T["const"])
            load("start", CP[:, :], T["colp"])
            load("start", X[:, 2:4, :], T["ctx"])
            load("start", ALr, row("a_log"))
            load("start", DTr, row("dt"))
            group["start"].mark("start in", "rows 1c")
            e.wait_ge(vector_done, at("rwkv solved"))
            load("rwkv_rows", LNG, row("ln_g"))
            load("rwkv_rows", LNB, row("ln_b"))
            group["rwkv_rows"].mark("rows 1b")

            def after(ph):
                e.wait_ge(tensor_done, at(f"pe end {ph}"))
                e.wait_ge(scalar_done, at(f"act end {ph}"))
                e.wait_ge(vector_done, at(f"dve end {ph}"))

            after("rwkv")
            load("gdn_rows", NG, row("gdn_g"))
            group["gdn_rows"].mark("norm b")
            for i in range(2):
                after("eout" if i == 0 else "attn")
                load(f"ple{i}", M["pT"], T["pT"][i].rearrange("p (k c) -> p k c", k=2))
                load(f"ple{i}", M["pg"], row(f"ple{i}"))
                group[f"ple{i}"].mark(f"p{i}", f"rows ple{i}")
                if i == 0:
                    after("mlp0")
                    h = T["rel"]
                    for hd in range(16):
                        load("rel", REL[:, hd, :], toeplitz(h, hd * 513 + 129, [[1, P], [1, SEQ]]))
                    group["rel"].mark("rel")
            after("mlp1")
            load("ada0", MOD[0:2, :], row("bada0", 2))
            group["ada0"].mark("rows ada0")
            after("ada0")
            load("even", RC, T["rope"].rearrange("p (a c) -> p a c", a=2))
            load("even", NM, T["nmask"])
            load("even", SUBG, row("subln"))
            group["even"].mark("rope in")
            e.wait_ge(scalar_done, at("mod e rms"))
            for t in range(2):
                for rq in range(2):
                    for hd in range(8):
                        off = (hd * 15 + 7 - (2 * t + rq)) * P
                        load("bias", BM[64 * rq:64 * rq + 64, t, hd, :].rearrange("p (a b) -> p a b", a=4),
                             toeplitz(T["rpb"], off, [[1, 64], [P, 4], [1, 64]]))
            group["bias"].mark("bm loaded")
            after("ffn0")
            load("ada1", MOD[0:2, :], row("bada1", 2))
            group["ada1"].mark("rows ada1")
            after("ada1")
            load("odd", RC7, T["rope"].rearrange("p (a c) -> p a c", a=2))
            load("odd", ZT, T["hconst"][:, 0:SEQ])
            load("odd", DEC, T["hconst"][:, SEQ:SEQ + 2048].rearrange("p (a c) -> p a c", a=4))
            load("odd", DF, T["dft"][:, 0:1280].rearrange("p (a c) -> p a c", a=2))
            load("odd", DI, T["dft"][:, 1280:2560].rearrange("p (a c) -> p a c", a=5))
            group["odd"].mark("rope7 in", "hyena in")

        @block.tensor
        def _(tensor):
            pe_steps = [pe_start, lambda: (pe_norm("mix0", [0, 1], XN0), pe_rwkv()), pe_gdn, pe_eout, lambda: pe_mlp(0),
                        pe_attn, lambda: pe_mlp(1), lambda: pe_ada(0), pe_even, lambda: pe_ffn(0, 2), lambda: pe_ada(1), pe_odd,
                        lambda: pe_ffn(1, 1)]
            for name, f in zip(PH, pe_steps):
                f()
                phase_end(pe, name, "pe")

        @block.scalar
        def _(scalar):
            JK0 = ar2b
            act_steps = [act_start, lambda: (act_norm("mix0", [0, 1], JK0), act_rwkv()), act_gdn,
                         act_eout, lambda: act_mlp(0), act_attn, lambda: act_mlp(1),
                         lambda: act_ada(0), act_even, lambda: act_ffn(0, 2), lambda: act_ada(1), act_odd, lambda: act_ffn(1, 1)]
            for name, f in zip(PH, act_steps):
                f()
                phase_end(act, name, "act")

        @block.vector
        def _(vector):

            dve_steps = [dve_start,
                         lambda: (dve_norm("mix0", [0, 1], XN0, lambda t: C("mix0", 0, 8)), dve_rwkv()), dve_gdn, dve_eout, lambda: dve_mlp(0),
                         dve_attn, lambda: dve_mlp(1), lambda: dve_ada(0), dve_even, lambda: dve_ffn(0, 2), lambda: dve_ada(1), dve_odd,
                         lambda: dve_ffn(1, 1)]
            for name, f in zip(PH, dve_steps):
                f()
                phase_end(dve, name, "dve")

        names = {id(v): k for k, v in sems.items()}
        for k, v in marks.items():
            if k != "unknown":
                counts[k] = (names[id(v[0])], v[1])
    return counts


def lay_out(a):
    f = {k: np.asarray(v) for k, v in a.items()}

    def tiled(w):
        k, n = w.shape
        return w.reshape(k // P, P, n).transpose(1, 0, 2).reshape(P, -1)

    blocks = {}

    def put(name, w):
        blocks[name] = tiled(w)

    def cols(prefix, w, at=0):
        for i in range(w.shape[1] // 512):
            put(f"{prefix}{at + i}", w[:, i * 512:(i + 1) * 512])

    w = f["even_w_in"][0]
    cols("rkv", w[:, 0:1536])
    cols("bqkv", w[:, 1536:3072])
    put("bgate", w[:, 3072:3584])
    put("bab", w[:, 3584:3592])
    put("lora_in", np.concatenate([f["rwkv_w1"][0], f["rwkv_a1"][0], f["rwkv_g1"][0]], 1))
    up = np.zeros((P, 1536), np.float32)
    up[:64, 0:512], up[:64, 512:1024], up[:, 1024:] = f["rwkv_w2"][0], f["rwkv_a2"][0], f["rwkv_g2"][0]
    blocks["lora_out"] = up
    cols("eout", f["even_w_out"][0])
    for i in range(2):
        cols(f"up{i}.", f["mlp_w1"][i])
        for h in range(2):
            for n in range(4):
                put(f"down{i}.{h}.{n}", f["mlp_w2"][i][n * 1024:(n + 1) * 1024, h * 512:(h + 1) * 512])
            put(f"pgate{i}.{h}", f["ple_w_gate"][i][:, h * 512:(h + 1) * 512])
        put(f"pproj{i}", f["ple_w_proj"][i])
        cols(f"ada{i}.", f["w_ada_2"][i])
        wu = f["w_up_2"][i]
        pair = np.stack([wu[:, :2816].reshape(D, 22, P), wu[:, 2816:].reshape(D, 22, P)], 2).reshape(D, -1)
        cols(f"cup{i}.", pair)
        for h in range(2):
            for n in range(3):
                put(f"cdown{i}.{h}.{n}", f["w_down_2"][i][n * 1024:(n + 1) * 1024, h * 512:(h + 1) * 512])
    cols("qkv", f["attn_w_qkv"][0])
    cols("aout", f["attn_w_out"][0])
    cols("win", f["w_in_e_2"][0])
    cols("wout", f["w_out_e_2"][0])
    w = f["w_in_o_2"][0]
    put("gq", w[:, 0:512].reshape(D, 2, 4, 64).transpose(0, 2, 1, 3).reshape(D, 512))
    put("gkv", w[:, 512:768])
    cols("hin", w[:, 768:])
    hf = np.zeros((P, 1216), np.float32)
    hf[:33, 0:64] = f["hy_w1_2"][0]
    hf[:64, 64:128], hf[:64, 128:192], hf[:64, 192:] = f["hy_w2_2"][0], f["hy_w3_2"][0], f["hy_w4_2"][0]
    blocks["hfilter"] = hf
    cols("oout", f["w_out_o_2"][0])
    plan = weight_plan()
    W = np.zeros((len(plan), P, SLOT), np.float32)
    for i, (name, n) in enumerate(plan):
        assert blocks[name].shape[1] == n, (name, blocks[name].shape, n)
        W[i, :, :n] = blocks[name]

    def col(v):
        return np.ascontiguousarray(v).reshape(-1, P).T

    def twice(v):
        return np.concatenate([v, v])

    def pad(v):
        o = np.zeros((P,), np.float32)
        o[:v.shape[0]] = v
        return o[:, None]

    lam = [f[f"da_lambda_{n}_2"][0] for n in ("q1", "q2", "k1", "k2")]
    cp = {"mix0": col(f["norm_mix_g"][0]), "mix1": col(f["norm_mix_g"][1]), "ffn0": col(f["norm_ffn_g"][0]),
          "ffn1": col(f["norm_ffn_g"][1]), "mu_proj": col(f["rwkv_mu_proj"][0]), "mu_lora": col(f["rwkv_mu_lora"][0]),
          "w0": col(f["rwkv_w0"][0]), "a0": col(f["rwkv_a0"][0]), "k_k": col(f["rwkv_k_k"][0]), "k_a": col(f["rwkv_k_a"][0]),
          "r_k": col(f["rwkv_r_k"][0]), "conv": col(f["gdn_conv_w"][0]), "attn_q": twice(f["attn_q_g"][0])[:, None],
          "attn_k": twice(f["attn_k_g"][0])[:, None],
          "c": np.stack([col(f["c_2"][0]), col(f["c_ctx_2"])], 2).reshape(P, 16),
          "fconv_w0": col(f["ffn_conv_w_2"][0]), "fconv_b0": col(f["ffn_conv_b_2"][0]), "fconv_w1": col(f["ffn_conv_w_2"][1]),
          "fconv_b1": col(f["ffn_conv_b_2"][1]), "na_q": twice(f["na_q_gain_2"][0])[:, None], "na_k": twice(f["na_k_gain_2"][0])[:, None],
          "da_q": twice(f["da_q_gain_2"][0])[:, None], "da_k": twice(f["da_k_gain_2"][0])[:, None],
          "lam": np.concatenate([pad(v) for v in lam], 1), "gqa_q": twice(f["gqa_q_gain_2"][0])[:, None],
          "gqa_k": twice(f["gqa_k_gain_2"][0])[:, None], "hconv_w": col(f["hy_conv_w_2"][0]), "hconv_b": col(f["hy_conv_b_2"][0]),
          "hb": np.concatenate([pad(f[f"hy_b{j}_2"][0]) for j in (1, 2, 3)], 1), "hfreq": pad(f["hy_freq_2"][0]), "hskip": col(f["hy_skip_2"][0])}
    colp = np.zeros((P, NCOL), np.float32)
    for name, (at, n) in CPLAN.items():
        assert cp[name].shape == (P, n), (name, cp[name].shape)
        colp[:, at:at + n] = cp[name]
    rp = {"ln_g": f["rwkv_ln_g"][0], "ln_b": f["rwkv_ln_b"][0], "gdn_g": f["gdn_norm_g"][0], "a_log": f["gdn_a_log"][0],
          "dt": f["gdn_dt_bias"][0], "ple0": f["ple_norm_g"][0], "ple1": f["ple_norm_g"][1], "bada0": f["b_ada_2"][0],
          "bada1": f["b_ada_2"][1], "subln": f["da_subln_gain_2"][0]}
    rowp = np.concatenate([rp[n].reshape(-1) for n, _ in ROWS])[None, :]
    rpb = np.zeros((8, 15, P), np.float32)
    rpb[:, :, 48:79] = f["na_rpb_2"][0]
    hconst, dft = hyena_constants()

    def tokens(v):
        return np.ascontiguousarray(v[0].reshape(2, P, -1).transpose(1, 0, 2))

    return {"W": W, "colp": colp, "rowp": np.ascontiguousarray(rowp), "const": np.concatenate(list(CONST.values()), 1),
            "x": tokens(f["x"]), "ctx": tokens(f["ctx_2"]),
            "pT": np.ascontiguousarray(f["p"][:, 0].transpose(0, 2, 1).reshape(2, 2, P, SEQ).transpose(0, 2, 1, 3).reshape(2, P, 512)),
            "rel": np.ascontiguousarray(f["attn_rel_bias"][0]), "rpb": rpb, "rope": rope_constants(), "nmask": neighbour_mask(),
            "hconst": hconst, "dft": dft}


def kernel(**inputs):
    import concourse.bacc as bacc
    from concourse.bass_utils import run_bass_kernel_spmd

    arrays = {f"in_{k}": v for k, v in lay_out(inputs).items()}
    counts = {}
    for _ in range(2):
        nc = bacc.Bacc("TRN2", target_bir_lowering=False, num_devices=1)
        T = {k[3:]: nc.dram_tensor(k, v.shape, F32, kind="ExternalInput").ap() for k, v in arrays.items()}
        out = nc.dram_tensor("out_0", (1, SEQ, D), F32, kind="ExternalOutput").ap()
        counts = build(nc, T, out, counts)
    assert not counts["unknown"], counts["unknown"]
    r = run_bass_kernel_spmd(nc, [arrays], core_ids=[0])
    return r.results[0]["out_0"]
```

```python
from contextlib import ExitStack
import math

import numpy as np
import concourse.bass as bass
from concourse import mybir

ACT = mybir.ActivationFunctionType
ALU = mybir.AluOpType
AX = mybir.AxisListType
F32 = mybir.dt.float32

P = 128
D = 1024
KT = D // P
SEQ = 256
CH = 64
RING = 3
SLOT = 4096
NEG = -1e30


def shape_constants():
    s = np.arange(P)[:, None]
    t = np.arange(P)[None, :]
    same = (s // CH) == (t // CH)
    c = {
        "ident": np.eye(P),
        "ones": np.ones((P, P)),
        "head_ones": same,
        "upto": same & (s <= t),
        "before": same & (s < t),
        "head_pick": (s // CH) == np.arange(2)[None, :],
        "flip": s == P - 1 - t,
        "flip64": same & (s % CH == CH - 1 - t % CH),
    }
    for k in range(6):
        c[f"pair{k}"] = ((s >> (k + 1)) == (t >> (k + 1))) & (((s >> k) & 1) == 0) & (((t >> k) & 1) == 1)
    rot = np.zeros((P, P))
    rot[np.arange(1, P, 2), np.arange(0, P, 2)] = -1.0
    rot[np.arange(0, P, 2), np.arange(1, P, 2)] = 1.0
    c["rotate_pairs"] = rot
    c["carry"] = np.broadcast_to(np.arange(SEQ) % CH != 0, (P, SEQ))
    for i in range(2):
        c[f"stream{i}"] = np.broadcast_to(s == i, (P, P))
    c["late_query"] = np.broadcast_to(t < CH, (P, P))
    c["late_key"] = np.broadcast_to(np.where(t >= CH, NEG, 0.0), (P, P))
    for name, v in (("eps", 1e-6), ("gn_eps", 64e-5), ("one", 1.0)):
        c[name] = np.full((P, 1), v)
    return {k: np.ascontiguousarray(v, dtype=np.float32) for k, v in c.items()}


def rope_constants():
    tok = np.arange(SEQ)
    inv = 10000.0 ** (-np.arange(16, dtype=np.float32) / np.float32(16))
    ang = np.concatenate([(tok // 64)[:, None] * inv, (tok % 64)[:, None] * inv], -1).astype(np.float32)
    ang = np.repeat(ang.T, 2, axis=0)
    ang = np.concatenate([ang, ang], 0)
    return np.concatenate([np.cos(ang), np.sin(ang)], 1).astype(np.float32)


def neighbour_mask():
    q = np.arange(64)
    start = np.clip(q - 8, 0, 48)
    m = np.where((q[None, :] >= start[:, None]) & (q[None, :] < start[:, None] + 16), 0.0, NEG)
    m = m[::-1]
    return np.tile(m, (2, 4)).astype(np.float32)


def hyena_constants():
    n = SEQ
    t = np.linspace(0.0, 1.0, n, dtype=np.float32)[:, None]
    w = 2.0 * math.pi * np.arange(n, dtype=np.float32)[:, None] / n
    f = np.linspace(1e-4, 15, 16, dtype=np.float32)[None, :]
    z = np.concatenate([t, np.cos(f * w), -np.sin(f * w)], -1)
    zt = np.zeros((P, n))
    zt[:33] = z.T
    deltas = np.linspace(math.log(1e-2) / 1.5, math.log(1e-2) / 0.3, 512, dtype=np.float32)
    decay = np.exp(-t * np.abs(deltas))
    back = decay.copy()
    back[0] = 0.0
    dec = np.concatenate([decay.reshape(2, P, 512), back.reshape(2, P, 512)], 0).transpose(1, 0, 2).reshape(P, -1)
    tt = np.arange(n)[:, None].astype(np.float64)
    ff = np.arange(n + 1)[None, :].astype(np.float64)
    ang = 2 * np.pi * tt * ff / (2 * n)
    fre, fim = np.cos(ang), -np.sin(ang)
    fwd = np.zeros((P, 2, 2 * n + P))
    fwd[:, :, :n] = fre[:, :n].reshape(2, P, n).transpose(1, 0, 2)
    fwd[:, :, n:2 * n] = fim[:, :n].reshape(2, P, n).transpose(1, 0, 2)
    fwd[:, :, 2 * n:2 * n + 1] = fre[:, n:].reshape(2, P, 1).transpose(1, 0, 2)
    cf = np.full((n, 1), 2.0)
    cf[0] = 1.0
    ire = cf * fre[:, :n].T / (2 * n)
    iim = cf * fim[:, :n].T / (2 * n)
    ilast = np.zeros((P, n))
    ilast[0] = fre[:, n] / (2 * n)
    inv = np.concatenate([ire.reshape(2, P, n), iim.reshape(2, P, n), ilast[None]], 0).transpose(1, 0, 2)
    return (np.ascontiguousarray(np.concatenate([zt, dec], 1), np.float32),
            np.ascontiguousarray(np.concatenate([fwd.reshape(P, -1), inv.reshape(P, -1)], 1), np.float32))


def weight_plan():
    plan = []
    plan += [(f"rkv{i}", 4096) for i in range(3)] + [("lora_in", 8 * 256), ("lora_out", 3 * 512)]
    plan += [(f"ada{j // 12}.{j % 12}", 4096) for j in range(10)]
    plan += [(f"bqkv{i}", 4096) for i in range(3)] + [("bgate", 4096), ("bab", 64)]
    plan += [(f"ada{j // 12}.{j % 12}", 4096) for j in range(10, 24)]
    plan += [(f"eout{i}", 4096) for i in range(2)]

    def mlp(i):
        return ([(f"up{i}.{n}", 4096) for n in range(8)] + [(f"down{i}.{h}.{n}", 4096) for h in range(2) for n in range(4)]
                + [(f"pproj{i}", 2048)] + [(f"pgate{i}.{h}", 4096) for h in range(2)])

    def ffn(i):
        return ([(f"cup{i}.{n}", 4096) for n in range(11)]
                + [(f"cdown{i}.{h}.{n}", 4096 if n < 2 else 3072) for h in range(2) for n in range(3)])

    plan += mlp(0) + [(f"qkv{i}", 4096) for i in range(6)] + [(f"aout{i}", 4096) for i in range(2)] + mlp(1)
    plan += [(f"win{i}", 4096) for i in range(6)] + [(f"wout{i}", 4096) for i in range(2)] + ffn(0)
    plan += [("gq", 4096), ("gkv", 8 * 256), ("hin0", 4096), ("hfilter", 3 * 64 + 1024), ("hin1", 4096), ("hin2", 4096)]
    plan += [(f"oout{i}", 4096) for i in range(2)] + ffn(1)
    return plan


COLS = {}


def column_plan():
    at, out = 0, {}
    for name, n in (("mix0", 8), ("mix1", 8), ("ffn0", 8), ("ffn1", 8), ("mu_proj", 12), ("mu_lora", 24),
                    ("w0", 4), ("a0", 4), ("k_k", 4), ("k_a", 4), ("r_k", 4), ("conv", 48), ("attn_q", 1), ("attn_k", 1),
                    ("c", 16), ("fconv_w0", 66), ("fconv_b0", 22), ("fconv_w1", 66), ("fconv_b1", 22),
                    ("na_q", 1), ("na_k", 1), ("da_q", 1), ("da_k", 1), ("lam", 4), ("gqa_q", 1), ("gqa_k", 1),
                    ("hconv_w", 36), ("hconv_b", 12), ("hb", 3), ("hfreq", 1), ("hskip", 4), ("bada0", 48), ("bada1", 48)):
        out[name] = (at, n)
        at += n
    return out, at


ROWS = (("ln_g", 512), ("ln_b", 512), ("gdn_g", 128), ("a_log", 4), ("dt", 4), ("ple0", 1024), ("ple1", 1024),
        ("subln", 128))


def row_plan():
    at, out = 0, {}
    for name, n in ROWS:
        out[name] = (at, n)
        at += n
    return out, at


LOADS = ("first", "start", "rwkv_rows", "gdn_rows", "ple0", "rel", "ple1", "even", "bias", "odd")
CPLAN, NCOL = column_plan()
RPLAN, NROW = row_plan()
CONST = shape_constants()
KPLAN = {}
_at = 0
for _k, _v in CONST.items():
    KPLAN[_k] = (_at, _v.shape[1])
    _at += _v.shape[1]
NCONST = _at


class Steps:

    def __init__(self, eng, done, marks, by=1):
        self.eng, self.done, self.marks, self.by = eng, done, marks, by
        self.n, self.seen = 0, {}

    def one(self):
        self.n += self.by
        return self.by

    def wait_ge(self, sem, n):
        key = str(sem)
        if n > self.seen.get(key, 0):
            self.eng.wait_ge(sem, n)
            self.seen[key] = n

    def mark(self, *names):
        for name in names:
            self.marks[name] = (self.done, self.n)


def build(nc, T, out, counts):
    with ExitStack() as ctx:
        def sb(name, shape):
            return ctx.enter_context(nc.sbuf_tensor(name, shape, F32))

        def sem(name):
            return ctx.enter_context(nc.semaphore(name))

        tensor_done, scalar_done, vector_done = sem("tensor_done"), sem("scalar_done"), sem("vector_done")
        slot_loaded = [sem(f"slot_loaded{i}") for i in range(RING)]
        stored = sem("stored")
        loaded = {n: sem("loaded_" + n) for n in LOADS}
        sems = {"pe": tensor_done, "act": scalar_done, "dve": vector_done, **loaded}
        marks = {}
        for k, v in counts.items():
            if k != "unknown" and k != "banks":
                marks[k] = (sems[v[0]], v[1])
        banks = counts.setdefault("banks", {})
        unknown = counts["unknown"] = set()
        marks["unknown"] = unknown

        X = sb("X", [P, 4, D])
        HT = sb("HT", [P, KT, 512])
        ring = sb("ring", [P, RING, SLOT])
        KC = sb("KC", [P, NCONST])
        CP = sb("CP", [P, NCOL])
        small = sb("small", [P, 256])
        MODF = sb("MODF", [P, 208])
        MOD = MODF[:, 0:192].rearrange("p (i m s) -> p i m s", i=2, m=48)
        SC = MODF[:, 192:208].rearrange("p (k s) -> p k s", s=2)
        AR = (nc.sbuf_bytes_remaining if not callable(nc.sbuf_bytes_remaining) else nc.sbuf_bytes_remaining()) // 4 - 32
        arena = sb("arena", [P, AR])
        PS = [ctx.enter_context(nc.psum_tensor(f"bank{i}", [P, 512], F32)) for i in range(8)]

        def K(name):
            a, n = KPLAN[name]
            return KC[:, a:a + n]

        def C(name, i=0, n=1):
            a, _ = CPLAN[name]
            return CP[:, a + i:a + i + n]

        def bc(ap, shape):
            return ap.unsqueeze(len(shape) - 1).broadcast_to(shape)

        def rows(ap, n):
            return ap.unsqueeze(1).broadcast_to([P, n, ap.shape[-1]])

        class Arena:
            def __init__(self, at=0):
                self.at = at

            def take(self, *shape):
                n = int(np.prod(shape))
                v = arena[:, self.at:self.at + n]
                self.at += n
                assert self.at <= AR, (self.at, AR)
                names = "abc"[:len(shape)]
                if len(shape) > 1:
                    v = v.rearrange("p (" + " ".join(names) + ") -> p " + " ".join(names),
                                    **{names[i]: shape[i] for i in range(1, len(shape))})
                return v

        SM = small
        block = ctx.enter_context(nc.Block())
        PLAN = weight_plan()
        WAT = {name: i for i, (name, _) in enumerate(PLAN)}

        def at(name):
            if name not in marks:
                unknown.add(name)
                return 0
            return marks[name][1]

        state = {"bank": 0, "last": [None] * 8, "w": 0}

        pe = Steps(nc.tensor, tensor_done, marks)
        act = Steps(nc.scalar, scalar_done, marks)
        dve = Steps(nc.vector, vector_done, marks)

        def open_bank(name):
            b = state["bank"] % 8
            state["bank"] += 1
            if state["last"][b]:
                reader, n = marks.get("read " + state["last"][b], (scalar_done, 0))
                pe.wait_ge(reader, n)
            state["last"][b] = name
            banks[name] = b
            return PS[b]

        def full(e, name):
            e.wait_ge(tensor_done, at(name))
            return PS[banks.get(name, 0)]

        def weight(name):
            i = WAT[name]
            assert i == state["w"], (name, i, state["w"])
            pe.wait_ge(slot_loaded[i % RING], 16 * (i // RING + 1))
            state["w"] += 1
            return ring[:, i % RING, :]

        def mm(out_, lhsT, rhs, start, stop):
            return nc.tensor.matmul(out_, lhsT, rhs, start=start, stop=stop, skip_group_check=True)

        def weight_used(ins, name):
            ins.then_inc(tensor_done, pe.one())
            pe.mark("slot of " + name)

        def pe_feature_block(wname, label, tok=SEQ, kt=KT, tiles=4, act_of=None, m0=0, col=None, after=None):
            w = weight(wname)
            w = w[:, 0:kt * tiles * P].rearrange("p (k c) -> p k c", k=kt)
            per = 512 // tok
            act_of = act_of or (lambda k: HT[:, k, 0:tok])
            for m in range(tiles):
                if m % per == 0:
                    ps = open_bank(f"{label}.{(m0 + m) // per}")
                for k in range(kt):
                    last = mm(ps[:, (m % per) * tok:(m % per + 1) * tok], w[:, k, m * P:(m + 1) * P], act_of(k),
                              k == 0, k == kt - 1)
                if m == tiles - 1:
                    weight_used(last, wname)
                    pe.mark(f"{label}.{(m0 + m) // per}")
                elif m % per == per - 1:
                    last.then_inc(tensor_done, pe.one())
                    pe.mark(f"{label}.{(m0 + m) // per}")

        def pe_token_blocks(wnames, kts, label, lhs, tiles=2):
            pss = []
            k0 = 0
            total = sum(kts)
            for wname, kt in zip(wnames, kts):
                w = weight(wname)[:, 0:kt * 512].rearrange("p (k c) -> p k c", k=kt)
                for t in range(tiles):
                    if k0 == 0:
                        pss.append(open_bank(f"{label}.{t}"))
                    for k in range(kt):
                        last = mm(pss[t][:, :], lhs(k0 + k, t), w[:, k, :], k0 + k == 0, k0 + k == total - 1)
                    if t == tiles - 1:
                        weight_used(last, wname)
                    elif k0 + kt == total:
                        last.then_inc(tensor_done, pe.one())
                    if k0 + kt == total:
                        pe.mark(f"{label}.{t}")
                k0 += kt

        def ht(k, t):
            return HT[:, k, t * P:(t + 1) * P]

        def pe_turn(label, srcs):
            ps = open_bank(label)
            for i, s in enumerate(srcs):
                last = nc.tensor.transpose(ps[:, i * P:(i + 1) * P], s, K("ident"))
            last.then_inc(tensor_done, pe.one())
            pe.mark(label)

        def copy_out(e, label, dst, src=None):
            ps = full(e, label)
            s = ps[:, :] if src is None else src(ps)
            if e is act:
                nc.scalar.activation(dst, s, ACT.Copy).then_inc(e.done, e.one())
            else:
                nc.vector.tensor_copy(dst, s).then_inc(e.done, e.one())
            e.mark("read " + label)

        def phase_end(e, name, me):
            if me != "pe":
                e.wait_ge(e.done, e.n)
            e.mark(f"{me} end {name}")

        tt = nc.vector.tensor_tensor
        ts = nc.vector.tensor_scalar
        stt = nc.vector.scalar_tensor_tensor
        activation = nc.scalar.activation

        SS = SM[:, 0:4]
        RS = SM[:, 4:8]

        def act_norm(label, tiles, junk):
            for t in tiles:
                act.wait_ge(vector_done, at(f"{label} x{t}"))
                activation(junk[:, t % 2, :], X[:, t, :], ACT.Square, accum_out=SS[:, t:t + 1]).then_inc(scalar_done, act.one())
                act.wait_ge(scalar_done, act.n)
                activation(RS[:, t:t + 1], SS[:, t:t + 1], ACT.Sqrt, bias=K("eps"), scale=1.0 / D).then_inc(scalar_done, act.one())
                act.mark(f"{label} rms{t}")

        def dve_norm(label, tiles, xn, scale, shift=None, finish=None):

            def turned(t):
                for h in range(2):
                    n = f"{label} turned {t}.{h}"
                    ps = full(dve, n)
                    dst = HT[:, 4 * h:4 * h + 4, t * P:(t + 1) * P]
                    tt(dst, ps[:, :].rearrange("p (k c) -> p k c", k=4), bc(scale(t)[:, 4 * h:4 * h + 4], [P, 4, P]),
                       ALU.mult).then_inc(vector_done, dve.one())
                    dve.mark("read " + n)
                    if shift:
                        dve.wait_ge(vector_done, dve.n)
                        tt(dst, dst, bc(shift(t)[:, 4 * h:4 * h + 4], [P, 4, P]), ALU.add).then_inc(vector_done, dve.one())
                dve.wait_ge(vector_done, dve.n)
                dve.mark(f"{label} ready {t}")

            n = len(tiles)
            for i in range(n + 2):
                if i < n:
                    t = tiles[i]
                    if finish:
                        finish(t)
                    dve.wait_ge(vector_done, dve.n)
                    dve.mark(f"{label} x{t}")
                if 1 <= i <= n:
                    t = tiles[i - 1]
                    dve.wait_ge(scalar_done, at(f"{label} rms{t}"))
                    nc.vector.reciprocal(RS[:, t:t + 1], RS[:, t:t + 1]).then_inc(vector_done, dve.one())
                    dve.wait_ge(vector_done, dve.n)
                    if i >= 3:
                        dve.wait_ge(tensor_done, at(f"{label} turned {tiles[i - 3]}.1"))
                    ts(xn[:, t % 2, :], X[:, t, :], RS[:, t:t + 1], None, ALU.mult).then_inc(vector_done, dve.one())
                    dve.wait_ge(vector_done, dve.n)
                    dve.mark(f"{label} xn {t}")
                if i >= 2:
                    turned(tiles[i - 2])

        def pe_norm(label, tiles, xn):
            for t in tiles:
                pe.wait_ge(vector_done, at(f"{label} xn {t}"))
                for h in range(2):
                    pe_turn(f"{label} turned {t}.{h}", [xn[:, t % 2, (4 * h + i) * P:(4 * h + i + 1) * P] for i in range(4)])
            pe.wait_ge(vector_done, at(f"{label} ready {tiles[-1]}"))

        def pe_turn_all(label, src, tiles, parts=8):
            for t in tiles:
                pe.wait_ge(vector_done, at(f"{label} src{t}"))
                for h in range(parts // 4):
                    pe_turn(f"{label} turned {t}.{h}", [src[:, t, (4 * h + i) * P:(4 * h + i + 1) * P] for i in range(4)])
            pe.wait_ge(scalar_done, at(label + " ready"))

        def act_turn_all(label, tiles):
            for t in tiles:
                for h in range(2):
                    n = f"{label} turned {t}.{h}"
                    ps = full(act, n)
                    activation(HT[:, 4 * h:4 * h + 4, t * P:(t + 1) * P], ps[:, :].rearrange("p (k c) -> p k c", k=4), ACT.Copy).then_inc(scalar_done, act.one())
                    act.mark("read " + n)
            act.wait_ge(scalar_done, act.n)
            act.mark(label + " ready")

        def dve_head_norm(label, src, sq, gains):
            dve.wait_ge(vector_done, dve.n)
            tt(sq, src, src, ALU.mult).then_inc(vector_done, dve.one())
            dve.wait_ge(vector_done, dve.n)
            dve.mark(label + " sq")
            dve.wait_ge(scalar_done, at(label + " root"))
            nc.vector.reciprocal(sq, sq).then_inc(vector_done, dve.one())
            dve.wait_ge(vector_done, dve.n)
            for a, b, g in gains:
                stt(src[:, a:b], src[:, a:b], g, sq[:, a:b], ALU.mult, ALU.mult).then_inc(vector_done, dve.one())
            dve.wait_ge(vector_done, dve.n)
            dve.mark(label + " normed")

        def pe_head_norm(label, sq, n, which="head_ones"):
            pe.wait_ge(vector_done, at(label + " sq"))
            for i in range(n):
                ps = open_bank(f"{label} ss{i}")
                mm(ps[:, :], K(which), sq[:, i * 512:(i + 1) * 512], True, True).then_inc(tensor_done, pe.one())
                pe.mark(f"{label} ss{i}")

        def act_head_norm(label, sq, n, scale, eps="eps"):
            for i in range(n):
                ps = full(act, f"{label} ss{i}")
                activation(sq[:, i * 512:(i + 1) * 512], ps[:, :], ACT.Sqrt, bias=K(eps), scale=scale).then_inc(scalar_done, act.one())
                act.mark(f"read {label} ss{i}")
            act.wait_ge(scalar_done, act.n)
            act.mark(label + " root")

        def pe_solve(label, groups, XI, XT, tmp, meanwhile):
            for k in range(6):
                pe_ada(meanwhile + k, 0)
                for g in range(groups):
                    lab = f"{label} {k}.{g}"
                    pe.wait_ge(vector_done, at(lab + " masked"))
                    pe.wait_ge(vector_done, at(f"{label} {k}.{g} X"))
                    ps = open_bank(lab + " LX")
                    for i in range(4):
                        last = mm(ps[:, i * P:(i + 1) * P], tmp[:, g % 2, i, :], XI[:, 4 * g + i, :], True, True)
                    last.then_inc(tensor_done, pe.one())
                    pe.mark(lab + " LX")
                pe_ada(meanwhile + k, 1)
                for g in range(groups):
                    lab = f"{label} {k}.{g}"
                    pe.wait_ge(scalar_done, at(lab + " LX out"))
                    ps = open_bank(lab + " XLX")
                    for i in range(4):
                        last = mm(ps[:, i * P:(i + 1) * P], XT[:, 4 * g + i, :], tmp[:, 2 + g, i, :], True, True)
                    last.then_inc(tensor_done, pe.one())
                    pe.mark(lab + " XLX")
                    ps = open_bank(lab + " XLXt")
                    for i in range(4):
                        last = mm(ps[:, i * P:(i + 1) * P], tmp[:, 2 + g, i, :], XT[:, 4 * g + i, :], True, True)
                    last.then_inc(tensor_done, pe.one())
                    pe.mark(lab + " XLXt")

        def act_solve(label, groups, tmp, meanwhile):
            for k in range(6):
                if meanwhile + k > 0:
                    act_ada_columns(meanwhile + k - 1)
                for g in range(groups):
                    lab = f"{label} {k}.{g} LX"
                    ps = full(act, lab)
                    activation(tmp[:, 2 + g, :, :], k4(ps[:, :]), ACT.Copy).then_inc(scalar_done, act.one())
                    act.mark("read " + lab, lab + " out")
                act_ada(meanwhile + k)

        def dve_solve(label, groups, LT, XI, XT, tmp):
            for i in range(4 * groups):
                nc.vector.tensor_copy(XI[:, i, :], K("ident")).then_inc(vector_done, dve.one())
                nc.vector.tensor_copy(XT[:, i, :], K("ident")).then_inc(vector_done, dve.one())
            dve.wait_ge(vector_done, dve.n)
            dve.mark(*[f"{label} 0.{g} X" for g in range(groups)])

            def masked(i):
                k, g = divmod(i, groups)
                if i >= 2:
                    kk, gg = divmod(i - 2, groups)
                    dve.wait_ge(tensor_done, at(f"{label} {kk}.{gg} LX"))
                tt(tmp[:, g % 2, :, :], LT[:, 4 * g:4 * g + 4, :], rows(K(f"pair{k}"), 4), ALU.mult).then_inc(vector_done, dve.one())
                dve.mark(f"{label} {k}.{g} masked")

            masked(0)
            masked(1)
            for k in range(6):
                for i in range(groups * k + 2, min(groups * (k + 1) + 2, 6 * groups)):
                    masked(i)
                for g in range(groups):
                    lab = f"{label} {k}.{g}"
                    dve.wait_ge(tensor_done, at(lab + " XLXt"))
                    for M, n in ((XI, lab + " XLX"), (XT, lab + " XLXt")):
                        ps = full(dve, n)
                        tt(M[:, 4 * g:4 * g + 4, :], M[:, 4 * g:4 * g + 4, :],
                              ps[:, :].rearrange("p (k c) -> p k c", k=4), ALU.add).then_inc(vector_done, dve.one())
                        dve.mark("read " + n)
                    dve.mark(f"{label} {k + 1}.{g} X")
            dve.wait_ge(vector_done, dve.n)
            dve.mark(label + " solved")

        def unit_buffers(ar, dv=P):
            return {"P": ar.take(2, 512), "PT": ar.take(2, 512), "st": ar.take(2, 4)}

        def pe_attention(label, units, B):
            n = len(units)
            for i in range(n + 2):
                if i < n:
                    u = units[i]
                    ps = open_bank(f"{label} s{i}")
                    calls = [(ps[:, a:b], u["q"], k) for a, b, k in u["k"]] + [(ps[:, a:b], l, r) for a, b, l, r in u.get("bias", [])]
                    nb = len(calls)
                    for j, (o, l, r) in enumerate(calls):
                        first = j < len(u["k"])
                        last = mm(o, l, r, first, (not first) or not u.get("bias"))
                    last.then_inc(tensor_done, pe.one())
                    pe.mark(f"{label} s{i}")
                if 1 <= i <= n:
                    j = i - 1
                    pe.wait_ge(scalar_done, at(f"{label} p{j}"))
                    ps = open_bank(f"{label} pt{j}")
                    for a in range(0, units[j]["nk"], P):
                        last = nc.tensor.transpose(ps[:, a:a + P], B["P"][:, j % 2, a:a + P], K("ident"))
                    last.then_inc(tensor_done, pe.one())
                    pe.mark(f"{label} pt{j}")
                if i >= 2:
                    j = i - 2
                    u = units[j]
                    pe.wait_ge(vector_done, at(f"{label} pt out{j}"))
                    ps = open_bank(f"{label} o{j}")
                    nk = len(u["v"])
                    for a, v in enumerate(u["v"]):
                        last = mm(ps[:, 0:u["dv"]], B["PT"][:, j % 2, a * P:(a + 1) * P], v, a == 0, a == nk - 1)
                    last.then_inc(tensor_done, pe.one())
                    pe.mark(f"{label} o{j}")

        def act_attention(label, units, B):
            for i, u in enumerate(units):
                act.wait_ge(tensor_done, at(f"{label} s{i}"))
                act.wait_ge(vector_done, at(f"{label} max{i}"))
                if i >= 2:
                    act.wait_ge(tensor_done, at(f"{label} pt{i - 2}"))
                    act.wait_ge(vector_done, at(f"{label} inv{i - 2}"))
                ps = PS[banks.get(f"{label} s{i}", 0)]
                activation(B["P"][:, i % 2, 0:u["nk"]], ps[:, 0:u["nk"]], ACT.Exp, bias=B["st"][:, i % 2, 0:1],
                       accum_out=B["st"][:, i % 2, 1:2]).then_inc(scalar_done, act.one())
                act.wait_ge(scalar_done, act.n)
                act.mark(f"read {label} s{i}", f"{label} p{i}")

        def dve_attention(label, units, B):
            n = len(units)
            for i in range(n + 2):
                if i < n:
                    u = units[i]
                    ps = full(dve, f"{label} s{i}")
                    if i >= 2:
                        dve.wait_ge(scalar_done, at(f"{label} p{i - 2}"))
                    dve.wait_ge(vector_done, dve.n)
                    nc.vector.tensor_reduce(B["st"][:, i % 2, 0:1], ps[:, 0:u["nk"]], AX.X, ALU.max, negate=True).then_inc(vector_done, dve.one())
                    dve.wait_ge(vector_done, dve.n)
                    dve.mark(f"{label} max{i}")
                if 1 <= i <= n:
                    j = i - 1
                    if j >= 2:
                        dve.wait_ge(tensor_done, at(f"{label} o{j - 2}"))
                    copy_out(dve, f"{label} pt{j}", B["PT"][:, j % 2, 0:units[j]["nk"]], lambda p: p[:, 0:units[j]["nk"]])
                    dve.mark(f"{label} pt out{j}")
                    dve.wait_ge(vector_done, dve.n)
                    nc.vector.reciprocal(B["st"][:, j % 2, 2:3], B["st"][:, j % 2, 1:2]).then_inc(vector_done, dve.one())
                    dve.wait_ge(vector_done, dve.n)
                    dve.mark(f"{label} inv{j}")
                if i >= 2:
                    j = i - 2
                    u = units[j]
                    ps = full(dve, f"{label} o{j}")
                    ts(u["o"], ps[:, 0:u["dv"]], B["st"][:, j % 2, 2:3], None, ALU.mult).then_inc(vector_done, dve.one())
                    dve.mark(f"read {label} o{j}")
            dve.wait_ge(vector_done, dve.n)
            dve.mark(label + " done")

        def k4(ap):
            return ap.rearrange("p (k c) -> p k c", k=4)

        def flat(ap):
            return ap.rearrange("p a b -> p (a b)")

        ar = Arena()
        R1 = {}
        for n in ("R", "Kf", "Vf", "AV", "KK", "WI", "WN", "TMP"):
            R1[n] = ar.take(4, SEQ)
        R, KF, VF, AV, KK, WI, WN, TMP = (R1[n] for n in ("R", "Kf", "Vf", "AV", "KK", "WI", "WN", "TMP"))
        YA = ar.take(2, 512)
        GA = ar.take(2, 512)
        YB = ar.take(2, 512)
        base1 = ar.at
        VT, AT_, BT, KTM = (ar.take(2, 512) for _ in range(4))
        MRB, MRK = ar.take(16, P), ar.take(16, P)
        LT1, XI1, XT1 = ar.take(16, P), ar.take(16, P), ar.take(16, P)
        T1 = ar.take(6, 4 * P)
        T1v = T1.rearrange("p a (c d) -> p a c d", c=4)
        ar2 = Arena(base1)
        XN1 = ar2.take(2, D)
        DH = ar2.take(KT, SEQ)
        XW = [ar2.take(KT, SEQ) for _ in range(3)]
        ar2b = XW[0].rearrange("p a b -> p (a b)").rearrange("p (a b) -> p a b", a=2)
        LO = [ar2.take(SEQ) for _ in range(3)]
        LAK = XI1
        PU = T1[:, 0:2, :]
        APT = TMP
        AT_T = AT_
        SAs = LT1.rearrange("p a b -> p (a b)")[:, 0:512]
        ST = LT1.rearrange("p a b -> p (a b)")[:, 512:768]
        SQ1 = LT1.rearrange("p a b -> p (a b)")[:, 1024:2048].rearrange("p (a c) -> p a c", a=2)
        BON = SM[:, 16:32].rearrange("p (a b) -> p a b", a=2)
        LNG = XI1.rearrange("p a b -> p (a b)")[:, 0:512]
        LNB = XI1.rearrange("p a b -> p (a b)")[:, 512:1024]

        def slot8(t, hd):
            return t * 8 + (hd % 2) * 4 + hd // 2

        def pe_rwkv():
            for i, n in enumerate("rkv"):
                pe_feature_block(f"rkv{i}", f"raw {n}")
            w = weight("lora_in")[:, 0:2048].rearrange("p (k c) -> p k c", k=KT)
            for i, (a, b) in enumerate(((0, 64), (64, 128), (128, 256))):
                pe.wait_ge(vector_done, at(f"xw{i}"))
                ps = open_bank(f"lora{i}")
                for k in range(KT):
                    last = mm(ps[0:b - a, 0:SEQ], w[:, k, a:b], XW[i][:, k, :], k == 0, k == KT - 1)
                last.then_inc(tensor_done, pe.one())
                pe.mark(f"lora{i}")
            pe.mark("slot of lora_in")
            w = weight("lora_out")[:, 0:1536].rearrange("p (k c) -> p k c", k=3)
            for i in range(2):
                pe.wait_ge(scalar_done, at(f"lora out{i}"))
                for h in range(2):
                    ps = open_bank(f"lora up{i}.{h}")
                    for j in range(2):
                        m = 2 * h + j
                        last = mm(ps[:, j * SEQ:(j + 1) * SEQ], w[0:64, i, m * P:(m + 1) * P], LO[i][0:64, :], True, True)
                    last.then_inc(tensor_done, pe.one())
                    pe.mark(f"lora up{i}.{h}")
            pe.wait_ge(scalar_done, at("lora out2"))
            for t in range(2):
                ps = open_bank(f"gate a{t}")
                mm(ps[:, :], LO[2][:, t * P:(t + 1) * P], w[:, 2, :], True, True).then_inc(tensor_done, pe.one())
                pe.mark(f"gate a{t}")
            pe.mark("slot of lora_out")
            pe.wait_ge(vector_done, at("kk sq"))
            for h in range(2):
                ps = open_bank(f"kk ss{h}")
                mm(ps[:, :], K("head_ones"), flat(TMP)[:, h * 512:(h + 1) * 512], True, True).then_inc(tensor_done, pe.one())
                pe.mark(f"kk ss{h}")
            pe.wait_ge(vector_done, at("rkr"))
            ps = open_bank("bonus")
            for t in range(2):
                for g in range(4):
                    last = mm(ps[:, t * 8 + 2 * g:t * 8 + 2 * g + 2], TMP[:, g, t * P:(t + 1) * P], K("head_pick"), True, True)
            last.then_inc(tensor_done, pe.one())
            pe.mark("bonus")
            pe.wait_ge(vector_done, at("tilde"))
            for n, src in (("vt", VF), ("at", KK), ("bt", AV), ("kt", KF)):
                for t in range(2):
                    pe_turn(f"{n}{t}", [src[:, g, t * P:(t + 1) * P] for g in range(4)])
            for n, a, b in (("lt", AV, KK), ("lak", KF, KK), ("mrb", AV, R), ("mrk", KF, R)):
                for q in range(4):
                    ps = open_bank(f"{n}{q}")
                    for i in range(4):
                        t, g, r = q // 2, i, 64 * (q % 2)
                        last = mm(ps[:, i * P:(i + 1) * P], a[r:r + 64, g, t * P:(t + 1) * P],
                                  b[r:r + 64, g, t * P:(t + 1) * P], True, True)
                    last.then_inc(tensor_done, pe.one())
                    pe.mark(f"{n}{q}")
            pe.wait_ge(vector_done, at("lak ready"))
            pe.wait_ge(scalar_done, at("token-major"))
            for t in range(2):
                ps = open_bank(f"lv{t}")
                for hd in range(8):
                    last = mm(ps[:, hd * 64:hd * 64 + 64], LAK[:, slot8(t, hd), :], VT[:, t, hd * 64:hd * 64 + 64], True, True)
                last.then_inc(tensor_done, pe.one())
                pe.mark(f"lv{t}")
            pe.wait_ge(scalar_done, at("silu c"))
            pe_solve("rwkv", 4, XI1, XT1, T1v, 0)
            pe.wait_ge(vector_done, at("rwkv solved"))
            for t in range(2):
                ps = open_bank(f"u{t}")
                for hd in range(8):
                    last = mm(ps[:, hd * 64:hd * 64 + 64], XT1[:, slot8(t, hd), :], SQ1b[:, t, hd * 64:hd * 64 + 64], True, True)
                last.then_inc(tensor_done, pe.one())
                pe.mark(f"u{t}")
                ps = open_bank(f"apt{t}")
                for hd in range(8):
                    g, r = hd // 2, 64 * (hd % 2)
                    last = mm(ps[r:r + 64, g * P:(g + 1) * P], AT_[:, t, hd * 64:hd * 64 + 64], XT1[:, slot8(t, hd), :], True, True)
                last.then_inc(tensor_done, pe.one())
                pe.mark(f"apt{t}")
            for c in range(4):
                t, rb = c // 2, 64 * (c % 2)
                cols = slice(c * 64, c * 64 + 64)
                if c > 0:
                    pe.wait_ge(vector_done, at(f"state{c - 1}"))
                    pe.wait_ge(vector_done, at("apt ready"))
                    for half in range(2):
                        r = slice(64 * half, 64 * half + 64)
                        ps = open_bank(f"sa{c}.{half}")
                        for g in range(4):
                            for j, Q in enumerate((APT, R)):
                                last = mm(ps[rb:rb + 64, j * 256 + g * 64:j * 256 + g * 64 + 64], Q[r, g, cols],
                                          ST[r, g * 64:g * 64 + 64], True, True)
                        last.then_inc(tensor_done, pe.one())
                        pe.mark(f"sa{c}.{half}")
                pe_ada(6 + c, 0)
                pe.wait_ge(vector_done, at(f"sa out{c}"))
                ps = open_bank(f"y{c}")
                for hd in range(8):
                    o = ps[rb:rb + 64, hd * 64:hd * 64 + 64]
                    n = slot8(t, hd)
                    mm(o, MRB[rb:rb + 64, n, rb:rb + 64], SAs[rb:rb + 64, hd * 64:hd * 64 + 64], True, False)
                    last = mm(o, MRK[rb:rb + 64, n, rb:rb + 64], VT[rb:rb + 64, t, hd * 64:hd * 64 + 64], False, True)
                last.then_inc(tensor_done, pe.one())
                pe.mark(f"y{c}")
                if c < 3:
                    ps = open_bank(f"ds{c}")
                    for hd in range(8):
                        g, r = hd // 2, 64 * (hd % 2)
                        o = ps[r:r + 64, g * 64:g * 64 + 64]
                        mm(o, BT[rb:rb + 64, t, hd * 64:hd * 64 + 64], SAs[rb:rb + 64, hd * 64:hd * 64 + 64], True, False)
                        last = mm(o, KTM[rb:rb + 64, t, hd * 64:hd * 64 + 64], VT[rb:rb + 64, t, hd * 64:hd * 64 + 64], False, True)
                    last.then_inc(tensor_done, pe.one())
                    pe.mark(f"ds{c}")
                pe_ada(6 + c, 1)

        def act_rwkv():
            for n, dst in (("r", R), ("k", KF), ("v", VF)):
                for h in range(2):
                    copy_out(act, f"raw {n}.{h}", dst[:, 2 * h:2 * h + 2, :], lambda ps: ps[:, :].rearrange("p (a c) -> p a c", a=2))
                act.wait_ge(scalar_done, act.n)
                act.mark(f"raw {n} out")
            for i, f, m in ((0, ACT.Tanh, 64), (1, ACT.Copy, 64), (2, ACT.Sigmoid, P)):
                ps = full(act, f"lora{i}")
                activation(LO[i][0:m, :], ps[0:m, 0:SEQ], f).then_inc(scalar_done, act.one())
                act.wait_ge(scalar_done, act.n)
                act.mark(f"read lora{i}", f"lora out{i}")
            for i, dst, bias in ((0, TMP, "w0"), (1, AV, "a0")):
                for h in range(2):
                    ps = full(act, f"lora up{i}.{h}")
                    for j in range(2):
                        m = 2 * h + j
                        activation(dst[:, m, :], ps[:, j * SEQ:(j + 1) * SEQ], ACT.Sigmoid, bias=C(bias, m)).then_inc(scalar_done, act.one())
                    act.mark(f"read lora up{i}.{h}")
                act.wait_ge(scalar_done, act.n)
                act.mark(f"lora sig{i}")
            for t in range(2):
                copy_out(act, f"gate a{t}", GA[:, t, :])
            act.wait_ge(vector_done, at("cw"))
            activation(WI, WI, ACT.Exp).then_inc(scalar_done, act.one())
            activation(KK, KK, ACT.Exp).then_inc(scalar_done, act.one())
            activation(WN, WN, ACT.Exp).then_inc(scalar_done, act.one())
            act.wait_ge(scalar_done, act.n)
            act.mark("decays")
            act.wait_ge(vector_done, at("kk sq"))
            for h in range(2):
                ps = full(act, f"kk ss{h}")
                activation(flat(TMP)[:, h * 512:(h + 1) * 512], ps[:, :], ACT.Sqrt, bias=K("eps")).then_inc(scalar_done, act.one())
                act.wait_ge(scalar_done, act.n)
                act.mark(f"read kk ss{h}")
            act.mark("kk root")
            ps = full(act, "bonus")
            activation(SM[:, 16:32], ps[:, 0:16], ACT.Copy).then_inc(scalar_done, act.one())
            act.wait_ge(scalar_done, act.n)
            act.mark("read bonus")
            for n, dst in (("vt", VT), ("at", AT_), ("bt", BT), ("kt", KTM)):
                for t in range(2):
                    copy_out(act, f"{n}{t}", dst[:, t, :])
            act.wait_ge(scalar_done, act.n)
            act.mark("token-major")
            for t in range(2):
                copy_out(act, f"lv{t}", SQ1b[:, t, :])
            act.wait_ge(scalar_done, act.n)
            act.mark("lv out")
            act_solve("rwkv", 4, T1v, 0)
            for j in range(6, 10):
                act_ada_columns(j - 1)
                act_ada(j)
            act.wait_ge(vector_done, at("y var"))
            activation(SM[:, 48:64], SM[:, 32:48], ACT.Sqrt, bias=K("gn_eps"), scale=1.0 / 64).then_inc(scalar_done, act.one())
            act.wait_ge(scalar_done, act.n)
            act.mark("y root")

        def shift_mix(src, diff, n):
            tt(diff[:, :, 1:SEQ], src[:, :, 0:SEQ - 1], src[:, :, 1:SEQ], ALU.subtract).then_inc(vector_done, dve.one())
            ts(diff[:, :, 0:1], src[:, :, 0:1], -1.0, None, ALU.mult).then_inc(vector_done, dve.one())
            dve.wait_ge(vector_done, dve.n)

        def heads_of(ap, half):
            return ap.rearrange("p (g h c) -> p h g c", h=2, c=64)[:, half]

        def dve_rwkv():
            for i, (n, X_) in enumerate((("r", R), ("k", KF), ("v", VF))):
                dve.wait_ge(scalar_done, at(f"raw {n} out"))
                shift_mix(X_, TMP, 4)
                for g in range(4):
                    stt(X_[:, g, :], TMP[:, g, :], C("mu_proj", 4 * i + g), X_[:, g, :], ALU.mult, ALU.add).then_inc(vector_done, dve.one())
                dve.wait_ge(vector_done, dve.n)
            H2 = HT[:, :, 0:SEQ]
            shift_mix(H2, DH, 8)
            for i in range(3):
                for k in range(8):
                    stt(XW[i][:, k, :], DH[:, k, :], C("mu_lora", 8 * i + k), H2[:, k, :], ALU.mult, ALU.add).then_inc(vector_done, dve.one())
                dve.wait_ge(vector_done, dve.n)
                dve.mark(f"xw{i}")
            dve.wait_ge(scalar_done, at("lora sig0"))
            ts(TMP, TMP, -math.exp(-0.5), None, ALU.mult).then_inc(vector_done, dve.one())
            dve.wait_ge(vector_done, dve.n)
            for g in range(4):
                nc.vector.tensor_tensor_scan(WI[:, g, :], K("carry"), TMP[:, g, :], 0.0, ALU.mult, ALU.add).then_inc(vector_done, dve.one())
            dve.wait_ge(vector_done, dve.n)
            ts(WN, WI, -1.0, None, ALU.mult).then_inc(vector_done, dve.one())
            tt(KK, WI, TMP, ALU.subtract).then_inc(vector_done, dve.one())
            dve.wait_ge(vector_done, dve.n)
            dve.mark("cw")
            dve.wait_ge(scalar_done, at("decays"))
            for g in range(4):
                ts(VN1[:, g, :], KF[:, g, :], C("k_k", g), None, ALU.mult).then_inc(vector_done, dve.one())
            dve.wait_ge(vector_done, dve.n)
            tt(TMP, VN1, VN1, ALU.mult).then_inc(vector_done, dve.one())
            dve.wait_ge(vector_done, dve.n)
            dve.mark("kk sq")
            dve.wait_ge(scalar_done, at("kk root"))
            nc.vector.reciprocal(TMP, TMP).then_inc(vector_done, dve.one())
            dve.wait_ge(vector_done, dve.n)
            tt(VN1, VN1, TMP, ALU.mult).then_inc(vector_done, dve.one())
            dve.wait_ge(vector_done, dve.n)
            stt(KK, KK, -1.0, VN1, ALU.mult, ALU.mult).then_inc(vector_done, dve.one())
            dve.wait_ge(vector_done, dve.n)
            dve.wait_ge(scalar_done, at("lora sig1"))
            for g in range(4):
                ts(TMP[:, g, :], AV[:, g, :], 1.0, C("k_a", g), ALU.subtract, ALU.mult).then_inc(vector_done, dve.one())
            dve.wait_ge(vector_done, dve.n)
            stt(KF, TMP, 1.0, KF, ALU.add, ALU.mult).then_inc(vector_done, dve.one())
            dve.wait_ge(vector_done, dve.n)
            for g in range(4):
                stt(TMP[:, g, :], R[:, g, :], C("r_k", g), KF[:, g, :], ALU.mult, ALU.mult).then_inc(vector_done, dve.one())
            dve.wait_ge(vector_done, dve.n)
            dve.mark("rkr")
            tt(R, R, WI, ALU.mult).then_inc(vector_done, dve.one())
            tt(AV, AV, VN1, ALU.mult).then_inc(vector_done, dve.one())
            dve.wait_ge(vector_done, dve.n)
            tt(AV, AV, WN, ALU.mult).then_inc(vector_done, dve.one())
            tt(KF, KF, WN, ALU.mult).then_inc(vector_done, dve.one())
            dve.wait_ge(vector_done, dve.n)
            dve.mark("tilde")
            for n, dst, mask in (("lt", LT1, "before"), ("lak", LAK, "before"), ("mrb", MRB, "upto"), ("mrk", MRK, "upto")):
                for q in range(4):
                    ps = full(dve, f"{n}{q}")
                    tt(dst[:, 4 * q:4 * q + 4, :], ps[:, :].rearrange("p (k c) -> p k c", k=4), rows(K(mask), 4), ALU.mult).then_inc(vector_done, dve.one())
                    dve.mark(f"read {n}{q}")
                dve.wait_ge(vector_done, dve.n)
                dve.mark(f"{n} ready")
            dve.wait_ge(tensor_done, at("lv1"))
            dve_solve("rwkv", 4, LT1, XI1, XT1, T1v)
            dve.wait_ge(scalar_done, at("lv out"))
            dve.mark("rwkv solved")
            for t in range(2):
                copy_out(dve, f"u{t}", PU[:, t, :])
                copy_out(dve, f"apt{t}", APT[:, :, t * P:(t + 1) * P], lambda ps: ps[:, :].rearrange("p (k c) -> p k c", k=4))
            dve.wait_ge(vector_done, dve.n)
            dve.mark("apt ready")
            for c in range(4):
                t, rb = c // 2, 64 * (c % 2)
                r = slice(rb, rb + 64)
                if c == 0:
                    nc.vector.tensor_copy(SAs[r, :], PU[r, t, :]).then_inc(vector_done, dve.one())
                    dve.wait_ge(vector_done, dve.n)
                else:
                    for half in range(2):
                        ps = full(dve, f"sa{c}.{half}")
                        tt(heads_of(SAs[r, :], half), ps[r, 0:256].rearrange("p (g c) -> p g c", g=4),
                              heads_of(PU[r, t, :], half), ALU.add).then_inc(vector_done, dve.one())
                    dve.wait_ge(vector_done, dve.n)
                dve.mark(f"sa out{c}")
                if c < 3:
                    ps = full(dve, f"ds{c}")
                    wl = bc(WI[:, :, c * 64 + 63], [P, 4, 64])
                    S3 = ST.rearrange("p (g c) -> p g c", g=4)
                    p3 = ps[:, 0:256].rearrange("p (g c) -> p g c", g=4)
                    if c == 0:
                        tt(S3, p3, wl, ALU.mult).then_inc(vector_done, dve.one())
                        dve.wait_ge(vector_done, dve.n)
                    else:
                        tt(S3, S3, p3, ALU.add).then_inc(vector_done, dve.one())
                        dve.wait_ge(vector_done, dve.n)
                        tt(S3, S3, wl, ALU.mult).then_inc(vector_done, dve.one())
                        dve.wait_ge(vector_done, dve.n)
                    dve.mark(f"read ds{c}", f"state{c}")
                copy_out(dve, f"y{c}", YA[r, t, :], lambda ps: ps[r, :])
                dve.wait_ge(vector_done, dve.n)
                if c > 0:
                    for half in range(2):
                        ps = full(dve, f"sa{c}.{half}")
                        y_ = heads_of(YA[r, t, :], half)
                        tt(y_, y_, ps[r, 256:512].rearrange("p (g c) -> p g c", g=4), ALU.add).then_inc(vector_done, dve.one())
                        dve.mark(f"read sa{c}.{half}")
            dve.wait_ge(vector_done, dve.n)
            y = YA.rearrange("p t (h c) -> p (t h) c", h=8)
            sq = SQ1.rearrange("p t (h c) -> p (t h) c", h=8)
            nc.vector.tensor_reduce(SM[:, 32:48], y, AX.X, ALU.add).then_inc(vector_done, dve.one())
            dve.wait_ge(vector_done, dve.n)
            ts(SM[:, 32:48], SM[:, 32:48], 1.0 / 64, None, ALU.mult).then_inc(vector_done, dve.one())
            dve.wait_ge(vector_done, dve.n)
            tt(y, y, bc(SM[:, 32:48], [P, 16, 64]), ALU.subtract).then_inc(vector_done, dve.one())
            dve.wait_ge(vector_done, dve.n)
            tt(sq, y, y, ALU.mult).then_inc(vector_done, dve.one())
            dve.wait_ge(vector_done, dve.n)
            nc.vector.tensor_reduce(SM[:, 32:48], sq, AX.X, ALU.add).then_inc(vector_done, dve.one())
            dve.wait_ge(vector_done, dve.n)
            dve.mark("y var")
            dve.wait_ge(scalar_done, at("y root"))
            nc.vector.reciprocal(SM[:, 48:64], SM[:, 48:64]).then_inc(vector_done, dve.one())
            dve.wait_ge(vector_done, dve.n)
            tt(y, y, bc(SM[:, 48:64], [P, 16, 64]), ALU.mult).then_inc(vector_done, dve.one())
            dve.wait_ge(vector_done, dve.n)
            tt(sq, VT.rearrange("p t (h c) -> p (t h) c", h=8), bc(SM[:, 16:32], [P, 16, 64]), ALU.mult).then_inc(vector_done, dve.one())
            dve.wait_ge(vector_done, dve.n)
            dve.wait_ge(loaded["rwkv_rows"], at("rows 1b"))
            tt(YA, YA, rows(LNG, 2), ALU.mult).then_inc(vector_done, dve.one())
            dve.wait_ge(vector_done, dve.n)
            tt(YA, YA, rows(LNB, 2), ALU.add).then_inc(vector_done, dve.one())
            dve.wait_ge(vector_done, dve.n)
            tt(YA, YA, SQ1, ALU.add).then_inc(vector_done, dve.one())
            dve.wait_ge(vector_done, dve.n)
            tt(YA, YA, GA, ALU.mult).then_inc(vector_done, dve.one())
            dve.wait_ge(vector_done, dve.n)

        VN1 = YA.rearrange("p t c -> p (t c)").rearrange("p (g c) -> p g c", g=4)
        SQ1b = WN.rearrange("p g c -> p (g c)").rearrange("p (t c) -> p t c", t=2)

        ar = Arena()
        ar.at = 11 * 1024
        QR = ar.take(12, SEQ + 4)
        CV = ar.take(12, SEQ)
        YB_ = YB
        ar = Arena(0)
        GB = ar.take(2, 512)
        DT = ar.take(8, P)
        EG = ar.take(8, P)
        BB = ar.take(8, P)
        QK = ar.take(8, P)
        KTb, VTb, UB = ar.take(2, 512), ar.take(2, 512), ar.take(2, 512)
        assert ar.at <= 8 * 1024
        ar = Arena(11 * 1024 + 12 * (SEQ + 4) + 12 * SEQ)
        SQ2 = ar.take(8, SEQ)
        LT2, XI2, XT2 = ar.take(8, P), ar.take(8, P), ar.take(8, P)
        T2 = ar.take(4, 4 * P).rearrange("p a (c d) -> p a c d", c=4)
        QD, WT, KD, KBP = (ar.take(8, P) for _ in range(4))
        NG = ar.take(P)
        ar = Arena(11 * 1024)
        SB_, VNb = ar.take(4, P), ar.take(512)
        ALr, DTr = SM[:, 64:68], SM[:, 68:72]
        BETA, GTt, GC = SM[:, 72:80], SM[:, 80:88], SM[:, 88:96]
        BEG, KDS, ZZ, ZN = SM[:, 96:104], SM[:, 104:112], SM[:, 112:120], SM[:, 120:128]
        INV2 = SM[:, 128:136]

        def b3(ap):
            return ap.rearrange("p (t h) -> p t h", t=2)

        def pe_gdn():
            for i in range(3):
                pe_feature_block(f"bqkv{i}", "bq", m0=4 * i)
            pe_token_blocks(["bgate"], [KT], "gate b", ht)
            w = weight("bab")[:, 0:64].rearrange("p (k c) -> p k c", k=KT)
            ps = open_bank("ab")
            for t in range(2):
                for k in range(KT):
                    last = mm(ps[:, t * 8:t * 8 + 8], ht(k, t), w[:, k, :], k == 0, k == KT - 1)
            weight_used(last, "bab")
            pe.mark("ab")
            for j in (10, 11, 12, 13):
                pe_ada(j, 0)
                pe_ada(j, 1)
            pe_head_norm("bqk", SQ2f, 4, "ones")
            pe.wait_ge(vector_done, at("g"))
            ps = open_bank("gc")
            mm(ps[:, 0:8], K("upto"), GTt, True, True).then_inc(tensor_done, pe.one())
            pe.mark("gc")
            pe.wait_ge(vector_done, at("g wide"))
            for t in range(2):
                ps = open_bank(f"gcb{t}")
                for h in range(4):
                    last = mm(ps[:, h * P:(h + 1) * P], GW[:, t * 4 + h, :], K("upto"), True, True)
                last.then_inc(tensor_done, pe.one())
                pe.mark(f"gcb{t}")
                ps = open_bank(f"betab{t}")
                for h in range(4):
                    last = mm(ps[:, h * P:(h + 1) * P], BW[:, t * 4 + h, :], K("ident"), True, True)
                last.then_inc(tensor_done, pe.one())
                pe.mark(f"betab{t}")
            pe.wait_ge(vector_done, at("bqk normed"))
            for n, o in (("kb", 4), ("vb", 8)):
                for t in range(2):
                    pe_turn(f"{n}{t}", [CV[:, o + h, t * P:(t + 1) * P] for h in range(4)])
            for t in range(2):
                tk = slice(t * P, (t + 1) * P)
                for n, o in (("kkb", 4), ("qkb", 0)):
                    ps = open_bank(f"{n}{t}")
                    for h in range(4):
                        last = mm(ps[:, h * P:(h + 1) * P], CV[:, 4 + h, tk], CV[:, o + h, tk], True, True)
                    last.then_inc(tensor_done, pe.one())
                    pe.mark(f"{n}{t}")
            pe_solve("gdn", 2, XI2, XT2, T2, 14)
            pe.wait_ge(vector_done, at("gdn solved"))
            for t in range(2):
                ps = open_bank(f"ub{t}")
                for h in range(4):
                    last = mm(ps[:, h * P:(h + 1) * P], XT2[:, t * 4 + h, :], VTb[:, t, h * P:(h + 1) * P], True, True)
                last.then_inc(tensor_done, pe.one())
                pe.mark(f"ub{t}")
                ps = open_bank(f"wb{t}")
                for h in range(4):
                    last = mm(ps[:, h * P:(h + 1) * P], KBP[:, t * 4 + h, :], XT2[:, t * 4 + h, :], True, True)
                last.then_inc(tensor_done, pe.one())
                pe.mark(f"wb{t}")
            for c in range(4):
                t, rb = c // 2, 64 * (c % 2)
                r = slice(rb, rb + 64)
                if c > 0:
                    pe.wait_ge(vector_done, at(f"bstate{c - 1}"))
                    pe.wait_ge(vector_done, at("u ready"))
                    ps = open_bank(f"vn{c}")
                    for h in range(4):
                        last = mm(ps[r, h * P:(h + 1) * P], WT[:, t * 4 + h, r], SB_[:, h, :], True, True)
                    last.then_inc(tensor_done, pe.one())
                    pe.mark(f"vn{c}")
                pe_ada(20 + c, 0)
                pe.wait_ge(vector_done, at(f"vn out{c}"))
                ps = open_bank(f"ob{c}")
                for h in range(4):
                    o = ps[r, h * P:(h + 1) * P]
                    if c > 0:
                        mm(o, QD[:, t * 4 + h, r], SB_[:, h, :], True, False)
                    last = mm(o, QK[r, t * 4 + h, r], VNb[r, h * P:(h + 1) * P], c == 0, True)
                last.then_inc(tensor_done, pe.one())
                pe.mark(f"ob{c}")
                if c < 3:
                    ps = open_bank(f"dsb{c}")
                    for h in range(4):
                        last = mm(ps[:, h * P:(h + 1) * P], KD[r, t * 4 + h, :], VNb[r, h * P:(h + 1) * P], True, True)
                    last.then_inc(tensor_done, pe.one())
                    pe.mark(f"dsb{c}")
                pe_ada(20 + c, 1)
            pe_ada_turn(23)

        def act_gdn():
            act.wait_ge(vector_done, at("dve end rwkv"))
            for j in range(6):
                copy_out(act, f"bq.{j}", QR[:, 2 * j:2 * j + 2, 3:3 + SEQ], lambda ps: ps[:, :].rearrange("p (a c) -> p a c", a=2))
            act.wait_ge(scalar_done, act.n)
            act.mark("bq out")
            for t in range(2):
                ps = full(act, f"gate b.{t}")
                activation(GB[:, t, :], ps[:, :], ACT.Silu).then_inc(scalar_done, act.one())
                act.mark(f"read gate b.{t}")
            ps = full(act, "ab")
            p3 = ps[:, 0:16].rearrange("p (t c) -> p t c", t=2)
            activation(b3(BETA), p3[:, :, 0:4], ACT.Sigmoid).then_inc(scalar_done, act.one())
            activation(b3(ZZ), p3[:, :, 4:8], ACT.Copy).then_inc(scalar_done, act.one())
            act.wait_ge(scalar_done, act.n)
            act.mark("read ab", "ab out")
            for j in (10, 11, 12, 13):
                act_ada_columns(j - 1)
                act_ada(j)
            act.wait_ge(vector_done, at("conv"))
            activation(CV, CV, ACT.Silu).then_inc(scalar_done, act.one())
            act.wait_ge(scalar_done, act.n)
            act.mark("conv silu")
            act_head_norm("bqk", SQ2f, 4, 1.0)
            act.wait_ge(vector_done, at("z"))
            activation(ALr, ALr, ACT.Exp).then_inc(scalar_done, act.one())
            activation(ZN, ZN, ACT.Exp).then_inc(scalar_done, act.one())
            act.wait_ge(scalar_done, act.n)
            activation(ZN, ZN, ACT.Ln, bias=K("one")).then_inc(scalar_done, act.one())
            act.wait_ge(scalar_done, act.n)
            act.mark("softplus")
            act.wait_ge(vector_done, at("gcb in"))
            activation(DT, DT, ACT.Exp).then_inc(scalar_done, act.one())
            activation(EG, EG, ACT.Exp).then_inc(scalar_done, act.one())
            act.wait_ge(scalar_done, act.n)
            activation(BEG, GC, ACT.Exp).then_inc(scalar_done, act.one())
            act.wait_ge(scalar_done, act.n)
            act.mark("gcb exp")
            act_solve("gdn", 2, T2, 14)
            for j in range(20, 24):
                act_ada_columns(j - 1)
                act_ada(j)
            act_ada_columns(23)
            act.wait_ge(vector_done, at("ob sq"))
            activation(INV2, INV2, ACT.Sqrt, bias=K("eps"), scale=1.0 / P).then_inc(scalar_done, act.one())
            act.wait_ge(scalar_done, act.n)
            act.mark("ob root")

        def dve_gdn():
            dve.wait_ge(tensor_done, at("pe end rwkv"))
            dve.wait_ge(scalar_done, at("act end rwkv"))
            nc.vector.memset(QR[:, :, 0:3], 0.0).then_inc(vector_done, dve.one())
            dve.wait_ge(vector_done, dve.n)
            dve.wait_ge(scalar_done, at("bq out"))
            for m in range(12):
                ts(CV[:, m, :], QR[:, m, 3:3 + SEQ], C("conv", 36 + m), None, ALU.mult).then_inc(vector_done, dve.one())
            dve.wait_ge(vector_done, dve.n)
            for i in (2, 1, 0):
                for m in range(12):
                    stt(CV[:, m, :], QR[:, m, i:i + SEQ], C("conv", 12 * i + m), CV[:, m, :], ALU.mult, ALU.add).then_inc(vector_done, dve.one())
                dve.wait_ge(vector_done, dve.n)
            dve.mark("conv")
            dve.wait_ge(scalar_done, at("ab out"))
            dve.wait_ge(loaded["start"], at("rows 1c"))
            tt(b3(ZZ), b3(ZZ), rows(DTr, 2), ALU.add).then_inc(vector_done, dve.one())
            dve.wait_ge(vector_done, dve.n)
            stt(ZN, ZZ, -1.0, ZZ, ALU.mult, ALU.min).then_inc(vector_done, dve.one())
            dve.wait_ge(vector_done, dve.n)
            dve.mark("z")
            dve.wait_ge(scalar_done, at("conv silu"))
            dve_head_norm("bqk", CV[:, 0:8, :].rearrange("p a b -> p (a b)"), SQ2f,
                          [(0, 1024, P ** -0.5), (1024, 2048, 1.0)])
            dve.wait_ge(scalar_done, at("softplus"))
            stt(ZZ, ZZ, 0.0, ZN, ALU.max, ALU.add).then_inc(vector_done, dve.one())
            dve.wait_ge(vector_done, dve.n)
            stt(b3(GTt), b3(ZZ), -1.0, rows(ALr, 2), ALU.mult, ALU.mult).then_inc(vector_done, dve.one())
            dve.wait_ge(vector_done, dve.n)
            dve.mark("g")
            nc.vector.tensor_copy(GW, bc(GTt, [P, 8, P])).then_inc(vector_done, dve.one())
            dve.wait_ge(vector_done, dve.n)
            nc.vector.tensor_copy(BW, bc(BETA, [P, 8, P])).then_inc(vector_done, dve.one())
            dve.wait_ge(vector_done, dve.n)
            dve.mark("g wide")
            copy_out(dve, "gc", GC, lambda ps: ps[:, 0:8])
            dve.wait_ge(vector_done, dve.n)
            for t in range(2):
                ps = full(dve, f"gcb{t}")
                nc.vector.tensor_copy(EG[:, 4 * t:4 * t + 4, :], k4(ps[:, :])).then_inc(vector_done, dve.one())
                for h in range(4):
                    ts(DT[:, 4 * t + h, :], ps[:, h * P:(h + 1) * P], GC[:, 4 * t + h:4 * t + h + 1], 0.0,
                          ALU.subtract, ALU.min).then_inc(vector_done, dve.one())
                dve.mark(f"read gcb{t}")
                copy_out(dve, f"betab{t}", BB[:, 4 * t:4 * t + 4, :], lambda ps: k4(ps[:, :]))
            dve.wait_ge(vector_done, dve.n)
            dve.mark("gcb in")
            for t in range(2):
                copy_out(dve, f"kb{t}", KTb[:, t, :])
            for t in range(2):
                copy_out(dve, f"vb{t}", VTb[:, t, :])
            dve.wait_ge(vector_done, dve.n)
            dve.wait_ge(scalar_done, at("gcb exp"))
            tt(DT, DT, rows(K("upto"), 8), ALU.mult).then_inc(vector_done, dve.one())
            dve.wait_ge(vector_done, dve.n)
            for t in range(2):
                s4 = slice(4 * t, 4 * t + 4)
                ps = full(dve, f"kkb{t}")
                stt(LT2[:, s4, :].rearrange("p a b -> p (a b)"), ps[:, :], -1.0, DT[:, s4, :].rearrange("p a b -> p (a b)"), ALU.mult, ALU.mult).then_inc(vector_done, dve.one())
                dve.wait_ge(vector_done, dve.n)
                dve.mark(f"read kkb{t}")
                ps = full(dve, f"qkb{t}")
                tt(QK[:, s4, :], k4(ps[:, :]), DT[:, s4, :], ALU.mult).then_inc(vector_done, dve.one())
                dve.mark(f"read qkb{t}")
            tt(LT2, LT2, rows(K("before"), 8), ALU.mult).then_inc(vector_done, dve.one())
            dve.wait_ge(vector_done, dve.n)
            tt(LT2, LT2, BB, ALU.mult).then_inc(vector_done, dve.one())
            dve.wait_ge(vector_done, dve.n)
            dve_solve("gdn", 2, LT2, XI2, XT2, T2)
            tt(BEG, BEG, BETA, ALU.mult).then_inc(vector_done, dve.one())
            dve.wait_ge(vector_done, dve.n)
            nc.vector.tensor_copy(KDS[0:64, :], DT[0:64, :, 63]).then_inc(vector_done, dve.one())
            nc.vector.tensor_copy(KDS[64:P, :], DT[64:P, :, P - 1]).then_inc(vector_done, dve.one())
            dve.wait_ge(vector_done, dve.n)
            k8 = KTb.rearrange("p t (h c) -> p (t h) c", h=4)
            v8 = VTb.rearrange("p t (h c) -> p (t h) c", h=4)
            tt(v8, v8, bc(BETA, [P, 8, P]), ALU.mult).then_inc(vector_done, dve.one())
            tt(KBP, k8, bc(BEG, [P, 8, P]), ALU.mult).then_inc(vector_done, dve.one())
            tt(KD, k8, bc(KDS, [P, 8, P]), ALU.mult).then_inc(vector_done, dve.one())
            for t in range(2):
                tt(QD[:, 4 * t:4 * t + 4, :], CV[:, 0:4, t * P:(t + 1) * P], EG[:, 4 * t:4 * t + 4, :], ALU.mult).then_inc(vector_done, dve.one())
            dve.wait_ge(vector_done, dve.n)
            dve.mark("gdn solved")
            for t in range(2):
                copy_out(dve, f"ub{t}", UB[:, t, :])
                copy_out(dve, f"wb{t}", WT[:, 4 * t:4 * t + 4, :], lambda ps: k4(ps[:, :]))
            dve.wait_ge(vector_done, dve.n)
            dve.mark("u ready")
            for c in range(4):
                t, rb = c // 2, 64 * (c % 2)
                r = slice(rb, rb + 64)
                if c == 0:
                    nc.vector.tensor_copy(VNb[r, :], UB[r, t, :]).then_inc(vector_done, dve.one())
                    dve.wait_ge(vector_done, dve.n)
                else:
                    ps = full(dve, f"vn{c}")
                    tt(VNb[r, :], UB[r, t, :], ps[r, :], ALU.subtract).then_inc(vector_done, dve.one())
                    dve.wait_ge(vector_done, dve.n)
                    dve.mark(f"read vn{c}")
                dve.mark(f"vn out{c}")
                if c < 3:
                    ps = full(dve, f"dsb{c}")
                    if c == 0:
                        nc.vector.tensor_copy(SB_, k4(ps[:, :])).then_inc(vector_done, dve.one())
                        dve.wait_ge(vector_done, dve.n)
                    else:
                        for h in range(4):
                            stt(SB_[:, h, :], SB_[:, h, :], EG[:, 4 * t + h, rb + 63:rb + 64], ps[:, h * P:(h + 1) * P],
                                   ALU.mult, ALU.add).then_inc(vector_done, dve.one())
                        dve.wait_ge(vector_done, dve.n)
                    dve.mark(f"read dsb{c}", f"bstate{c}")
                copy_out(dve, f"ob{c}", YB[r, t, :], lambda ps: ps[r, :])
            dve.wait_ge(vector_done, dve.n)
            y = YB.rearrange("p t (h c) -> p (t h) c", h=4)
            tt(QK, y, y, ALU.mult).then_inc(vector_done, dve.one())
            dve.wait_ge(vector_done, dve.n)
            nc.vector.tensor_reduce(INV2, QK, AX.X, ALU.add).then_inc(vector_done, dve.one())
            dve.wait_ge(vector_done, dve.n)
            dve.mark("ob sq")
            dve.wait_ge(scalar_done, at("ob root"))
            nc.vector.reciprocal(INV2, INV2).then_inc(vector_done, dve.one())
            dve.wait_ge(vector_done, dve.n)
            tt(y, y, bc(INV2, [P, 8, P]), ALU.mult).then_inc(vector_done, dve.one())
            dve.wait_ge(vector_done, dve.n)
            dve.wait_ge(loaded["gdn_rows"], at("norm b"))
            tt(y, y, rows(NG, 8), ALU.mult).then_inc(vector_done, dve.one())
            dve.wait_ge(vector_done, dve.n)
            tt(YB, YB, GB, ALU.mult).then_inc(vector_done, dve.one())
            dve.wait_ge(vector_done, dve.n)
            dve_scales()

        SQ2f = SQ2.rearrange("p a b -> p (a b)")
        GW = QD
        BW = WT

        def dve_add(label, h, tiles, gate=None):
            for t in tiles:
                ps = full(dve, f"{label}{h}.{t}")
                dst = X[:, t, h * 512:(h + 1) * 512]
                if gate is None:
                    tt(dst, dst, ps[:, :], ALU.add).then_inc(vector_done, dve.one())
                else:
                    tt(junk512, ps[:, :], gate(t)[:, h * 512:(h + 1) * 512], ALU.mult).then_inc(vector_done, dve.one())
                    dve.wait_ge(vector_done, dve.n)
                    tt(dst, dst, junk512, ALU.add).then_inc(vector_done, dve.one())
                    dve.wait_ge(vector_done, dve.n)
                dve.mark(f"read {label}{h}.{t}")

        def pe_start():
            pe.wait_ge(loaded["first"], at("first in"))

        def act_start():
            act.wait_ge(loaded["first"], at("first in"))
            activation(SC, C("c", 0, 16).rearrange("p (k s) -> p k s", s=2), ACT.Silu).then_inc(scalar_done, act.one())
            act.mark("silu c")

        def dve_start():
            dve.wait_ge(loaded["first"], at("first in"))
            for n in ("attn_q", "na_q", "da_q", "gqa_q"):
                ts(C(n), C(n), 0.125, None, ALU.mult).then_inc(vector_done, dve.one())

        def act_eout():
            act_turn_all("ymix", [0, 1])

        def dve_eout():
            dve.mark("ymix src")
            dve_add("eout", 0, [0, 1])

        def pe_eout():
            pe.wait_ge(vector_done, at("ymix src"))
            for t in range(2):
                for h, Y in enumerate((YA, YB)):
                    pe_turn(f"ymix turned {t}.{h}", [Y[:, t, i * P:(i + 1) * P] for i in range(4)])
            pe.wait_ge(scalar_done, at("ymix ready"))
            for h in range(2):
                pe_token_blocks([f"eout{h}"], [KT], f"eout{h}", ht)

        def mlp_places():
            ar = Arena()
            d = {"xn": ar.take(2, D), "H": ar.take(32, SEQ), "pT": ar.take(2, SEQ), "PP": ar.take(2, D),
                 "pg": ar.take(D), "sg": ar.take(2, 512), "junk": ar.take(2, D)}
            return d

        M = mlp_places()
        HH = M["H"]

        def pe_mlp(i):
            pe_norm(f"ffn{i}", [0, 1], M["xn"])
            for n in range(8):
                pe_feature_block(f"up{i}.{n}", f"up{i}", m0=4 * n)
            pe.wait_ge(vector_done, at(f"hidden{i}"))
            for h in range(2):
                pe_token_blocks([f"down{i}.{h}.{n}" for n in range(4)], [8] * 4, f"down{i}.{h}", lambda k, t: HH[:, k, t * P:(t + 1) * P])
            pe.wait_ge(loaded[f"ple{i}"], at(f"p{i}"))
            w = weight(f"pproj{i}")[:, 0:2048].rearrange("p (k c) -> p k c", k=2)
            for t in range(2):
                for h in range(2):
                    ps = open_bank(f"pproj{i}.{t}.{h}")
                    for k in range(2):
                        last = mm(ps[:, :], M["pT"][:, k, t * P:(t + 1) * P], w[:, k, h * 512:(h + 1) * 512], k == 0, k == 1)
                    last.then_inc(tensor_done, pe.one())
                    pe.mark(f"pproj{i}.{t}.{h}")
            pe.mark(f"slot of pproj{i}")
            pe_turn_all(f"xt{i}", X, [0, 1])
            for h in range(2):
                pe_token_blocks([f"pgate{i}.{h}"], [KT], f"pgate{i}.{h}", ht)

        def act_mlp(i):
            act_norm(f"ffn{i}", [0, 1], M["junk"])
            for j in range(16):
                copyf = f"up{i}.{j}"
                ps = full(act, copyf)
                activation(HH[:, 2 * j:2 * j + 2, :], ps[:, :].rearrange("p (a c) -> p a c", a=2), ACT.Relu).then_inc(scalar_done, act.one())
                act.wait_ge(scalar_done, act.n)
                act.mark("read " + copyf, f"relu{i}.{j}")
            act_turn_all(f"xt{i}", [0, 1])
            for t in range(2):
                for h in range(2):
                    copy_out(act, f"pproj{i}.{t}.{h}", M["PP"][:, t, h * 512:(h + 1) * 512])
            act.wait_ge(scalar_done, act.n)
            for t in range(2):
                activation(M["junk"][:, t, :], M["PP"][:, t, :], ACT.Square, accum_out=SS[:, t:t + 1]).then_inc(scalar_done, act.one())
                act.wait_ge(scalar_done, act.n)
            activation(RS[:, 0:2], SS[:, 0:2], ACT.Sqrt, bias=K("eps"), scale=1.0 / D).then_inc(scalar_done, act.one())
            act.wait_ge(scalar_done, act.n)
            act.mark(f"pproj root{i}")
            for h in range(2):
                for t in range(2):
                    n = f"pgate{i}.{h}.{t}"
                    ps = full(act, n)
                    if h == 1:
                        act.wait_ge(vector_done, at(f"sg used{i}.{t}"))
                    activation(M["sg"][:, t, :], ps[:, :], ACT.Sigmoid).then_inc(scalar_done, act.one())
                    act.wait_ge(scalar_done, act.n)
                    act.mark("read " + n, f"sg{i}.{h}.{t}")

        def dve_mlp(i):
            mixed = "aout" if i else "eout"
            dve_norm(f"ffn{i}", [0, 1], M["xn"], lambda t: C(f"ffn{i}", 0, 8), finish=lambda t: dve_add(mixed, 1, [t]))
            for j in range(16):
                dve.wait_ge(scalar_done, at(f"relu{i}.{j}"))
                c = HH[:, 2 * j:2 * j + 2, :]
                tt(c, c, c, ALU.mult).then_inc(vector_done, dve.one())
            dve.mark(f"hidden{i}")
            dve_add(f"down{i}.", 0, [0, 1])
            for t in range(2):
                dve_add(f"down{i}.", 1, [t])
                dve.wait_ge(vector_done, dve.n)
                dve.mark(f"xt{i} src{t}")
            dve.wait_ge(scalar_done, at(f"pproj root{i}"))
            dve.wait_ge(loaded[f"ple{i}"], at(f"rows ple{i}"))
            nc.vector.reciprocal(RS[:, 0:2], RS[:, 0:2]).then_inc(vector_done, dve.one())
            dve.wait_ge(vector_done, dve.n)
            for t in range(2):
                stt(M["PP"][:, t, :], M["PP"][:, t, :], RS[:, t:t + 1], M["pg"], ALU.mult, ALU.mult).then_inc(vector_done, dve.one())
            dve.wait_ge(vector_done, dve.n)
            for t in range(2):
                dve_embed(i, 0, t)

        def dve_embed(i, h, t):
            dve.wait_ge(scalar_done, at(f"sg{i}.{h}.{t}"))
            c = slice(h * 512, (h + 1) * 512)
            tt(M["sg"][:, t, :], M["sg"][:, t, :], M["PP"][:, t, c], ALU.mult).then_inc(vector_done, dve.one())
            dve.wait_ge(vector_done, dve.n)
            tt(X[:, t, c], X[:, t, c], M["sg"][:, t, :], ALU.add).then_inc(vector_done, dve.one())
            if h == 0:
                dve.mark(f"sg used{i}.{t}")

        ar = Arena()
        QB, KB, VB = ar.take(8, SEQ), ar.take(8, SEQ), ar.take(2, D)
        XN3 = ar.take(2, D)
        SQ3 = XN3.rearrange("p a b -> p (a b)")
        JK3 = ar.take(2, D)
        REL = ar.take(16, SEQ)
        OB_ = ar.take(2, D)
        BUF3 = unit_buffers(ar)
        units_b = []
        for hd in range(16):
            g, r = hd // 2, 64 * (hd % 2)
            for t in range(2):
                nk = P * (t + 1)
                u = {"q": QB[r:r + 64, g, t * P:(t + 1) * P], "k": [(0, nk, KB[r:r + 64, g, 0:nk])], "nk": nk, "dv": 64,
                     "v": [VB[:, a, hd * 64:hd * 64 + 64] for a in range(t + 1)], "o": OB_[:, t, hd * 64:hd * 64 + 64]}
                u["bias"] = [(a * P, (a + 1) * P, REL[:, hd, (t - a) * P:(t - a + 1) * P], K("flip")) for a in range(t + 1)]
                u["bias"].append((t * P, (t + 1) * P, K("late_query")[0:1, :], K("late_key")[0:1, :]))
                units_b.append(u)

        def pe_attn():
            pe_norm("mix1", [0, 1], XN3)
            for i in range(3):
                pe_feature_block(f"qkv{i}", "qk", m0=4 * i)
            pe_head_norm("q3", SQ3, 4)
            pe_feature_block("qkv3", "qk", m0=12)
            pe_token_blocks(["qkv4"], [KT], "v0", ht)
            pe_head_norm("k3", SQ3, 4)
            pe_token_blocks(["qkv5"], [KT], "v1", ht)
            pe.wait_ge(vector_done, at("k3 normed"))
            pe.wait_ge(scalar_done, at("v out"))
            pe.wait_ge(loaded["rel"], at("rel"))
            pe_attention("band", units_b, BUF3)
            pe_turn_all("ob", OB_, [0, 1])
            for h in range(2):
                pe_token_blocks([f"aout{h}"], [KT], f"aout{h}", ht)

        def act_attn():
            act_norm("mix1", [0, 1], JK3)
            def qk_out(j):
                dst = (QB if j < 4 else KB)[:, 2 * (j % 4):2 * (j % 4) + 2, :]
                copy_out(act, f"qk.{j}", dst, lambda ps: ps[:, :].rearrange("p (a c) -> p a c", a=2))

            for j in range(4):
                qk_out(j)
            act.wait_ge(scalar_done, act.n)
            act.mark("q out")
            for j in (4, 5):
                qk_out(j)
            act_head_norm("q3", SQ3, 4, 1.0 / 64)
            for j in (6, 7):
                qk_out(j)
            act.wait_ge(scalar_done, act.n)
            act.mark("k out")
            for t in range(2):
                copy_out(act, f"v0.{t}", VB[:, t, 0:512])
            act_head_norm("k3", SQ3, 4, 1.0 / 64)
            for t in range(2):
                copy_out(act, f"v1.{t}", VB[:, t, 512:1024])
            act.wait_ge(scalar_done, act.n)
            act.mark("v out")
            act_attention("band", units_b, BUF3)
            act_turn_all("ob", [0, 1])

        def dve_attn():
            dve_norm("mix1", [0, 1], XN3, lambda t: C("mix1", 0, 8), finish=lambda t: dve_embed(0, 1, t))
            dve.wait_ge(scalar_done, at("q out"))
            dve_head_norm("q3", QB.rearrange("p a b -> p (a b)"), SQ3, [(0, 2048, C("attn_q"))])
            dve.wait_ge(scalar_done, at("k out"))
            dve_head_norm("k3", KB.rearrange("p a b -> p (a b)"), SQ3, [(0, 2048, C("attn_k"))])
            dve_attention("band", units_b, BUF3)
            dve.mark("ob src0", "ob src1")
            dve_add("aout", 0, [0, 1])

        ar = Arena()
        GT_ = ar.take(2, 2, D)
        junk512 = ar.take(512)
        base2 = ar.at

        def ada_row(j):
            return HT[0:2, 2 * (j % 2):2 * (j % 2) + 2, SEQ:2 * SEQ]

        ada_bank = {}

        def pe_ada(j, half):
            i, n = divmod(j, 12)
            if half == 0:
                if j > 0:
                    pe_ada_turn(j - 1)
                ada_bank[j] = open_bank(f"ada{i}.{n}"), weight(f"ada{i}.{n}").rearrange("p (k c) -> p k c", k=KT)
            ps, w = ada_bank[j]
            for k in range(4 * half, 4 * half + 4):
                last = mm(ps[0:2, :], SC[:, k, :], w[:, k, :], k == 0, k == KT - 1)
            if half:
                weight_used(last, f"ada{i}.{n}")
                pe.mark(f"ada{i}.{n}")

        def pe_ada_turn(j):
            pe.wait_ge(scalar_done, at(f"ada row{j}"))
            ps = open_bank(f"ada turned{j}")
            for m in range(4):
                last = mm(ps[:, 2 * m:2 * m + 2], ada_row(j)[:, m // 2, (m % 2) * P:(m % 2 + 1) * P], K("ident")[0:2, 0:2], True, True)
            last.then_inc(tensor_done, pe.one())
            pe.mark(f"ada turned{j}")

        def act_ada(j):
            i, n = divmod(j, 12)
            ps = full(act, f"ada{i}.{n}")
            activation(ada_row(j), ps[0:2, :].rearrange("p (a c) -> p a c", a=2), ACT.Copy).then_inc(scalar_done, act.one())
            act.mark(f"read ada{i}.{n}", f"ada row{j}")

        def act_ada_columns(j):
            i, n = divmod(j, 12)
            ps = full(act, f"ada turned{j}")
            for m in range(4):
                activation(MOD[:, i, 4 * n + m, :], ps[:, 2 * m:2 * m + 2], ACT.Identity, bias=C(f"bada{i}", 4 * n + m))\
                    .then_inc(scalar_done, act.one())
            act.mark(f"read ada turned{j}", f"mod{i}.{n}")

        def pe_gate(i, s, j):
            pe.wait_ge(vector_done, at(f"diag{i}.{s}.{j}"))
            for h in range(2):
                ps = open_bank(f"gate{i}.{s}.{j}.{h}")
                mm(ps[:, :], K("ones"), DG[:, 4 * h:4 * h + 4, :], True, True).then_inc(tensor_done, pe.one())
                pe.mark(f"gate{i}.{s}.{j}.{h}")

        def act_gate(i, s, j):
            for h in range(2):
                copy_out(act, f"gate{i}.{s}.{j}.{h}", GT_[:, s, j, h * 512:(h + 1) * 512])
            act.mark(f"gate out{i}.{s}.{j}")

        def dve_gate(i, s, j, before=None):
            m = (2, 5)[j]
            if before:
                dve.wait_ge(tensor_done, at(f"gate{before}.1"))
            tt(DG, rows(K("ident"), 8), bc(MOD[:, i, 8 * m:8 * m + 8, s], [P, 8, P]), ALU.mult).then_inc(vector_done, dve.one())
            dve.wait_ge(vector_done, dve.n)
            dve.mark(f"diag{i}.{s}.{j}")

        def dve_scales():
            dve.wait_ge(scalar_done, at("mod1.11"))
            for i in range(2):
                for m in (1, 4):
                    c = MOD[:, i, 8 * m:8 * m + 8, :]
                    ts(c, c, 1.0, None, ALU.add).then_inc(vector_done, dve.one())
            dve.wait_ge(vector_done, dve.n)

        def mod_scale(i, w):
            return lambda t: MOD[:, i, 8 * (3 * w + 1):8 * (3 * w + 1) + 8, t // 2]

        def mod_shift(i, w):
            return lambda t: MOD[:, i, 8 * 3 * w:8 * 3 * w + 8, t // 2]

        def gate_row(w):
            return lambda t: GT_[:, t // 2, w, :]

        def ffn_places():
            ar = Arena(base2)
            return {"H": ar.take(22, 512), "xn": ar.take(2, D), "junk": ar.take(2, D), "raw": ar.take(2, 2, 260), "cv": ar.take(2, 512),
                    "g": ar.take(2, 512)}

        F = ffn_places()
        FH = F["H"]

        def pe_ffn(i, S):
            tiles = list(range(2 * S))
            pe_norm(f"cffn{i}", tiles, F["xn"])
            for n in range(11):
                w = weight(f"cup{i}.{n}").rearrange("p (k c) -> p k c", k=KT)
                for j in range(2):
                    for gv in range(2):
                        lab = f"{'gv'[gv]}up{i}.{2 * n + j}"
                        ps = open_bank(lab)
                        m = 2 * j + gv
                        for k in range(KT):
                            last = mm(ps[:, 0:S * SEQ], w[:, k, m * P:(m + 1) * P], HT[:, k, 0:S * SEQ], k == 0, k == KT - 1)
                        last.then_inc(tensor_done, pe.one())
                        pe.mark(lab)
                pe.mark(f"slot of cup{i}.{n}")
            pe.wait_ge(vector_done, at(f"chidden{i}"))
            for h in range(2):
                pe_token_blocks([f"cdown{i}.{h}.{n}" for n in range(3)], [8, 8, 6], f"cdown{i}.{h}",
                                lambda k, t: FH[:, k, t * P:(t + 1) * P], tiles=2 * S)

        def act_ffn(i, S):
            act_norm(f"cffn{i}", list(range(2 * S)), F["junk"] if i == 0 else Arena(base2).take(2, D))
            for m in range(22):
                b = m % 2
                ps = full(act, f"gup{i}.{m}")
                act.wait_ge(vector_done, at(f"raw ready{i}.{m}"))
                for s in range(S):
                    activation(F["raw"][:, b, s, 1:1 + SEQ], ps[:, s * SEQ:(s + 1) * SEQ], ACT.Copy).then_inc(scalar_done, act.one())
                act.wait_ge(scalar_done, act.n)
                act.mark(f"read gup{i}.{m}", f"raw{i}.{m}")
                act.wait_ge(vector_done, at(f"cv{i}.{m}"))
                if m >= 2:
                    act.wait_ge(vector_done, at(f"h{i}.{m - 2}"))
                activation(F["g"][:, b, 0:S * SEQ], F["cv"][:, b, 0:S * SEQ], ACT.Silu, bias=C(f"fconv_b{i}", m)).then_inc(scalar_done, act.one())
                act.wait_ge(scalar_done, act.n)
                act.mark(f"sg{i}.{m}")

        def dve_ffn(i, S):
            tiles = list(range(2 * S))
            mixed = "oout" if i else "wout"
            dve_norm(f"cffn{i}", tiles, F["xn"], mod_scale(i, 1), mod_shift(i, 1), finish=lambda t: dve_add(mixed, 1, [t], gate_row(0)))
            nc.vector.memset(F["raw"], 0.0).then_inc(vector_done, dve.one())
            dve.wait_ge(vector_done, dve.n)
            dve.mark(f"raw ready{i}.0", f"raw ready{i}.1")

            def conv(m):
                b = m % 2
                dve.wait_ge(scalar_done, at(f"raw{i}.{m}"))
                if m >= 2:
                    dve.wait_ge(scalar_done, at(f"sg{i}.{m - 2}"))
                c = F["cv"][:, b, 0:S * SEQ].rearrange("p (s c) -> p s c", s=S)
                raw = F["raw"][:, b, 0:S, :]
                ts(c, raw[:, :, 0:SEQ], C(f"fconv_w{i}", m), None, ALU.mult).then_inc(vector_done, dve.one())
                dve.wait_ge(vector_done, dve.n)
                stt(c, raw[:, :, 1:1 + SEQ], C(f"fconv_w{i}", 22 + m), c, ALU.mult, ALU.add).then_inc(vector_done, dve.one())
                dve.wait_ge(vector_done, dve.n)
                stt(c, raw[:, :, 2:2 + SEQ], C(f"fconv_w{i}", 44 + m), c, ALU.mult, ALU.add).then_inc(vector_done, dve.one())
                dve.wait_ge(vector_done, dve.n)
                dve.mark(f"cv{i}.{m}", f"raw ready{i}.{m + 2}")

            def gate(m):
                b = m % 2
                dve.wait_ge(scalar_done, at(f"sg{i}.{m}"))
                ps = full(dve, f"vup{i}.{m}")
                tt(FH[:, m, 0:S * SEQ], F["g"][:, b, 0:S * SEQ], ps[:, 0:S * SEQ], ALU.mult).then_inc(vector_done, dve.one())
                dve.wait_ge(vector_done, dve.n)
                dve.mark(f"read vup{i}.{m}", f"h{i}.{m}")

            for m in range(22):
                conv(m)
                gate(m)
            dve.mark(f"chidden{i}")
            dve_add(f"cdown{i}.", 0, tiles, gate_row(1))
            if i == 1:
                dve_add("cdown1.", 1, tiles, gate_row(1))

        ar = Arena(base2)
        RC = ar.take(2, SEQ)
        QN, KN, VN = ar.take(4, 512), ar.take(4, 512), ar.take(4, 512)
        QD5, KD5, VD5 = ar.take(4, 512), ar.take(4, 512), ar.take(4, 512)
        SQ5 = ar.take(4, 512)
        YN = ar.take(4, 512)
        BM = ar.take(2, 8, SEQ)
        NM = ar.take(SEQ)
        LAMR, SUBG = SM[:, 136:144], None
        ar = Arena(ar.at)
        SUBG = ar.take(P)
        XN5 = SQ5.rearrange("p a b -> p (a b)").rearrange("p (a b) -> p a b", a=2)
        JK5 = BM.rearrange("p a b c -> p (a b c)")[:, 0:2 * D].rearrange("p (a b) -> p a b", a=2)
        DG = arena[:, AR - 1024:AR].rearrange("p (a b) -> p a b", a=8)
        BUF5 = {"P": SQ5[:, 0:2, :], "PT": SQ5[:, 2:4, :], "st": SM[:, 144:152].rearrange("p (a b) -> p a b", a=2)}
        OD = HT.rearrange("p k c -> p (k c)").rearrange("p (t c) -> p t c", t=4)
        YD = BM.rearrange("p a b c -> p (a b c)")[:, 0:2048].rearrange("p (t c) -> p t c", t=4)

        def heads64(Q, g, r, a, b):
            return Q[r:r + 64, g, a:b]

        na_units, na_ctx, da_units, da_ctx = [], [], [], []
        for hd in range(8):
            g, r = hd // 2, 64 * (hd % 2)
            for t in range(4):
                q = QN[r:r + 64, g, t * P:(t + 1) * P]
                o = YN[:, t, hd * 64:hd * 64 + 64]
                lo = 0 if t < 2 else 2
                u = {"q": q, "k": [(0, 512 - lo * P, KN[r:r + 64, g, lo * P:512])], "nk": 512 - lo * P, "dv": 64, "o": o,
                     "v": [VN[:, a, hd * 64:hd * 64 + 64] for a in range(lo, 4)]}
                if t < 2:
                    u["bias"] = [(0, SEQ, K("flip64"), BM[:, t, hd, :])]
                na_units.append(u)
                da_units.append({"q": QD5[r:r + 64, g, t * P:(t + 1) * P], "k": [(0, 512 - lo * P, KD5[r:r + 64, g, lo * P:512])],
                                 "nk": 512 - lo * P, "dv": P, "o": OD[:, t, hd * P:(hd + 1) * P],
                                 "v": [VD5[:, a, g * P:(g + 1) * P] for a in range(lo, 4)]})

        def fl(ap):
            return ap.rearrange("p a b -> p (a b)")

        def pe_even():
            pe_norm("mod e", [0, 1, 2, 3], XN5)
            pe_feature_block("win0", "qn", tok=512)
            pe_gate(0, 0, 0)
            pe_feature_block("win1", "kn", tok=512)
            pe_head_norm("qn5", fl(SQ5), 4)
            pe_token_blocks(["win2"], [KT], "vn", ht, tiles=4)
            pe_gate(0, 0, 1)
            pe_head_norm("kn5", fl(SQ5), 4)
            pe_feature_block("win3", "qd", tok=512)
            pe_gate(0, 1, 0)
            pe_feature_block("win4", "kd", tok=512)
            pe_head_norm("qd5", fl(SQ5), 4)
            pe_token_blocks(["win5"], [KT], "vd", ht, tiles=4)
            pe_gate(0, 1, 1)
            pe_head_norm("kd5", fl(SQ5), 4)
            ps = open_bank("lam")
            pe.wait_ge(vector_done, at("lam in"))
            mm(ps[:, 0:2], K("ones"), LAMR[:, 0:2], True, True).then_inc(tensor_done, pe.one())
            pe.mark("lam")
            for n, Q in (("qd", QD5), ("kd", KD5)):
                pe.wait_ge(vector_done, at(f"{n}5 normed"))
                for g in range(4):
                    ps = open_bank(f"rot {n}{g}")
                    mm(ps[:, 0:SEQ], K("rotate_pairs"), Q[:, g, 0:SEQ], True, True).then_inc(tensor_done, pe.one())
                    pe.mark(f"rot {n}{g}")
            pe.wait_ge(vector_done, at("even heads"))
            pe.wait_ge(vector_done, at("bm ready"))
            pe_attention("na", na_units, BUF5)
            pe_attention("da", da_units, BUF5)
            for h, Y in enumerate((YN, YD)):
                for t in range(4):
                    if h == 1:
                        pe.wait_ge(vector_done, at(f"yd src{t}"))
                    pe_turn(f"yd turned {t}.{h}", [Y[:, t, i * P:(i + 1) * P] for i in range(4)])
            pe.wait_ge(scalar_done, at("yd ready"))
            for h in range(2):
                pe_token_blocks([f"wout{h}"], [KT], f"wout{h}", lambda k, t: (QN if k < 4 else KN)[:, k % 4, t * P:(t + 1) * P], tiles=4)

        def act_even():
            act_norm("mod e", [0, 1, 2, 3], JK5)
            for n, Q in (("qn", QN), ((0, 0), None), ("kn", KN), ("qn5", None), ("vn", VN), ((0, 1), None), ("kn5", None), ("qd", QD5),
                         ((1, 0), None), ("kd", KD5), ("qd5", None), ("vd", VD5), ((1, 1), None), ("kd5", None)):
                if Q is None and n in ((0, 0), (0, 1), (1, 0), (1, 1)):
                    act_gate(0, *n)
                    continue
                if Q is None:
                    act_head_norm(n, fl(SQ5), 4, 1.0 / 64)
                    continue
                for j in range(4):
                    copy_out(act, f"{n}.{j}", Q[:, j, :])
                act.wait_ge(scalar_done, act.n)
                act.mark(f"{n} out")
            ps = full(act, "lam")
            activation(LAMR[:, 2:4], ps[:, 0:2], ACT.Exp).then_inc(scalar_done, act.one())
            act.wait_ge(scalar_done, act.n)
            act.mark("read lam", "lam exp")
            act_attention("na", na_units, BUF5)
            act_attention("da", da_units, BUF5)
            for t in range(4):
                act.wait_ge(vector_done, at(f"subln ss{t}"))
                ss = SM[:, 152 + 4 * t:156 + 4 * t]
                activation(ss, ss, ACT.Sqrt, bias=K("eps"), scale=1.0 / P).then_inc(scalar_done, act.one())
                act.mark(f"subln root{t}")
            for h, Q in enumerate((QN, KN)):
                for t in range(4):
                    n = f"yd turned {t}.{h}"
                    ps = full(act, n)
                    activation(Q[:, :, t * P:(t + 1) * P], k4(ps[:, :]), ACT.Copy).then_inc(scalar_done, act.one())
                    act.mark("read " + n)
            act.wait_ge(scalar_done, act.n)
            act.mark("yd ready")

        def dve_rope(n, Q, tmp):
            for g in range(4):
                ps = full(dve, f"rot {n}{g}")
                tt(tmp[:, 0:SEQ], ps[:, 0:SEQ], RC[:, 1, :], ALU.mult).then_inc(vector_done, dve.one())
                dve.wait_ge(vector_done, dve.n)
                dve.mark(f"read rot {n}{g}")
                tt(Q[:, g, 0:SEQ], Q[:, g, 0:SEQ], RC[:, 0, :], ALU.mult).then_inc(vector_done, dve.one())
                dve.wait_ge(vector_done, dve.n)
                tt(Q[:, g, 0:SEQ], Q[:, g, 0:SEQ], tmp[:, 0:SEQ], ALU.add).then_inc(vector_done, dve.one())
                dve.wait_ge(vector_done, dve.n)

        def dve_even():
            dve_norm("mod e", [0, 1, 2, 3], XN5, mod_scale(0, 0), mod_shift(0, 0),
                     finish=lambda t: dve_embed(1, 1, t) if t < 2 else None)
            before = None
            for (n, Q), g in zip((("qn", QN), ("kn", KN), ("qd", QD5), ("kd", KD5)), ((0, 0), (0, 1), (1, 0), (1, 1))):
                dve_gate(0, *g, before)
                before = f"0.{g[0]}.{g[1]}"
                dve.wait_ge(scalar_done, at(f"{n} out"))
                col = C({"qn": "na_q", "kn": "na_k", "qd": "da_q", "kd": "da_k"}[n])
                dve_head_norm(n + "5", fl(Q), fl(SQ5), [(0, 2048, col)])
                if n == "kn":
                    tt(LAMR[:, 0:2], C("lam", 0, 2), C("lam", 2, 2), ALU.mult).then_inc(vector_done, dve.one())
                    dve.wait_ge(vector_done, dve.n)
                    dve.mark("lam in")
                    dve.wait_ge(loaded["even"], at("rope in"))
                    dve.wait_ge(loaded["bias"], at("bm loaded"))
                    tt(BM.rearrange("p a b c -> p (a b) c"), BM.rearrange("p a b c -> p (a b) c"), rows(NM, 16), ALU.add).then_inc(vector_done, dve.one())
                    dve.wait_ge(vector_done, dve.n)
                    dve.mark("bm ready")
            dve.wait_ge(loaded["even"], at("rope in"))
            dve_rope("qd", QD5, fl(SQ5))
            dve_rope("kd", KD5, fl(SQ5))
            dve.wait_ge(scalar_done, at("vd out"))
            dve.wait_ge(scalar_done, at("vn out"))
            dve.mark("even heads")
            dve_attention("na", na_units, BUF5)
            dve_attention("da", da_units, BUF5)
            dve.wait_ge(scalar_done, at("lam exp"))
            tt(LAMR[:, 4:5], LAMR[:, 3:4], LAMR[:, 2:3], ALU.subtract).then_inc(vector_done, dve.one())
            dve.wait_ge(vector_done, dve.n)
            ts(LAMR[:, 4:5], LAMR[:, 4:5], -(0.8 - 0.6), None, ALU.add).then_inc(vector_done, dve.one())
            dve.wait_ge(vector_done, dve.n)
            y, sq = YD.rearrange("p t (h c) -> p t h c", h=4), OD[:, 0:2, :].rearrange("p t (w h c) -> p (t w) h c", w=2, h=4)
            for t in range(4):
                o = OD[:, t, :].rearrange("p (h w c) -> p h w c", h=4, w=2)
                stt(y[:, t], o[:, :, 1, :], LAMR[:, 4:5], o[:, :, 0, :], ALU.mult, ALU.add).then_inc(vector_done, dve.one())
            dve.wait_ge(vector_done, dve.n)
            for t in range(4):
                tt(sq[:, t], y[:, t], y[:, t], ALU.mult).then_inc(vector_done, dve.one())
                dve.wait_ge(vector_done, dve.n)
                nc.vector.tensor_reduce(SM[:, 152 + 4 * t:156 + 4 * t], sq[:, t], AX.X, ALU.add).then_inc(vector_done, dve.one())
                dve.mark(f"subln ss{t}")
            for t in range(4):
                dve.wait_ge(scalar_done, at(f"subln root{t}"))
                ss = SM[:, 152 + 4 * t:156 + 4 * t]
                nc.vector.reciprocal(ss, ss).then_inc(vector_done, dve.one())
                dve.wait_ge(vector_done, dve.n)
                tt(y[:, t], y[:, t], bc(ss, [P, 4, P]), ALU.mult).then_inc(vector_done, dve.one())
                dve.wait_ge(vector_done, dve.n)
                stt(y[:, t], y[:, t], 1.0 - (0.8 - 0.6), rows(SUBG, 4), ALU.mult, ALU.mult).then_inc(vector_done, dve.one())
                dve.mark(f"yd src{t}")
            dve.wait_ge(scalar_done, at("gate out0.1.1"))
            dve_add("wout", 0, [0, 1, 2, 3], gate_row(0))

        ar = Arena(base2)
        QG, KG, VG = ar.take(4, SEQ), ar.take(512), ar.take(4, P)
        UR = ar.take(12, SEQ + 2)
        UC = ar.take(12, SEQ)
        ZT = ar.take(SEQ)
        DEC = ar.take(4, 512)
        DF = ar.take(2, 2 * SEQ + P)
        DI = ar.take(5, SEQ)
        RC7 = ar.take(2, SEQ)
        SQ7 = ar.take(1024)
        HS = ar.take(4, 512)
        JK7 = Arena(ar.at).take(2, D)
        YT7 = ar.take(4, SEQ)
        ZTM = ar.take(2, 512)
        HF = ar.take(SEQ)
        KF7 = ar.take(5, 512)
        XN7 = HS.rearrange("p a b -> p (a b)").rearrange("p (a b) -> p a b", a=2)
        ZF = HT.rearrange("p k c -> p (k c)")[:, 0:2560].rearrange("p (a c) -> p a c", a=5)
        TF = DEC.rearrange("p a b -> p (a b)")[:, 0:1024].rearrange("p (a c) -> p a c", a=2)
        YG = HT.rearrange("p k c -> p (k c)")[:, 2560:3584].rearrange("p (t c) -> p t c", t=2)
        OT7 = SQ7.rearrange("p (g c) -> p g c", g=4)
        BUF7 = {"P": HS[:, 0:2, :], "PT": HS[:, 2:4, :], "st": SM[:, 144:152].rearrange("p (a b) -> p a b", a=2)}
        gqa_units = []
        for kv in range(2):
            r = 64 * kv
            for g in range(4):
                hd = 4 * kv + g
                for t in range(2):
                    gqa_units.append({"q": QG[r:r + 64, g, t * P:(t + 1) * P], "k": [(0, 512, KG[r:r + 64, :])],
                                      "nk": 512, "dv": 64, "o": YG[:, t, hd * 64:hd * 64 + 64],
                                      "v": [VG[:, a, kv * 64:kv * 64 + 64] for a in range(4)]})

        def pe_odd():
            pe_norm("mod o", [0, 1, 2, 3], XN7)
            pe_feature_block("gq", "gq")
            w = weight("gkv")[:, 0:2048].rearrange("p (k c) -> p k c", k=KT)
            ps = open_bank("gk")
            for k in range(KT):
                last = mm(ps[:, :], w[:, k, 0:P], HT[:, k, :], k == 0, k == KT - 1)
            last.then_inc(tensor_done, pe.one())
            pe.mark("gk")
            ps = open_bank("gv")
            for t in range(4):
                for k in range(KT):
                    last = mm(ps[:, t * P:(t + 1) * P], ht(k, t), w[:, k, P:2 * P], k == 0, k == KT - 1)
            weight_used(last, "gkv")
            pe.mark("gv")
            pe_feature_block("hin0", "hu", m0=0)
            pe_head_norm("gq7", SQ7, 2)
            w = weight("hfilter")
            pe.wait_ge(loaded["odd"], at("hyena in"))

            def filter_layer(j, src):
                ps = open_bank(f"filter mm{j}")
                n = 33 if j == 0 else 64
                mm(ps[0:64, 0:SEQ], w[0:n, j * 64:(j + 1) * 64], src, True, True).then_inc(tensor_done, pe.one())
                pe.mark(f"filter mm{j}")

            filter_layer(0, ZT[0:33, :])
            pe_feature_block("hin1", "hu", m0=4)
            pe_head_norm("gk7", SQ7, 1)
            pe.wait_ge(scalar_done, at("filter0"))
            filter_layer(1, HF[0:64, :])
            pe_gate(1, 0, 0)
            pe_feature_block("hin2", "hu", m0=8)
            pe.wait_ge(scalar_done, at("filter1"))
            filter_layer(2, HF[0:64, :])
            pe_gate(1, 0, 1)
            pe.wait_ge(vector_done, at("gk7 normed"))
            for n, Q in [(f"gq{g}", QG[:, g, :]) for g in range(4)] + [("gk", KG[:, 0:SEQ])]:
                ps = open_bank("rot " + n)
                mm(ps[:, 0:SEQ], K("rotate_pairs"), Q, True, True).then_inc(tensor_done, pe.one())
                pe.mark("rot " + n)
            pe.wait_ge(scalar_done, at("filter2"))
            for h in range(2):
                for t in range(2):
                    ps = open_bank(f"taps{h}.{t}")
                    mm(ps[:, :], HF[0:64, t * P:(t + 1) * P], w[0:64, 192 + h * 512:192 + (h + 1) * 512], True, True).then_inc(tensor_done, pe.one())
                    pe.mark(f"taps{h}.{t}")
            pe.mark("slot of hfilter")
            pe.wait_ge(vector_done, at("taps abs"))
            ps = open_bank("taps sum")
            for j in range(4):
                last = mm(ps[:, :], K("ones"), TABS[:, j, :], j == 0, j == 3)
            last.then_inc(tensor_done, pe.one())
            pe.mark("taps sum")
            def spectrum(label, even, odd):
                for j in range(5):
                    ps = open_bank(f"{label}{j}")
                    m = P if j < 4 else 1
                    for t in range(2):
                        s = (even if j in (0, 1, 4) else odd)[:, t, :]
                        last = mm(ps[0:m, :], DF[:, t, j * P:j * P + m], s, t == 0, t == 1)
                    last.then_inc(tensor_done, pe.one())
                    pe.mark(f"{label}{j}")

            pe.wait_ge(vector_done, at("taps ready"))
            spectrum("kf", DEC[:, 0:2, :], DEC[:, 2:4, :])
            pe.wait_ge(vector_done, at("z fm"))
            for t in range(2):
                pe_turn(f"z turned{t}", [UC[:, 8 + g, t * P:(t + 1) * P] for g in range(4)])
            pe.wait_ge(scalar_done, at("z tm"))
            spectrum("zf", ZTM, ZTM)
            pe.wait_ge(vector_done, at("spectrum"))
            for q in range(2):
                ps = open_bank(f"long{q}")
                for i in range(2):
                    g = 2 * q + i
                    o = ps[:, i * SEQ:(i + 1) * SEQ]
                    for j in range(4):
                        mm(o, ZF[:, j, g * P:(g + 1) * P], DI[:, j, :], j == 0, False)
                    last = mm(o, ZF[0:1, 4, g * P:(g + 1) * P], DI[0:1, 4, :], False, True)
                last.then_inc(tensor_done, pe.one())
                pe.mark(f"long{q}")
            pe.wait_ge(vector_done, at("gqa heads"))
            pe_attention("gqa", gqa_units, BUF7)
            pe.wait_ge(vector_done, at("yg"))
            for t in range(2):
                pe_turn(f"yg turned{t}", [YG[:, t, i * P:(i + 1) * P] for i in range(4)])
            pe.wait_ge(scalar_done, at("yg ready"))
            for h in range(2):
                pe_token_blocks([f"oout{h}"], [KT], f"oout{h}", lambda k, t: (OT7 if k < 4 else YT7)[:, k % 4, t * P:(t + 1) * P])

        def act_odd():
            act_norm("mod o", [0, 1, 2, 3], JK7)
            for j in range(2):
                copy_out(act, f"gq.{j}", QG[:, 2 * j:2 * j + 2, :], lambda ps: ps[:, :].rearrange("p (a c) -> p a c", a=2))
            copy_out(act, "gk", KG)
            copy_out(act, "gv", VG.rearrange("p a b -> p (a b)"))
            act.wait_ge(scalar_done, act.n)
            act.mark("g out")
            act.wait_ge(vector_done, at("ur zero"))

            def hu_out(i):
                for j in (2 * i, 2 * i + 1):
                    copy_out(act, f"hu.{j}", UR[:, 2 * j:2 * j + 2, 1:1 + SEQ], lambda ps: ps[:, :].rearrange("p (a c) -> p a c", a=2))

            def sine(j):
                act.wait_ge(vector_done, at(f"angle{j}"))
                activation(HF[0:64, :], HF[0:64, :], ACT.Sin).then_inc(scalar_done, act.one())
                act.mark(f"filter{j}")

            hu_out(0)
            act_head_norm("gq7", SQ7, 2, 1.0 / 64)
            sine(0)
            hu_out(1)
            act_head_norm("gk7", SQ7, 1, 1.0 / 64)
            sine(1)
            act_gate(1, 0, 0)
            hu_out(2)
            act.mark("hu out")
            sine(2)
            act_gate(1, 0, 1)
            for j in range(5):
                m = P if j < 4 else 1
                copy_out2(act, f"kf{j}", KF7[0:m, j, :], m)
            act.mark("kf out")
            for t in range(2):
                copy_out(act, f"z turned{t}", ZTM[:, t, :])
            act.mark("z tm")
            for j in range(5):
                m = P if j < 4 else 1
                copy_out2(act, f"zf{j}", ZF[0:m, j, :], m)
            act.mark("zf out")
            act_attention("gqa", gqa_units, BUF7)
            for t in range(2):
                n = f"yg turned{t}"
                ps = full(act, n)
                activation(OT7[:, :, t * P:(t + 1) * P], k4(ps[:, :]), ACT.Copy).then_inc(scalar_done, act.one())
                act.mark("read " + n)
            act.wait_ge(scalar_done, act.n)
            act.mark("yg ready")

        def copy_out2(e, label, dst, m):
            ps = full(e, label)
            nc.scalar.activation(dst, ps[0:m, :], ACT.Copy).then_inc(e.done, e.one())
            e.mark("read " + label)

        TABS = JK7.rearrange("p a b -> p (a b)").rearrange("p (a c) -> p a c", a=4)
        TWO_PI_HI = 6.28125
        TWO_PI_LO = 2 * math.pi - 6.28125
        ROUND = 12582912.0

        def dve_odd():
            dve_norm("mod o", [0, 1, 2, 3], XN7, mod_scale(1, 0), mod_shift(1, 0),
                     finish=lambda t: dve_add("cdown0.", 1, [t], gate_row(1)))
            nc.vector.memset(UR, 0.0).then_inc(vector_done, dve.one())
            dve.wait_ge(vector_done, dve.n)
            dve.mark("ur zero")
            tmp = RC7B[0:64, :]
            h = HF[0:64, :]

            def angle(j):
                ps = full(dve, f"filter mm{j}")
                ts(h, ps[0:64, 0:SEQ], C("hb", j)[0:64, :], C("hfreq")[0:64, :], ALU.add, ALU.mult).then_inc(vector_done, dve.one())
                dve.wait_ge(vector_done, dve.n)
                dve.mark(f"read filter mm{j}")
                ts(tmp, h, 1.0 / (2 * math.pi), ROUND, ALU.mult, ALU.add).then_inc(vector_done, dve.one())
                dve.wait_ge(vector_done, dve.n)
                ts(tmp, tmp, ROUND, None, ALU.subtract).then_inc(vector_done, dve.one())
                dve.wait_ge(vector_done, dve.n)
                stt(h, tmp, -TWO_PI_HI, h, ALU.mult, ALU.add).then_inc(vector_done, dve.one())
                dve.wait_ge(vector_done, dve.n)
                stt(h, tmp, -TWO_PI_LO, h, ALU.mult, ALU.add).then_inc(vector_done, dve.one())
                dve.wait_ge(vector_done, dve.n)
                ts(h, h, 3.1415925, -3.1415925, ALU.min, ALU.max).then_inc(vector_done, dve.one())
                dve.wait_ge(vector_done, dve.n)
                dve.mark(f"angle{j}")

            dve_gate(1, 0, 0)
            dve.wait_ge(scalar_done, at("g out"))
            dve_head_norm("gq7", fl(QG), SQ7, [(0, 1024, C("gqa_q"))])
            angle(0)
            dve_head_norm("gk7", KG, SQ7[:, 0:512], [(0, 512, C("gqa_k"))])
            angle(1)
            dve_gate(1, 0, 1, "1.0.0")
            angle(2)
            dve.wait_ge(loaded["odd"], at("rope7 in"))
            dve.wait_ge(loaded["odd"], at("hyena in"))
            for n, Q in [(f"gq{g}", QG[:, g, :]) for g in range(4)] + [("gk", KG[:, 0:SEQ])]:
                ps = full(dve, "rot " + n)
                tt(JN[:, 0:SEQ], ps[:, 0:SEQ], RC7[:, 1, :], ALU.mult).then_inc(vector_done, dve.one())
                dve.mark("read rot " + n)
                tt(Q, Q, RC7[:, 0, :], ALU.mult).then_inc(vector_done, dve.one())
                dve.wait_ge(vector_done, dve.n)
                tt(Q, Q, JN[:, 0:SEQ], ALU.add).then_inc(vector_done, dve.one())
                dve.wait_ge(vector_done, dve.n)
            dve.mark("gqa heads")
            for hh in range(2):
                for t in range(2):
                    ps = full(dve, f"taps{hh}.{t}")
                    tt(HS[:, 2 * hh + t, :], ps[:, :], DEC[:, 2 * hh + t, :], ALU.mult).then_inc(vector_done, dve.one())
                    dve.mark(f"read taps{hh}.{t}")
            dve.wait_ge(vector_done, dve.n)
            stt(TABS, HS, -1.0, HS, ALU.mult, ALU.max).then_inc(vector_done, dve.one())
            dve.wait_ge(vector_done, dve.n)
            dve.mark("taps abs")
            ps = full(dve, "taps sum")
            nc.vector.reciprocal(JN, ps[:, :]).then_inc(vector_done, dve.one())
            dve.wait_ge(vector_done, dve.n)
            dve.mark("read taps sum")
            tt(HS, HS, rows(JN, 4), ALU.mult).then_inc(vector_done, dve.one())
            dve.wait_ge(vector_done, dve.n)
            tt(DEC[:, 0:2, :], HS[:, 0:2, :], HS[:, 2:4, :], ALU.add).then_inc(vector_done, dve.one())
            tt(DEC[:, 2:4, :], HS[:, 0:2, :], HS[:, 2:4, :], ALU.subtract).then_inc(vector_done, dve.one())
            dve.wait_ge(vector_done, dve.n)
            dve.mark("taps ready")
            dve.wait_ge(scalar_done, at("hu out"))
            for g in range(12):
                ts(UC[:, g, :], UR[:, g, 0:SEQ], C("hconv_w", g), C("hconv_b", g), ALU.mult, ALU.add).then_inc(vector_done, dve.one())
            dve.wait_ge(vector_done, dve.n)
            for i in (1, 2):
                for g in range(12):
                    stt(UC[:, g, :], UR[:, g, i:i + SEQ], C("hconv_w", 12 * i + g), UC[:, g, :], ALU.mult, ALU.add).then_inc(vector_done, dve.one())
                dve.wait_ge(vector_done, dve.n)
            tt(UC[:, 8:12, :], UC[:, 8:12, :], UC[:, 4:8, :], ALU.mult).then_inc(vector_done, dve.one())
            dve.wait_ge(vector_done, dve.n)
            dve.mark("z fm")
            dve.wait_ge(scalar_done, at("zf out"))
            dve.wait_ge(scalar_done, at("kf out"))
            Zr, Zi, Kr, Ki = ZF[:, 0:2, :], ZF[:, 2:4, :], KF7[:, 0:2, :], KF7[:, 2:4, :]
            T0, T1_ = DEC[:, 0:2, :], DEC[:, 2:4, :]
            tt(ZF[0:1, 4, :], ZF[0:1, 4, :], KF7[0:1, 4, :], ALU.mult).then_inc(vector_done, dve.one())
            tt(T0, Zi, Ki, ALU.mult).then_inc(vector_done, dve.one())
            tt(T1_, Zi, Kr, ALU.mult).then_inc(vector_done, dve.one())
            dve.wait_ge(vector_done, dve.n)
            tt(Zi, Zr, Ki, ALU.mult).then_inc(vector_done, dve.one())
            dve.wait_ge(vector_done, dve.n)
            tt(Zr, Zr, Kr, ALU.mult).then_inc(vector_done, dve.one())
            dve.wait_ge(vector_done, dve.n)
            tt(Zi, Zi, T1_, ALU.add).then_inc(vector_done, dve.one())
            dve.wait_ge(vector_done, dve.n)
            tt(Zr, Zr, T0, ALU.subtract).then_inc(vector_done, dve.one())
            dve.wait_ge(vector_done, dve.n)
            dve.mark("spectrum")
            for q in range(2):
                ps = full(dve, f"long{q}")
                for i in range(2):
                    g = 2 * q + i
                    stt(YT7[:, g, :], UC[:, 8 + g, :], C("hskip", g), ps[:, i * SEQ:(i + 1) * SEQ], ALU.mult, ALU.add).then_inc(vector_done, dve.one())
                    dve.wait_ge(vector_done, dve.n)
                    tt(YT7[:, g, :], YT7[:, g, :], UC[:, g, :], ALU.mult).then_inc(vector_done, dve.one())
                    dve.wait_ge(vector_done, dve.n)
                dve.mark(f"read long{q}")
            dve_attention("gqa", gqa_units, BUF7)
            dve.mark("yg")
            dve.wait_ge(scalar_done, at("gate out1.0.1"))
            dve_add("oout", 0, [0, 1], gate_row(0))

        def toeplitz(ap, offset, pattern):
            return bass.AP(tensor=ap.tensor, offset=offset, ap=pattern)

        JN = junk512
        RC7B = junk512[:, 0:SEQ]

        XN0 = XN1

        PH = ["start", "rwkv", "gdn", "eout", "mlp0", "attn", "mlp1", "even", "ffn0", "odd", "ffn1"]

        @block.sync
        def _(sp):
            e = Steps(sp, stored, marks)
            first = Steps(sp, loaded["first"], marks, by=16)
            for dst, src in ((X[:, 0:2, :], T["x"]), (KC[:, :], T["const"]), (CP[:, :], T["colp"])):
                sp.dma_start(dst, src).then_inc(loaded["first"], first.one())
            first.mark("first in")
            for i, (name, cols) in enumerate(PLAN):
                if i >= RING:
                    e.wait_ge(tensor_done, at("slot of " + PLAN[i - RING][0]))
                sp.dma_start(ring[:, i % RING, 0:cols], T["W"][i, :, 0:cols]).then_inc(slot_loaded[i % RING], 16)
            e.wait_ge(vector_done, at("dve end ffn1"))
            sp.dma_start(out.rearrange("b (t p) d -> p (b t) d", p=P), X[:, 0:2, :]).then_inc(stored, 16)
            sp.wait_ge(stored, 16)

        @block.gpsimd
        def _(pool):
            e = Steps(pool, loaded["start"], marks, by=16)
            group = {n: Steps(pool, loaded[n], marks, by=16) for n in LOADS}

            def load(which, dst, src):
                pool.dma_start(dst, src).then_inc(loaded[which], group[which].one())

            def row(name, n=P):
                a, c = RPLAN[name]
                return T["rowp"][0:1, a:a + c].broadcast_to([n, c])

            load("start", X[:, 2:4, :], T["ctx"])
            load("start", ALr, row("a_log"))
            load("start", DTr, row("dt"))
            group["start"].mark("start in", "rows 1c")
            e.wait_ge(vector_done, at("rwkv solved"))
            load("rwkv_rows", LNG, row("ln_g"))
            load("rwkv_rows", LNB, row("ln_b"))
            group["rwkv_rows"].mark("rows 1b")

            def after(ph):
                e.wait_ge(tensor_done, at(f"pe end {ph}"))
                e.wait_ge(scalar_done, at(f"act end {ph}"))
                e.wait_ge(vector_done, at(f"dve end {ph}"))

            after("rwkv")
            load("gdn_rows", NG, row("gdn_g"))
            group["gdn_rows"].mark("norm b")
            for i in range(2):
                after("eout" if i == 0 else "attn")
                load(f"ple{i}", M["pT"], T["pT"][i].rearrange("p (k c) -> p k c", k=2))
                load(f"ple{i}", M["pg"], row(f"ple{i}"))
                group[f"ple{i}"].mark(f"p{i}", f"rows ple{i}")
                if i == 0:
                    after("mlp0")
                    e.wait_ge(vector_done, at("mix1 x1"))
                    h = T["rel"]
                    for hd in range(16):
                        load("rel", REL[:, hd, :], toeplitz(h, hd * 513 + 129, [[1, P], [1, SEQ]]))
                    group["rel"].mark("rel")
            after("mlp1")
            e.wait_ge(vector_done, at("mod e x1"))
            load("even", RC, T["rope"].rearrange("p (a c) -> p a c", a=2))
            load("even", NM, T["nmask"])
            load("even", SUBG, row("subln"))
            group["even"].mark("rope in")
            e.wait_ge(scalar_done, at("mod e rms3"))
            for t in range(2):
                for rq in range(2):
                    for hd in range(8):
                        off = (hd * 15 + 7 - (2 * t + rq)) * P
                        load("bias", BM[64 * rq:64 * rq + 64, t, hd, :].rearrange("p (a b) -> p a b", a=4),
                             toeplitz(T["rpb"], off, [[1, 64], [P, 4], [1, 64]]))
            group["bias"].mark("bm loaded")
            after("ffn0")
            load("odd", RC7, T["rope"].rearrange("p (a c) -> p a c", a=2))
            load("odd", ZT, T["hconst"][:, 0:SEQ])
            load("odd", DEC, T["hconst"][:, SEQ:SEQ + 2048].rearrange("p (a c) -> p a c", a=4))
            load("odd", DF, T["dft"][:, 0:1280].rearrange("p (a c) -> p a c", a=2))
            load("odd", DI, T["dft"][:, 1280:2560].rearrange("p (a c) -> p a c", a=5))
            group["odd"].mark("rope7 in", "hyena in")

        @block.tensor
        def _(tensor):
            pe_steps = [pe_start, lambda: (pe_norm("mix0", [0, 1], XN0), pe_rwkv()), pe_gdn, pe_eout, lambda: pe_mlp(0),
                        pe_attn, lambda: pe_mlp(1), pe_even, lambda: pe_ffn(0, 2), pe_odd,
                        lambda: pe_ffn(1, 1)]
            for name, f in zip(PH, pe_steps):
                f()
                phase_end(pe, name, "pe")

        @block.scalar
        def _(scalar):
            JK0 = ar2b
            act_steps = [act_start, lambda: (act_norm("mix0", [0, 1], JK0), act_rwkv()), act_gdn,
                         act_eout, lambda: act_mlp(0), act_attn, lambda: act_mlp(1),
                         act_even, lambda: act_ffn(0, 2), act_odd, lambda: act_ffn(1, 1)]
            for name, f in zip(PH, act_steps):
                f()
                phase_end(act, name, "act")

        @block.vector
        def _(vector):

            dve_steps = [dve_start,
                         lambda: (dve_norm("mix0", [0, 1], XN0, lambda t: C("mix0", 0, 8)), dve_rwkv()), dve_gdn, dve_eout, lambda: dve_mlp(0),
                         dve_attn, lambda: dve_mlp(1), dve_even, lambda: dve_ffn(0, 2), dve_odd,
                         lambda: dve_ffn(1, 1)]
            for name, f in zip(PH, dve_steps):
                f()
                phase_end(dve, name, "dve")

        names = {id(v): k for k, v in sems.items()}
        for k, v in marks.items():
            if k != "unknown":
                counts[k] = (names[id(v[0])], v[1])
    return counts


def lay_out(a):
    f = {k: np.asarray(v) for k, v in a.items()}

    def tiled(w):
        k, n = w.shape
        return w.reshape(k // P, P, n).transpose(1, 0, 2).reshape(P, -1)

    blocks = {}

    def put(name, w):
        blocks[name] = tiled(w)

    def cols(prefix, w, at=0):
        for i in range(w.shape[1] // 512):
            put(f"{prefix}{at + i}", w[:, i * 512:(i + 1) * 512])

    w = f["even_w_in"][0]
    cols("rkv", w[:, 0:1536])
    cols("bqkv", w[:, 1536:3072])
    put("bgate", w[:, 3072:3584])
    put("bab", w[:, 3584:3592])
    put("lora_in", np.concatenate([f["rwkv_w1"][0], f["rwkv_a1"][0], f["rwkv_g1"][0]], 1))
    up = np.zeros((P, 1536), np.float32)
    up[:64, 0:512], up[:64, 512:1024], up[:, 1024:] = f["rwkv_w2"][0], f["rwkv_a2"][0], f["rwkv_g2"][0]
    blocks["lora_out"] = up
    cols("eout", f["even_w_out"][0])
    for i in range(2):
        cols(f"up{i}.", f["mlp_w1"][i])
        for h in range(2):
            for n in range(4):
                put(f"down{i}.{h}.{n}", f["mlp_w2"][i][n * 1024:(n + 1) * 1024, h * 512:(h + 1) * 512])
            put(f"pgate{i}.{h}", f["ple_w_gate"][i][:, h * 512:(h + 1) * 512])
        put(f"pproj{i}", f["ple_w_proj"][i])
        cols(f"ada{i}.", f["w_ada_2"][i])
        wu = f["w_up_2"][i]
        pair = np.stack([wu[:, :2816].reshape(D, 22, P), wu[:, 2816:].reshape(D, 22, P)], 2).reshape(D, -1)
        cols(f"cup{i}.", pair)
        for h in range(2):
            for n in range(3):
                put(f"cdown{i}.{h}.{n}", f["w_down_2"][i][n * 1024:(n + 1) * 1024, h * 512:(h + 1) * 512])
    cols("qkv", f["attn_w_qkv"][0])
    cols("aout", f["attn_w_out"][0])
    cols("win", f["w_in_e_2"][0])
    cols("wout", f["w_out_e_2"][0])
    w = f["w_in_o_2"][0]
    put("gq", w[:, 0:512].reshape(D, 2, 4, 64).transpose(0, 2, 1, 3).reshape(D, 512))
    put("gkv", w[:, 512:768])
    cols("hin", w[:, 768:])
    hf = np.zeros((P, 1216), np.float32)
    hf[:33, 0:64] = f["hy_w1_2"][0]
    hf[:64, 64:128], hf[:64, 128:192], hf[:64, 192:] = f["hy_w2_2"][0], f["hy_w3_2"][0], f["hy_w4_2"][0]
    blocks["hfilter"] = hf
    cols("oout", f["w_out_o_2"][0])
    plan = weight_plan()
    W = np.zeros((len(plan), P, SLOT), np.float32)
    for i, (name, n) in enumerate(plan):
        assert blocks[name].shape[1] == n, (name, blocks[name].shape, n)
        W[i, :, :n] = blocks[name]

    def col(v):
        return np.ascontiguousarray(v).reshape(-1, P).T

    def twice(v):
        return np.concatenate([v, v])

    def pad(v):
        o = np.zeros((P,), np.float32)
        o[:v.shape[0]] = v
        return o[:, None]

    lam = [f[f"da_lambda_{n}_2"][0] for n in ("q1", "q2", "k1", "k2")]
    cp = {"mix0": col(f["norm_mix_g"][0]), "mix1": col(f["norm_mix_g"][1]), "ffn0": col(f["norm_ffn_g"][0]),
          "ffn1": col(f["norm_ffn_g"][1]), "mu_proj": col(f["rwkv_mu_proj"][0]), "mu_lora": col(f["rwkv_mu_lora"][0]),
          "w0": col(f["rwkv_w0"][0]), "a0": col(f["rwkv_a0"][0]), "k_k": col(f["rwkv_k_k"][0]), "k_a": col(f["rwkv_k_a"][0]),
          "r_k": col(f["rwkv_r_k"][0]), "conv": col(f["gdn_conv_w"][0]), "attn_q": twice(f["attn_q_g"][0])[:, None],
          "attn_k": twice(f["attn_k_g"][0])[:, None],
          "c": np.stack([col(f["c_2"][0]), col(f["c_ctx_2"])], 2).reshape(P, 16),
          "fconv_w0": col(f["ffn_conv_w_2"][0]), "fconv_b0": col(f["ffn_conv_b_2"][0]), "fconv_w1": col(f["ffn_conv_w_2"][1]),
          "fconv_b1": col(f["ffn_conv_b_2"][1]), "na_q": twice(f["na_q_gain_2"][0])[:, None], "na_k": twice(f["na_k_gain_2"][0])[:, None],
          "da_q": twice(f["da_q_gain_2"][0])[:, None], "da_k": twice(f["da_k_gain_2"][0])[:, None],
          "lam": np.concatenate([pad(v) for v in lam], 1), "gqa_q": twice(f["gqa_q_gain_2"][0])[:, None],
          "gqa_k": twice(f["gqa_k_gain_2"][0])[:, None], "hconv_w": col(f["hy_conv_w_2"][0]), "hconv_b": col(f["hy_conv_b_2"][0]),
          "hb": np.concatenate([pad(f[f"hy_b{j}_2"][0]) for j in (1, 2, 3)], 1), "hfreq": pad(f["hy_freq_2"][0]), "hskip": col(f["hy_skip_2"][0]),
          "bada0": col(f["b_ada_2"][0]), "bada1": col(f["b_ada_2"][1])}
    colp = np.zeros((P, NCOL), np.float32)
    for name, (at, n) in CPLAN.items():
        assert cp[name].shape == (P, n), (name, cp[name].shape)
        colp[:, at:at + n] = cp[name]
    rp = {"ln_g": f["rwkv_ln_g"][0], "ln_b": f["rwkv_ln_b"][0], "gdn_g": f["gdn_norm_g"][0], "a_log": f["gdn_a_log"][0],
          "dt": f["gdn_dt_bias"][0], "ple0": f["ple_norm_g"][0], "ple1": f["ple_norm_g"][1], "subln": f["da_subln_gain_2"][0]}
    rowp = np.concatenate([rp[n].reshape(-1) for n, _ in ROWS])[None, :]
    rpb = np.zeros((8, 15, P), np.float32)
    rpb[:, :, 48:79] = f["na_rpb_2"][0]
    hconst, dft = hyena_constants()

    def tokens(v):
        return np.ascontiguousarray(v[0].reshape(2, P, -1).transpose(1, 0, 2))

    return {"W": W, "colp": colp, "rowp": np.ascontiguousarray(rowp), "const": np.concatenate(list(CONST.values()), 1),
            "x": tokens(f["x"]), "ctx": tokens(f["ctx_2"]),
            "pT": np.ascontiguousarray(f["p"][:, 0].transpose(0, 2, 1).reshape(2, 2, P, SEQ).transpose(0, 2, 1, 3).reshape(2, P, 512)),
            "rel": np.ascontiguousarray(f["attn_rel_bias"][0]), "rpb": rpb, "rope": rope_constants(), "nmask": neighbour_mask(),
            "hconst": hconst, "dft": dft}


def kernel(**inputs):
    import concourse.bacc as bacc
    from concourse.bass_utils import run_bass_kernel_spmd

    arrays = {f"in_{k}": v for k, v in lay_out(inputs).items()}
    counts = {}
    for _ in range(2):
        nc = bacc.Bacc("TRN2", target_bir_lowering=False, num_devices=1)
        T = {k[3:]: nc.dram_tensor(k, v.shape, F32, kind="ExternalInput").ap() for k, v in arrays.items()}
        out = nc.dram_tensor("out_0", (1, SEQ, D), F32, kind="ExternalOutput").ap()
        counts = build(nc, T, out, counts)
    assert not counts["unknown"], counts["unknown"]
    r = run_bass_kernel_spmd(nc, [arrays], core_ids=[0])
    return r.results[0]["out_0"]
```
